# Optimizing a Trainium2 kernel written in Bass

```python
import jax, jax.numpy as jnp
from jax import lax
import numpy as np

D_MODEL = 1024
BATCH = 1
SEQ = 512
DEPTH = 1
DEC_BATCH = 8
DEC_SEQ = 1
PAST_LEN = 2048
PAGE_SIZE = 128

HEAD_DIM = 64
MIX_WIDTH = D_MODEL
A_WIDTH = MIX_WIDTH // 2
A_GROUPS = A_WIDTH // HEAD_DIM
CHUNK = 128
B_WIDTH = MIX_WIDTH - A_WIDTH
B_HEADS = B_WIDTH // HEAD_DIM
KV_HEADS = 2
Q_PER_KV = B_HEADS // KV_HEADS
KV_WIDTH = KV_HEADS * HEAD_DIM
WINDOW = 128
IN_WIDTH = 2 * A_WIDTH + B_WIDTH + 2 * KV_WIDTH
N_EXPERTS = 32
TOP_K = 4
D_FF = D_MODEL
SWIGLU_ALPHA = 1.702
SWIGLU_LIMIT = 7.0
PLE_DIM = 256
MOE_BLOCK = 128
EPS = 1e-5

kernel_name = 'hymba_gmlp_swa_sink_moe_ple_step'

def rmsnorm(x, g):
    xf = x.astype(jnp.float32)
    y = xf * lax.rsqrt(jnp.mean(xf * xf, axis=-1, keepdims=True) + EPS)
    return (y * g.astype(jnp.float32)).astype(x.dtype)

def layernorm(x, g, b):
    xf = x.astype(jnp.float32)
    mu = jnp.mean(xf, axis=-1, keepdims=True)
    xc = xf - mu
    y = xc * lax.rsqrt(jnp.mean(xc * xc, axis=-1, keepdims=True) + EPS)
    return (y * g.astype(jnp.float32) + b.astype(jnp.float32)).astype(x.dtype)

def alibi_slopes(n):
    return jnp.exp2(-8.0 * jnp.arange(1, n + 1, dtype=jnp.float32) / n)

def causal_spatial_weights(w_sp):
    mask = jnp.tril(jnp.ones((CHUNK, CHUNK), dtype=bool))
    return jnp.where(mask, w_sp, jnp.zeros_like(w_sp))

def chunk_mlp_prompt(u, v, w_sp, b_sp):
    b_, s_, _ = u.shape
    nc = s_ // CHUNK
    vc = v.reshape(b_, nc, CHUNK, A_GROUPS, HEAD_DIM)
    w = causal_spatial_weights(w_sp)
    mixed = jnp.einsum('gts,bcsgd->bctgd', w, vc) + b_sp.T[None, None, :, :, None]
    return u * mixed.reshape(b_, s_, A_WIDTH)

def chunk_mlp_sample(u, v, w_sp, b_sp):
    b_, n, _ = u.shape
    w = causal_spatial_weights(w_sp)[:, :n, :n]
    vg = v.reshape(b_, n, A_GROUPS, HEAD_DIM)
    mixed = jnp.einsum('gts,bsgd->btgd', w, vg) + b_sp[:, :n].T[None, :, :, None]
    return u * mixed.reshape(b_, n, A_WIDTH)

def sink_attention(q, k, v, dist, valid, sinks):
    b_, c_, lq = q.shape[:3]
    qg = q.reshape(b_, c_, lq, KV_HEADS, Q_PER_KV, HEAD_DIM)
    s = jnp.einsum('bcqkgd,bcskd->bckgqs', qg, k).astype(jnp.float32) * (HEAD_DIM ** -0.5)
    slopes = alibi_slopes(B_HEADS).reshape(KV_HEADS, Q_PER_KV, 1, 1)
    s = s - slopes * dist.astype(jnp.float32)[None, :, None, None]
    s = jnp.where(valid[None, :, None, None], s, jnp.finfo(jnp.float32).min)
    sink = jnp.broadcast_to(sinks.astype(jnp.float32).reshape(KV_HEADS, Q_PER_KV, 1, 1), s.shape[:-1] + (1,))
    p = jax.nn.softmax(jnp.concatenate([s, sink], axis=-1), axis=-1)[..., :-1]
    out = jnp.einsum('bckgqs,bcskd->bcqkgd', p.astype(v.dtype), v)
    return out.reshape(b_, c_, lq, B_WIDTH)

def swa_prompt(q, k, v, sinks):
    b_, s_ = q.shape[:2]
    nb = s_ // WINDOW
    qb = q.reshape(b_, nb, WINDOW, B_HEADS, HEAD_DIM)

    def with_prev(xs):
        xb = xs.reshape(b_, nb, WINDOW, KV_HEADS, HEAD_DIM)
        prev = jnp.pad(xb[:, :-1], ((0, 0), (1, 0), (0, 0), (0, 0), (0, 0)))
        return jnp.concatenate([prev, xb], axis=2)

    i = jnp.arange(WINDOW)[:, None]
    j = jnp.arange(2 * WINDOW)[None, :]
    dist = i + WINDOW - j
    blk = jnp.arange(nb)[:, None, None]
    valid = (dist >= 0) & (dist < WINDOW) & ((blk > 0) | (j >= WINDOW))
    out = sink_attention(qb, with_prev(k), with_prev(v), dist[None], valid, sinks)
    return out.reshape(b_, s_, B_WIDTH)

def swa_sample(q, k_new, v_new, cache_k, cache_v, sinks):
    w = cache_k.shape[1]
    n = q.shape[1]
    keys = jnp.concatenate([cache_k.astype(k_new.dtype), k_new], axis=1)
    vals = jnp.concatenate([cache_v.astype(v_new.dtype), v_new], axis=1)
    i = jnp.arange(n)[:, None]
    j = jnp.arange(w + n)[None, :]
    dist = i + w - j
    valid = (dist >= 0) & (dist < WINDOW)
    out = sink_attention(q[:, None], keys[:, None], vals[:, None], dist[None], valid[None], sinks)
    return out[:, 0], keys[:, -WINDOW:], vals[:, -WINDOW:]

def clamped_swiglu(hid):
    gate = jnp.minimum(hid[..., :D_FF], SWIGLU_LIMIT)
    up = jnp.clip(hid[..., D_FF:], -SWIGLU_LIMIT, SWIGLU_LIMIT)
    return (up + 1.0) * gate * jax.nn.sigmoid(SWIGLU_ALPHA * gate)

def moe(x, w_router, b_router, w_gu, b_gu, w_dn, b_dn):
    n, d = x.shape
    logits = x.astype(jnp.float32) @ w_router.astype(jnp.float32) + b_router.astype(jnp.float32)
    top_val, top_idx = lax.top_k(logits, TOP_K)
    gates = jax.nn.softmax(top_val, axis=-1)
    nk = n * TOP_K
    flat_e = top_idx.reshape(nk)
    flat_tok = jnp.arange(nk) // TOP_K
    flat_gate = gates.reshape(nk)
    order = jnp.argsort(flat_e)
    sorted_e = flat_e[order]
    counts = jnp.bincount(flat_e, length=N_EXPERTS)
    padded = (counts + MOE_BLOCK - 1) // MOE_BLOCK * MOE_BLOCK
    pad_end = jnp.cumsum(padded)
    pad_start = pad_end - padded
    start = jnp.cumsum(counts) - counts
    dest = pad_start[sorted_e] + jnp.arange(nk) - start[sorted_e]
    n_blocks = (nk + N_EXPERTS * (MOE_BLOCK - 1) + MOE_BLOCK - 1) // MOE_BLOCK
    n_rows = n_blocks * MOE_BLOCK
    row_tok = jnp.full((n_rows,), n, dtype=jnp.int32).at[dest].set(flat_tok[order].astype(jnp.int32))
    row_gate = jnp.zeros((n_rows,), x.dtype).at[dest].set(flat_gate[order].astype(x.dtype))
    block_e = jnp.minimum(jnp.searchsorted(pad_end, jnp.arange(n_blocks) * MOE_BLOCK, side='right'), N_EXPERTS - 1)
    x_pad = jnp.concatenate([x, jnp.zeros((1, d), x.dtype)], axis=0)
    xs = x_pad[row_tok].reshape(n_blocks, MOE_BLOCK, d)

    def expert_block(args):
        xb, e = args
        hid = xb @ w_gu[e] + b_gu[e]
        return clamped_swiglu(hid) @ w_dn[e] + b_dn[e]

    ys = lax.map(expert_block, (xs, block_e)).reshape(n_rows, d)
    out = jnp.zeros((n + 1, d), x.dtype).at[row_tok].add(ys * row_gate[:, None])
    return out[:n]

def layer_forward(h, ple, cache_k, cache_v, g_mix, w_in, ln_v_g, ln_v_b, w_sp, b_sp, sinks,
                  g_out_a, g_out_b, w_o, g_moe, w_router, b_router, w_gu, b_gu, w_dn, b_dn,
                  g_ple, w_ple_gate, w_ple_proj):
    b_, s_, _ = h.shape
    z = rmsnorm(h, g_mix) @ w_in
    u = jax.nn.gelu(z[..., :A_WIDTH])
    va = layernorm(jax.nn.gelu(z[..., A_WIDTH:2 * A_WIDTH]), ln_v_g, ln_v_b)
    o = 2 * A_WIDTH
    q = z[..., o:o + B_WIDTH].reshape(b_, s_, B_HEADS, HEAD_DIM)
    o = o + B_WIDTH
    k = z[..., o:o + KV_WIDTH].reshape(b_, s_, KV_HEADS, HEAD_DIM)
    vb = z[..., o + KV_WIDTH:].reshape(b_, s_, KV_HEADS, HEAD_DIM)
    if cache_k is None:
        ya = chunk_mlp_prompt(u, va, w_sp, b_sp)
        yb = swa_prompt(q, k, vb, sinks)
        new_k, new_v = k[:, -WINDOW:], vb[:, -WINDOW:]
    else:
        ya = chunk_mlp_sample(u, va, w_sp, b_sp)
        yb, new_k, new_v = swa_sample(q, k, vb, cache_k, cache_v, sinks)
    mix = jnp.concatenate([rmsnorm(ya, g_out_a), rmsnorm(yb, g_out_b)], axis=-1) @ w_o
    h = h + mix
    h = h + moe(rmsnorm(h, g_moe).reshape(b_ * s_, D_MODEL), w_router, b_router,
                w_gu, b_gu, w_dn, b_dn).reshape(b_, s_, D_MODEL)
    gate = jax.nn.sigmoid(rmsnorm(h, g_ple) @ w_ple_gate)
    h = h + gate * (ple.astype(h.dtype) @ w_ple_proj)
    return h, new_k, new_v, va

def setup_inputs(seed: int = 0) -> dict:
    key = jax.random.key(seed)
    ks = iter(jax.random.split(key, 32))

    def nrm(shape, scale):
        return scale * jax.random.normal(next(ks), shape, jnp.float32)

    L = DEPTH
    w = min(WINDOW, PAST_LEN)
    return {
        'x_prompt': nrm((BATCH, SEQ, D_MODEL), 1.0),
        'x_sample': nrm((DEC_BATCH, DEC_SEQ, D_MODEL), 1.0),
        'cache_swa_k': nrm((L, DEC_BATCH, w, KV_HEADS, HEAD_DIM), 1.0),
        'cache_swa_v': nrm((L, DEC_BATCH, w, KV_HEADS, HEAD_DIM), 1.0),
        'p_prompt': nrm((L, BATCH, SEQ, PLE_DIM), 1.0),
        'p_sample': nrm((L, DEC_BATCH, DEC_SEQ, PLE_DIM), 1.0),
        'g_mix': 1.0 + nrm((L, D_MODEL), 0.05),
        'w_in': nrm((L, D_MODEL, IN_WIDTH), D_MODEL ** -0.5),
        'ln_v_g': 1.0 + nrm((L, A_WIDTH), 0.05),
        'ln_v_b': nrm((L, A_WIDTH), 0.02),
        'w_sp': nrm((L, A_GROUPS, CHUNK, CHUNK), CHUNK ** -0.5),
        'b_sp': 1.0 + nrm((L, A_GROUPS, CHUNK), 0.05),
        'sinks': nrm((L, B_HEADS), 0.5),
        'g_out_a': 1.0 + nrm((L, A_WIDTH), 0.05),
        'g_out_b': 1.0 + nrm((L, B_WIDTH), 0.05),
        'w_o': nrm((L, MIX_WIDTH, D_MODEL), MIX_WIDTH ** -0.5),
        'g_moe': 1.0 + nrm((L, D_MODEL), 0.05),
        'w_router': nrm((L, D_MODEL, N_EXPERTS), D_MODEL ** -0.5),
        'b_router': nrm((L, N_EXPERTS), 0.01),
        'w_gu': nrm((L, N_EXPERTS, D_MODEL, 2 * D_FF), D_MODEL ** -0.5),
        'b_gu': nrm((L, N_EXPERTS, 2 * D_FF), 0.02),
        'w_dn': nrm((L, N_EXPERTS, D_FF, D_MODEL), D_FF ** -0.5),
        'b_dn': nrm((L, N_EXPERTS, D_MODEL), 0.02),
        'g_ple': 1.0 + nrm((L, D_MODEL), 0.05),
        'w_ple_gate': nrm((L, D_MODEL, D_MODEL), D_MODEL ** -0.5),
        'w_ple_proj': nrm((L, PLE_DIM, D_MODEL), PLE_DIM ** -0.5),
        'g_final': 1.0 + nrm((D_MODEL,), 0.05),
    }

def reference(x_prompt, x_sample, cache_swa_k, cache_swa_v, p_prompt, p_sample,
              g_mix, w_in, ln_v_g, ln_v_b, w_sp, b_sp, sinks, g_out_a, g_out_b, w_o,
              g_moe, w_router, b_router, w_gu, b_gu, w_dn, b_dn,
              g_ple, w_ple_gate, w_ple_proj, g_final):
    hp = x_prompt
    hs = x_sample
    pk, pv, sk, sv, scv = [], [], [], [], []
    for l in range(DEPTH):
        lw = (g_mix[l], w_in[l], ln_v_g[l], ln_v_b[l], w_sp[l], b_sp[l], sinks[l],
              g_out_a[l], g_out_b[l], w_o[l], g_moe[l], w_router[l], b_router[l],
              w_gu[l], b_gu[l], w_dn[l], b_dn[l], g_ple[l], w_ple_gate[l], w_ple_proj[l])
        hp, k_p, v_p, _ = layer_forward(hp, p_prompt[l], None, None, *lw)
        hs, k_s, v_s, va_s = layer_forward(hs, p_sample[l], cache_swa_k[l], cache_swa_v[l], *lw)
        pk.append(k_p)
        pv.append(v_p)
        sk.append(k_s)
        sv.append(v_s)
        scv.append(va_s)
    y_prompt = rmsnorm(hp, g_final)
    y_sample = rmsnorm(hs, g_final)
    return (y_prompt, y_sample, jnp.stack(pk), jnp.stack(pv), jnp.stack(sk), jnp.stack(sv), jnp.stack(scv))


_drawn_inputs = setup_inputs


def setup_inputs(seed=0):
    import zlib

    import numpy as np

    out = dict(_drawn_inputs(seed))
    spreads = {}
    factors = {'ln_v_b': 2.88, 'b_gu': 6.982, 'b_dn': 8.0, 'g_ple': 8.0}
    for name, (base, spread) in spreads.items():
        noise = np.random.default_rng([zlib.crc32(name.encode()), seed]).standard_normal(out[name].shape)
        drawn = base * np.exp(spread * noise) if base else spread * noise
        out[name] = __import__('jax').numpy.asarray(drawn.astype(out[name].dtype))
    for name, factor in factors.items():
        out[name] = (out[name] * factor).astype(out[name].dtype)
    return out
```

```python
from contextlib import ExitStack

import concourse.bass as bass
from concourse import mybir

F32 = mybir.dt.float32
F32R = mybir.dt.float32r
I32 = mybir.dt.int32
U32 = mybir.dt.uint32
ALU = mybir.AluOpType
ACT = mybir.ActivationFunctionType
AX = mybir.AxisListType.X

P = 128
EPS = 1e-5
NEG = -3.4028235e38
ALPHA = 1.702
LIMIT = 7.0


class Signals:

    def __init__(self, engine, step):
        self.engine, self.step = engine, step
        self.count, self.grows, self.turn, self.last = {}, {}, 0, None

    def __call__(self, instruction, sem=None):
        sem = self.step if sem is None else sem
        instruction.then_inc(sem, 1)
        self.count[sem] = self.count.get(sem, 0) + 1
        self.last = sem
        return instruction

    def on(self, engine):
        self.engine = engine
        return self

    def settle(self):
        sem = self.last
        self.engine.wait_ge(sem, self.turn * self.grows.get(sem, 0) + self.count[sem])

    def enter_loop(self, turn, grows):
        self.turn, self.grows, self.entry = turn, grows, dict(self.count)

    def leave_loop(self, turns):
        for sem, n in self.count.items():
            assert n - self.entry.get(sem, 0) == self.grows.get(sem, 0), (sem, n - self.entry.get(sem, 0))
        self.count = dict(self.entry)
        self.turn = turns


def product(nc, out, x_hi, x_lo, w_hi, w_lo, chunks, cols, start, stop):
    for i, (cx, cw) in enumerate(chunks):
        for j, (a, b) in enumerate(((x_hi, w_hi), (x_hi, w_lo), (x_lo, w_hi))):
            last = nc.tensor.matmul(out, a(cx), b[:, cw, 0:cols], start=start and i == 0 and j == 0,
                                    stop=stop and i == len(chunks) - 1 and j == 2)
    return last


def hybrid_layer(nc, x_prompt, x_sample, cache_k, cache_v, p_prompt, p_sample, g_mix, w_in, ln_v_g,
                 ln_v_b, w_sp, b_sp, sinks, g_out_a, g_out_b, w_o, g_moe, w_router, b_router, w_gu,
                 b_gu, w_dn, b_dn, g_ple, w_ple_gate, w_ple_proj, g_final,
                 y_prompt, y_sample, prompt_k, prompt_v, sample_k, sample_v, sample_chunk_v):
    SEQ, D = x_prompt.shape[1:]
    NS = x_sample.shape[0]
    NT = SEQ // P
    TILES = NT + 1
    ROWS = [P] * NT + [NS]
    TOK = SEQ + NS
    KC = D // P
    HALFK = KC // 2
    G, CH = w_sp.shape[1:3]
    HD = cache_k.shape[-1]
    KV = cache_k.shape[3]
    AW = G * HD
    H = sinks.shape[1]
    HG = H // KV
    BW = H * HD
    KVW = KV * HD
    E = w_router.shape[2]
    TOPK = 4
    PLE = w_ple_proj.shape[1]
    PC = PLE // P
    CB = 512
    OVER = TOPK * TOK // (P + 1)
    NBMAX = E + OVER
    TABLE = (NBMAX + 2) * P
    NOWHERE = 1 << 20
    assert CH == P and AW == CB and BW == CB and D == 2 * CB and KC == 8 and TOK * TOPK < NOWHERE
    SLOPES = [2.0 ** (-8.0 * (h + 1) / H) for h in range(H)]
    LEAD = 3

    TILE_B = KC * CB * 4
    HALF_B = TILE_B // 2
    RAW = -(-nc.sbuf_base // 64) * 64
    SPLIT = RAW + 6 * TILE_B
    MAIN = SPLIT + 2 * LEAD * HALF_B
    SIDE = RAW + 4 * TILE_B
    XT_B = KC * TOK * 4

    def at(name, shape, dt, offset):
        return nc.alloc_sbuf_tensor_at(name, shape, dt, offset=offset)

    raw = [at(f"raw_{s}", [P, KC, CB], F32, RAW + s * TILE_B) for s in range(6)]
    half_hi = [at(f"half_hi_{s}", [P, HALFK, CB], F32R, SPLIT + 2 * s * HALF_B) for s in range(LEAD)]
    half_lo = [at(f"half_lo_{s}", [P, HALFK, CB], F32R, SPLIT + (2 * s + 1) * HALF_B) for s in range(LEAD)]

    uq = at("uq", [P, TILES, 2 * CB], F32, MAIN + 2 * XT_B)
    va = at("va", [P, TILES, CB], F32, MAIN + 2 * XT_B + TILES * 2 * CB * 4)
    keep = MAIN + 2 * XT_B + TILES * 3 * CB * 4
    ident = at("ident", [P, P], F32, keep)
    gates = at("gates", [P, TILES, TOPK], F32, keep + 512)
    gate_table = at("gate_table", [P, TILES, E], F32, keep + 640)
    END = keep + 640 + TILES * E * 4
    assert END <= nc.sbuf_usable_end, (END, nc.sbuf_usable_end)

    ctx = ExitStack()

    def sem(name):
        return ctx.enter_context(nc.semaphore(name))

    def dram(name, shape, dt):
        return nc.dram_tensor(name, shape, dt, kind="Internal").ap()

    hn_rows = dram("hn_rows", [TOK, D], F32)
    h_rows = dram("h_rows", [TOK, D], F32)
    expert_rows = dram("expert_rows", [TOPK * TOK, D], F32)
    slot_table = dram("slot_table", [TABLE, 2], I32)
    bias_rows = dram("bias_rows", [E, 2, 2, D], F32)
    bank = ctx.enter_context(nc.psum_tensor("bank", [P, 8, 512], F32))

    def tokens(ap_prompt, ap_sample, t):
        return ap_prompt[t * P:(t + 1) * P] if t < NT else ap_sample

    def column(t):
        return NS + t * P if t < NT else 0

    def stationary(xT, t):
        return lambda c: xT[:, c, column(t):column(t) + P]

    x_p, x_s = x_prompt[0], x_sample[:, 0, :]
    w_in_v = w_in[0].rearrange("(c p) n -> p c n", p=P)
    w_o_v = w_o[0].rearrange("(c p) n -> p c n", p=P)
    w_gu_v = w_gu[0].rearrange("e (c p) n -> e p c n", p=P)
    w_dn_v = w_dn[0].rearrange("e (c p) n -> e p c n", p=P)
    w_pg_v = w_ple_gate[0].rearrange("(c p) n -> p c n", p=P)
    w_pp_v = w_ple_proj[0].rearrange("(c p) n -> p c n", p=P)
    IN_COLS = [CB, CB, CB, 2 * KVW]

    raw_landed = [sem(f"raw_landed_{s}") for s in range(6)]

    xin = [at(f"xin_{i}", [P, D], F32, SIDE + i * D * 4) for i in range(2)]
    wsp = at("wsp", [P, G, P], F32, SIDE + 8192)
    wspT = at("wspT", [P, G, P], F32, SIDE + 12288)
    gain = at("gain", [P, D], F32, SIDE + 16384)
    lng = at("lng", [P, CB], F32, SIDE + 20480)
    lnb = at("lnb", [P, CB], F32, SIDE + 22528)
    k_nat = at("k_nat", [P, TILES, KVW], F32, SIDE + 24576)
    v_nat = at("v_nat", [P, TILES, KVW], F32, SIDE + 24576 + TILES * KVW * 4)
    small = SIDE + 24576 + 2 * TILES * KVW * 4
    stat = at("stat", [P, 8 * TILES], F32, small)
    bnst = at("bnst", [P, TILES, 6], F32, small + 256)
    bspT = at("bspT", [P, G], F32, small + 512)
    w00 = at("w00", [NS, G], F32, small + 576)
    b00 = at("b00", [NS, G], F32, small + 640)
    sink_b = at("sink_b", [P, H], F32, small + 704)
    sink64 = at("sink64", [NS * H, 1], F32, small + 768)
    nowhere = at("nowhere", [P, 2 * TABLE // P], I32, small + 832)
    xT_hi = at("xT_hi", [P, KC, TOK], F32R, MAIN)
    xT_lo = at("xT_lo", [P, KC, TOK], F32R, MAIN + XT_B)
    NQ = 4
    bias_f = at("bias_f", [E * NQ, 2 * D // NQ], F32, MAIN + 2 * XT_B + TILES * 2 * CB * 4)
    bias_h = at("bias_h", [E * NQ, 2 * D // NQ], F32R, MAIN + 2 * XT_B + TILES * 2 * CB * 4 + 2048)
    bias_l = at("bias_l", [E * NQ, 2 * D // NQ], F32R, MAIN + 2 * XT_B + TILES * 2 * CB * 4 + 4096)

    def ss(t):
        return stat[0:ROWS[t], 8 * t:8 * t + 1]

    def rstd(t):
        return stat[0:ROWS[t], 8 * t + 1:8 * t + 2]

    x_landed = [sem(f"x_landed_{i}") for i in range(2)]
    gain_landed, consts_landed, bias_landed0, bias_stored = sem("gain_landed"), sem("consts_landed"), sem("bias_landed0"), sem("bias_stored")
    bias_low = sem("bias_low")
    p_out, ident_ready = sem("p_out"), sem("ident_ready")
    p_act, p_dve, x_ss, x_normed, x_cut, xT_banked = sem("p_act"), sem("p_dve"), sem("x_ss"), sem("x_normed"), sem("x_cut"), sem("xT_banked")
    xT_hi_ready, xT_lo_ready = sem("xT_hi_ready"), sem("xT_lo_ready")
    p_hi, p_lo, z_first = sem("p_hi"), sem("p_lo"), sem("z_first")
    z_done, z_read, v_var, v_std, va_ready, bias_cut = sem("z_done"), sem("z_read"), sem("v_var"), sem("v_std"), sem("va_ready"), sem("bias_cut")
    wsp_cut, table_ready = sem("wsp_cut"), sem("table_ready")
    pool_steps = Signals(None, sem("pool_step"))

    def raw_half(s, h, cols=CB):
        return raw[s][:, h * HALFK:(h + 1) * HALFK, 0:cols]

    def split_columns(w):
        return IN_COLS[w] if w < len(IN_COLS) else CB

    def write_hi(act, n, s, h, cols, hi_sem, wait_used, landed_value):
        act.wait_ge(raw_landed[s], landed_value)
        if n >= LEAD:
            wait_used(act, n - LEAD)
        nc.scalar.activation(half_hi[n % LEAD][:, :, 0:cols], raw_half(s, h, cols), ACT.Copy).then_inc(hi_sem, 1)

    def write_lo(dve, n, s, h, cols, hi_sem, lo_sem, wait_used, landed_value):
        dve.wait_ge(raw_landed[s], landed_value)
        dve.wait_ge(hi_sem, n + 1)
        if n >= LEAD:
            wait_used(dve, n - LEAD)
        nc.vector.tensor_tensor(half_lo[n % LEAD][:, :, 0:cols], raw_half(s, h, cols),
                                half_hi[n % LEAD][:, :, 0:cols].bitcast(F32), ALU.subtract).then_inc(lo_sem, 1)

    def used_after(first, done):
        def wait_used(engine, n):
            if n % 2 == 0:
                engine.wait_ge(first, n // 2 + 1)
            else:
                engine.wait_ge(done, TILES * (n // 2 + 1))
        return wait_used

    NZ = 2 * len(IN_COLS)

    z_used = used_after(z_first, z_done)

    def zbank(w, t):
        return (TILES * w + t) % 8

    with nc.Block() as block:
        @block.sync
        def _(sp):
            col = 0
            for w, cols in enumerate(IN_COLS):
                sp.dma_start(raw[w][:, :, 0:cols], w_in_v[:, :, col:col + cols]).then_inc(raw_landed[w], 16)
                col += cols
            sp.wait_ge(bias_cut, 1)
            sp.wait_ge(bias_low, 1)
            for part, rows in enumerate((bias_h, bias_l)):
                sp.dma_start(bias_rows[:, :, part, :].rearrange("e s (f n) -> (e s) f n", n=CB), rows[:].bitcast(F32)).then_inc(bias_stored, 16)
            for w in range(2):
                sp.wait_ge(p_hi, 2 * w + 2)
                sp.wait_ge(p_lo, 2 * w + 2)
                sp.dma_start(raw[w][:], w_o_v[:, :, w * CB:(w + 1) * CB]).then_inc(raw_landed[w], 16)
            for w in range(2, 4):
                sp.wait_ge(p_hi, 2 * w + 2)
                sp.wait_ge(p_lo, 2 * w + 2)
                c0 = (w - 2) * D + CB
                sp.dma_start(raw[w][:], w_gu_v[0, :, :, c0:c0 + CB]).then_inc(raw_landed[w], 16)

        @block.gpsimd
        def _(pool):
            mine = pool_steps.on(pool)
            pool.dma_start(gain[:], g_mix[0:1, :].to_broadcast([P, D])).then_inc(gain_landed, 16)
            for t in range(TILES):
                if t >= 2:
                    pool.wait_ge(x_cut, t - 1)
                pool.dma_start(xin[t % 2][0:ROWS[t], :], tokens(x_p, x_s, t)).then_inc(x_landed[t % 2], 16)
                if t == 1:
                    mine(nc.gpsimd.memset(ident[:], 0.0))
                    mine.settle()
                    nc.gpsimd.affine_select(out=ident[:], in_=ident[:], compare_op=ALU.not_equal, fill=1.0, base=0,
                                            pattern=[[-1, P]], channel_multiplier=1).then_inc(ident_ready, 1)
                    mine(nc.gpsimd.memset(nowhere[:], NOWHERE))
            mine.settle()
            pool.dma_start(slot_table.rearrange("(p n) o -> p (n o)", p=P), nowhere[:]).then_inc(table_ready, 16)
            pool.dma_start(wsp[:], w_sp[0].rearrange("g t s -> t g s")).then_inc(consts_landed, 16)
            with nc.allow_non_contiguous_dma(reason="a few hundred single elements"):
                pool.dma_start(bspT[:], b_sp[0].rearrange("g t -> t g")).then_inc(consts_landed, 16)
                pool.dma_start(w00[:], w_sp[0, :, 0, 0:1].rearrange("g o -> o g").to_broadcast([NS, G])).then_inc(consts_landed, 16)
                pool.dma_start(b00[:], b_sp[0, :, 0:1].rearrange("g o -> o g").to_broadcast([NS, G])).then_inc(consts_landed, 16)
                for b in range(NS):
                    pool.dma_start(sink64[b * H:(b + 1) * H, :], sinks.rearrange("o h -> h o")).then_inc(consts_landed, 16)
            pool.dma_start(lng[:], ln_v_g[0:1, :].to_broadcast([P, CB])).then_inc(consts_landed, 16)
            pool.dma_start(lnb[:], ln_v_b[0:1, :].to_broadcast([P, CB])).then_inc(consts_landed, 16)
            pool.dma_start(sink_b[:], sinks[0:1, :].to_broadcast([P, H])).then_inc(consts_landed, 16)
            pool.wait_ge(consts_landed, 16 * (7 + NS))
            nc.gpsimd.affine_select(out=wsp[:], in_=wsp[:], compare_op=ALU.is_ge, fill=0.0, base=0,
                                    pattern=[[0, G], [-1, P]], channel_multiplier=1).then_inc(wsp_cut, 1)
            pool.wait_ge(table_ready, 16)
            pool.wait_ge(va_ready, 1)
            pool.dma_start(sample_chunk_v[0, :, 0, :], va[0:NS, NT, :]).then_inc(p_out, 16)
            pool.wait_ge(z_read, 4 * TILES)
            pool.dma_start(prompt_k[0, 0].rearrange("s k d -> s (k d)"), k_nat[:, NT - 1, :]).then_inc(p_out, 16)
            pool.dma_start(prompt_v[0, 0].rearrange("s k d -> s (k d)"), v_nat[:, NT - 1, :]).then_inc(p_out, 16)
            pool.wait_ge(p_out, 48)

        @block.scalar
        def _(act):
            mine = Signals(act, p_act)
            act.dma_start(bias_f[:], b_gu[0].rearrange("e (q n) -> (e q) n", q=NQ)).then_inc(bias_landed0, 16)
            for t in range(TILES):
                R = ROWS[t]
                act.wait_ge(x_landed[t % 2], 16 * (t // 2 + 1))
                mine(nc.scalar.activation(uq[0:R, t, :], xin[t % 2][0:R, :], ACT.Square, accum_out=ss(t)))
                mine.settle()
                nc.scalar.activation(ss(t), ss(t), ACT.Sqrt, scale=1.0 / D, bias=EPS).then_inc(x_ss, 1)
            act.wait_ge(bias_landed0, 16)
            nc.scalar.activation(bias_h[:], bias_f[:], ACT.Copy).then_inc(bias_cut, 1)
            for t in range(TILES):
                R, c0 = ROWS[t], column(t)
                act.wait_ge(xT_banked, t + 1)
                b = 2 * (t % 4)
                for j in range(2):
                    last = nc.scalar.activation(xT_hi[:, 4 * j:4 * j + 4, c0:c0 + R],
                                                bank[:, b + j, 0:4 * R].rearrange("p (c r) -> p c r", c=4), ACT.Copy)
                last.then_inc(xT_hi_ready, 1)
            def hi(n):
                w = n // 2
                write_hi(act, n, w, n % 2, split_columns(w), p_hi, z_used, 16)
            for n in range(LEAD):
                hi(n)
            for w in range(len(IN_COLS)):
                if 2 * w + LEAD < NZ:
                    hi(2 * w + LEAD)
                for t in range(TILES):
                    R, src = ROWS[t], bank[0:ROWS[t], zbank(w, t), :]
                    act.wait_ge(z_done, TILES * w + t + 1)
                    if w == 1 and t == 0:
                        act.wait_ge(bias_stored, 32)
                    if w == 0:
                        ins = nc.scalar.activation(uq[0:R, t, 0:CB], src, ACT.Gelu_apprx_tanh)
                    elif w == 1:
                        ins = nc.scalar.activation(va[0:R, t, :], src, ACT.Gelu_apprx_tanh)
                    elif w == 2:
                        ins = nc.scalar.activation(uq[0:R, t, CB:2 * CB].rearrange("p (i g d) -> p g i d", g=KV, i=HG),
                                                   src.rearrange("p (g i d) -> p g i d", g=KV, i=HG), ACT.Copy)
                    else:
                        nc.scalar.activation(k_nat[0:R, t, :], src[:, 0:KVW], ACT.Copy)
                        ins = nc.scalar.activation(v_nat[0:R, t, :], src[:, KVW:2 * KVW], ACT.Copy)
                    ins.then_inc(z_read, 1)
                if 2 * w + LEAD + 1 < NZ:
                    hi(2 * w + LEAD + 1)
            for t in range(TILES):
                act.wait_ge(v_var, t + 1)
                nc.scalar.activation(stat[0:ROWS[t], 8 * t + 4:8 * t + 5], stat[0:ROWS[t], 8 * t + 3:8 * t + 4],
                                     ACT.Sqrt, bias=EPS).then_inc(v_std, 1)

        @block.vector
        def _(dve):
            mine = Signals(dve, p_dve)
            dve.wait_ge(gain_landed, 16)
            for t in range(TILES):
                R = ROWS[t]
                dve.wait_ge(x_ss, t + 1)
                mine(nc.vector.reciprocal(rstd(t), ss(t)))
                mine.settle()
                mine(nc.vector.scalar_tensor_tensor(uq[0:R, t, :], xin[t % 2][0:R, :], rstd(t), gain[0:R, :],
                                               ALU.mult, ALU.mult), x_cut)
            dve.wait_ge(bias_cut, 1)
            mine(nc.vector.tensor_tensor(bias_l[:], bias_f[:], bias_h[:].bitcast(F32), ALU.subtract), bias_low)
            for t in range(TILES):
                R, c0 = ROWS[t], column(t)
                dve.wait_ge(xT_banked, t + 1)
                dve.wait_ge(xT_hi_ready, t + 1)
                b = 2 * (t % 4)
                for j in range(2):
                    last = nc.vector.tensor_tensor(xT_lo[:, 4 * j:4 * j + 4, c0:c0 + R],
                                                   bank[:, b + j, 0:4 * R].rearrange("p (c r) -> p c r", c=4),
                                                   xT_hi[:, 4 * j:4 * j + 4, c0:c0 + R].bitcast(F32), ALU.subtract)
                last.then_inc(xT_lo_ready, 1)
            for n in range(NZ):
                w = n // 2
                write_lo(dve, n, w, n % 2, split_columns(w), p_hi, p_lo, z_used, 16)
            for t in range(TILES):
                R = ROWS[t]
                dve.wait_ge(z_read, TILES + t + 1)
                mine(nc.vector.bn_stats(bnst[0:R, t, :], va[0:R, t, :]))
                mine.settle()
                nc.vector.bn_aggr(stat[0:R, 8 * t + 2:8 * t + 4], bnst[0:R, t, :]).then_inc(v_var, 1)
            dve.wait_ge(consts_landed, 16 * (7 + NS))
            for t in reversed(range(TILES)):
                R, v = ROWS[t], va[0:ROWS[t], t, :]
                dve.wait_ge(v_std, TILES)
                mine(nc.vector.reciprocal(stat[0:R, 8 * t + 5:8 * t + 6], stat[0:R, 8 * t + 4:8 * t + 5]))
                mine.settle()
                mine(nc.vector.tensor_scalar(v, v, stat[0:R, 8 * t + 2:8 * t + 3], stat[0:R, 8 * t + 5:8 * t + 6],
                                             ALU.subtract, ALU.mult))
                mine.settle()
                mine(nc.vector.tensor_tensor(v, v, lng[0:R, :], ALU.mult))
                mine.settle()
                mine(nc.vector.tensor_tensor(v, v, lnb[0:R, :], ALU.add), va_ready)

        @block.tensor
        def _(pe):
            pe.wait_ge(ident_ready, 1)
            for t in range(TILES):
                R = ROWS[t]
                pe.wait_ge(x_cut, t + 1)
                if t == 4:
                    pe.wait_ge(xT_hi_ready, 1)
                    pe.wait_ge(xT_lo_ready, 1)
                for c in range(KC):
                    last = nc.tensor.transpose(bank[:, 2 * (t % 4) + c // 4, (c % 4) * R:(c % 4 + 1) * R],
                                               uq[0:R, t, c * P:(c + 1) * P], ident[0:R, 0:R])
                last.then_inc(xT_banked, 1)
            pe.wait_ge(xT_hi_ready, TILES)
            pe.wait_ge(xT_lo_ready, TILES)
            for n in range(NZ):
                w, h = n // 2, n % 2
                pe.wait_ge(p_hi, n + 1)
                pe.wait_ge(p_lo, n + 1)
                for t in range(TILES):
                    if h == 0 and TILES * w + t >= 8:
                        pe.wait_ge(z_read, TILES * w + t - 7)
                    last = product(nc, bank[:, zbank(w, t), 0:IN_COLS[w]], stationary(xT_hi, t), stationary(xT_lo, t),
                                   half_hi[n % LEAD], half_lo[n % LEAD],
                                   [(h * HALFK + k, k) for k in range(HALFK)], IN_COLS[w], h == 0, h == 1)
                    if h == 1:
                        last.then_inc(z_done, 1)
                if h == 0:
                    last.then_inc(z_first, 1)

    o = MAIN
    def scratch(name, shape, dt=F32):
        nonlocal o
        size = 4
        for n in shape[1:]:
            size *= n
        t = at(name, shape, dt, o)
        o += -(-size // 32) * 32
        return t

    alibi = at("alibi", [P, H, 2 * P], F32, SPLIT + 2048)
    kT = scratch("kT", [P, SEQ])
    qT = scratch("qT", [P, NT, HG, P])
    probs = [scratch(f"probs_{i}", [P, HG, 2 * P]) for i in range(2)]
    pT = scratch("pT", [P, HG * 2, P])
    m_ = [scratch(f"stats_{i}", [P, 8, HG]) for i in range(2)]
    bias_s = scratch("bias_s", [P, H])
    dist_s = scratch("dist_s", [P, 2])
    slope_s = scratch("slope_s", [P, H])
    ksT = scratch("ksT", [P, NS, P])
    qsT = scratch("qsT", [P, HG, NS])
    s_pre = scratch("s_pre", [P, NS * H])
    s_exp = scratch("s_exp", [NS * H, P])
    s_st = scratch("s_st", [NS * H, 8])
    s_pT = scratch("s_pT", [P, NS * H])
    ysT = scratch("ysT", [P, HG, NS])
    assert o <= MAIN + 2 * XT_B, o - MAIN - 2 * XT_B
    k_win = at("k_win", [P, NS, KVW], F32, SIDE)
    v_win = at("v_win", [P, NS, KVW], F32, SIDE + NS * KVW * 4)
    dist_i = at("dist_i", [P, 2 * P], I32, SPLIT)
    dist_f = at("dist_f", [P, 2 * P], F32, SPLIT + 1024)
    UNITS = [(n, g) for n in range(NT) for g in range(KV)]

    a_dve = sem("a_dve")
    iota_ready, alibi_raw, alibi_ready = sem("iota_ready"), sem("alibi_raw"), sem("alibi_ready")
    win_landed, win_new_landed, a_out = sem("win_landed"), sem("win_new_landed"), sem("a_out")
    wspT_banked, wspT_ready, gate_done, gate_read = sem("wspT_banked"), sem("wspT_ready"), sem("gate_done"), sem("gate_read")
    kT_banked, kT_ready, qT_banked, qT_ready, ksT_banked, ksT_ready = (sem("kT_banked"), sem("kT_ready"),
        sem("qT_banked"), sem("qT_ready"), sem("ksT_banked"), sem("ksT_ready"))
    score_done, score_read, max_ready, exp_ready = sem("score_done"), sem("score_read"), sem("max_ready"), sem("exp_ready")
    pT_banked, pT_ready, pv_done, pv_read = sem("pT_banked"), sem("pT_ready"), sem("pv_done"), sem("pv_read")
    ss_done, ss_cut, ssT_done, ss_exp, ss_prob, spT_done, spT_ready, sy_done, sy_cut, syT_done, sy_ready = (
        sem(n) for n in ("s_score_done", "s_score_cut", "s_score_turned", "s_exp_ready", "s_prob_ready", "s_probT_done",
                         "s_probT_ready", "s_pv_done", "s_pv_cut", "s_pv_turned", "s_y_ready"))

    def turned(act, u):
        n, g = UNITS[u]
        act.wait_ge(pT_banked, u + 1)
        if n == 0:
            nc.scalar.activation(pT[:, 0:HG, :], bank[:, 4, :], ACT.Copy).then_inc(pT_ready, 1)
        else:
            nc.scalar.activation(pT[:], bank[:, 4:6, :], ACT.Copy).then_inc(pT_ready, 1)

    def s_bank(u):
        b = 2 * (u % 2)
        return bank[:, b:b + 2, :].rearrange("p b (i s) -> p (b i) s", s=2 * P)

    def o_bank(u):
        return bank[:, 6 + u % 2, 0:HG * HD].rearrange("p (i d) -> p i d", i=HG)

    with nc.Block() as block:
        @block.sync
        def _(sp):
            for win, cache, new in ((k_win, cache_k, k_nat), (v_win, cache_v, v_nat)):
                sp.dma_start(win[0:P - 1], cache[0, :, 1:P].rearrange("b s k d -> s b (k d)")).then_inc(win_landed, 16)
                sp.dma_start(win[P - 1:P], new[0:NS, NT, :]).then_inc(win_new_landed, 16)
            sp.wait_ge(win_landed, 32)
            sp.wait_ge(win_new_landed, 32)
            for win, out in ((k_win, sample_k), (v_win, sample_v)):
                sp.dma_start(out[0].rearrange("b s k d -> s b (k d)"), win[:]).then_inc(a_out, 16)
            sp.wait_ge(a_out, 32)

        @block.gpsimd
        def _(pool):
            mine = pool_steps.on(pool)
            nc.gpsimd.iota(dist_i[:], pattern=[[-1, 2 * P]], base=P, channel_multiplier=1).then_inc(iota_ready, 1)
            for h in range(H):
                mine(nc.gpsimd.memset(slope_s[:, h:h + 1], -SLOPES[h]))
            nc.gpsimd.iota(dist_s[:, 0:1].bitcast(I32), pattern=[[0, 1]], base=P - 1, channel_multiplier=-1).then_inc(iota_ready, 1)
            pool.wait_ge(alibi_raw, H)
            mine(nc.gpsimd.affine_select(out=alibi[:], in_=alibi[:], compare_op=ALU.is_ge, fill=NEG, base=P,
                                         pattern=[[0, H], [-1, 2 * P]], channel_multiplier=1))
            mine.settle()
            nc.gpsimd.affine_select(out=alibi[:], in_=alibi[:], compare_op=ALU.is_ge, fill=NEG, base=-1,
                                    pattern=[[0, H], [1, 2 * P]], channel_multiplier=-1).then_inc(alibi_ready, 1)

        @block.scalar
        def _(act):
            for j in range(2):
                act.wait_ge(wspT_banked, j + 1)
                nc.scalar.activation(wspT[:, 4 * j:4 * j + 4, :], bank[:, 4 + j, :], ACT.Copy).then_inc(wspT_ready, 1)
            act.wait_ge(kT_banked, 1)
            nc.scalar.activation(kT[:], bank[:, 6, :], ACT.Copy).then_inc(kT_ready, 1)
            for n in range(NT):
                act.wait_ge(qT_banked, n + 1)
                nc.scalar.activation(qT[:, n, :, :], bank[:, (7, 4, 5, 6)[n], :], ACT.Copy).then_inc(qT_ready, 1)

            def exps(u):
                n, g = UNITS[u]
                lo = P if n == 0 else 0
                st, pr = m_[u % 2], probs[u % 2]
                act.wait_ge(max_ready, u + 1)
                for i in range(HG):
                    nc.scalar.activation(pr[:, i, lo:2 * P], pr[:, i, lo:2 * P], ACT.Exp, bias=st[:, 1, i:i + 1],
                                         accum_out=st[:, 3, i:i + 1])
                nc.scalar.activation(st[:, 2, :], st[:, 2, :], ACT.Exp).then_inc(exp_ready, 1)

            for u in range(len(UNITS)):
                exps(u)
                if u >= 1:
                    turned(act, u - 1)
            turned(act, len(UNITS) - 1)
            for j in range(2):
                act.wait_ge(ksT_banked, j + 1)
                nc.scalar.activation(ksT[:, 4 * j:4 * j + 4, :], bank[:, j, :], ACT.Copy).then_inc(ksT_ready, 1)
            act.wait_ge(ksT_banked, 3)
            nc.scalar.activation(qsT[:], bank[:, 2, 0:HG * NS], ACT.Copy).then_inc(ksT_ready, 1)
            act.wait_ge(ss_cut, 2)
            nc.scalar.activation(s_exp[:], bank[0:NS * H, 4, 0:P], ACT.Exp, bias=s_st[:, 1:2], accum_out=s_st[:, 3:4])
            nc.scalar.activation(s_st[:, 2:3], s_st[:, 2:3], ACT.Exp).then_inc(ss_exp, 1)
            act.wait_ge(spT_done, 1)
            nc.scalar.activation(s_pT[:], bank[:, 5, 0:NS * H], ACT.Copy).then_inc(spT_ready, 1)
            act.wait_ge(sy_done, 1)
            pv = bank[:, 6, 0:NS * H].rearrange("p (b h) -> p h b", h=H)
            nc.scalar.activation(ysT[0:HD], pv[0:HD, 0:HG], ACT.Copy)
            nc.scalar.activation(ysT[HD:2 * HD], pv[HD:2 * HD, HG:H], ACT.Copy).then_inc(sy_cut, 1)
            act.wait_ge(syT_done, 1)
            nc.scalar.activation(uq[0:NS, NT, CB:2 * CB].rearrange("p (g i d) -> p i g d", g=KV, i=HG),
                                 bank[0:NS, 7, :].rearrange("p (i g d) -> p i g d", g=KV, i=HG), ACT.Copy).then_inc(sy_ready, 1)

        @block.vector
        def _(dve):
            mine = Signals(dve, a_dve)
            dve.wait_ge(iota_ready, 2)
            mine(nc.vector.tensor_copy(dist_f[:], dist_i[:]))
            mine(nc.vector.tensor_copy(dist_s[:, 1:2], dist_s[:, 0:1].bitcast(I32)))
            mine.settle()
            for h in range(H):
                nc.vector.tensor_scalar(alibi[:, h, :], dist_f[:], -SLOPES[h], None, ALU.mult).then_inc(alibi_raw, 1)
            dve.wait_ge(iota_ready, 2)
            mine(nc.vector.tensor_scalar(bias_s[:], slope_s[:], dist_s[:, 1:2], None, ALU.mult))
            for g in range(G):
                dve.wait_ge(gate_done, 2 * (g // 2) + 2)
                y = uq[:, 0:NT, g * HD:(g + 1) * HD]
                mine(nc.vector.scalar_tensor_tensor(y, bank[:, g // 2, (g % 2) * 256:(g % 2) * 256 + 256]
                     .rearrange("p (n d) -> p n d", n=NT), bspT[:, g:g + 1], y, ALU.add, ALU.mult), gate_read)
            vs = va[0:NS, NT, :].rearrange("p (g d) -> p g d", g=G)
            ys = uq[0:NS, NT, 0:CB].rearrange("p (g d) -> p g d", g=G)
            mine(nc.vector.tensor_tensor(vs, vs, w00[:].unsqueeze(2).to_broadcast([NS, G, HD]), ALU.mult))
            mine.settle()
            mine(nc.vector.tensor_tensor(vs, vs, b00[:].unsqueeze(2).to_broadcast([NS, G, HD]), ALU.add))
            mine.settle()
            mine(nc.vector.tensor_tensor(ys, ys, vs, ALU.mult))
            dve.wait_ge(alibi_ready, 1)

            def scores(u):
                n, g = UNITS[u]
                lo = P if n == 0 else 0
                st, pr = m_[u % 2], probs[u % 2]
                dve.wait_ge(score_done, u + 1)
                if u >= 2:
                    dve.wait_ge(pT_banked, u - 1)
                mine(nc.vector.scalar_tensor_tensor(pr[:, :, lo:2 * P], s_bank(u)[:, :, lo:2 * P], HD ** -0.5,
                     alibi[:, g * HG:(g + 1) * HG, lo:2 * P], ALU.mult, ALU.add), score_read)
                mine.settle()
                mine(nc.vector.tensor_reduce(st[:, 0, :], pr[:, :, lo:2 * P], AX, ALU.max))
                mine.settle()
                sk = sink_b[:, g * HG:(g + 1) * HG]
                mine(nc.vector.tensor_tensor(st[:, 0, :], st[:, 0, :], sk, ALU.max))
                mine.settle()
                mine(nc.vector.tensor_scalar(st[:, 1, :], st[:, 0, :], -1.0, None, ALU.mult))
                mine.settle()
                mine(nc.vector.tensor_tensor(st[:, 2, :], sk, st[:, 1, :], ALU.add), max_ready)

            def values(u):
                n, g = UNITS[u]
                st = m_[u % 2]
                dve.wait_ge(exp_ready, u + 1)
                mine(nc.vector.tensor_tensor(st[:, 4, :], st[:, 3, :], st[:, 2, :], ALU.add))
                mine.settle()
                mine(nc.vector.reciprocal(st[:, 5, :], st[:, 4, :]))
                mine.settle()
                dve.wait_ge(pv_done, u + 1)
                mine(nc.vector.tensor_tensor(
                    uq[:, n, CB + g * HG * HD:CB + (g + 1) * HG * HD].rearrange("p (i d) -> p i d", i=HG),
                    o_bank(u), st[:, 5, :].unsqueeze(2).to_broadcast([P, HG, HD]), ALU.mult), pv_read)

            for u in range(len(UNITS)):
                if u >= 2:
                    values(u - 2)
                scores(u)
            values(len(UNITS) - 2)
            values(len(UNITS) - 1)
            dve.wait_ge(ss_done, 1)
            for g in range(KV):
                h0 = g * HG
                ins = nc.vector.scalar_tensor_tensor(s_pre[:].rearrange("p (b h) -> p b h", h=H)[:, :, h0:h0 + HG],
                     bank[:, 2 + g, 0:NS * HG].rearrange("p (b h) -> p b h", h=HG), HD ** -0.5,
                     bias_s[:, h0:h0 + HG].unsqueeze(1).to_broadcast([P, NS, HG]), ALU.mult, ALU.add)
                mine(ins, ss_cut if g == KV - 1 else None)
            dve.wait_ge(ssT_done, 1)
            mine(nc.vector.tensor_reduce(s_st[:, 0:1], bank[0:NS * H, 4, 0:P], AX, ALU.max))
            mine.settle()
            mine(nc.vector.tensor_tensor(s_st[:, 0:1], s_st[:, 0:1], sink64[:], ALU.max))
            mine.settle()
            mine(nc.vector.tensor_scalar(s_st[:, 1:2], s_st[:, 0:1], -1.0, None, ALU.mult))
            mine.settle()
            mine(nc.vector.tensor_tensor(s_st[:, 2:3], sink64[:], s_st[:, 1:2], ALU.add), ss_cut)
            dve.wait_ge(ss_exp, 1)
            mine(nc.vector.tensor_tensor(s_st[:, 4:5], s_st[:, 3:4], s_st[:, 2:3], ALU.add))
            mine.settle()
            mine(nc.vector.reciprocal(s_st[:, 5:6], s_st[:, 4:5]))
            mine.settle()
            mine(nc.vector.tensor_scalar(s_exp[:], s_exp[:], s_st[:, 5:6], None, ALU.mult), ss_prob)

        @block.tensor
        def _(pe):
            for g in range(G):
                last = nc.tensor.transpose(bank[:, 4 + g // 4, (g % 4) * P:(g % 4 + 1) * P], wsp[:, g, :], ident[:])
                if g % 4 == 3:
                    last.then_inc(wspT_banked, 1)
            for n in range(NT):
                last = nc.tensor.transpose(bank[:, 6, n * P:(n + 1) * P], k_nat[:, n, :], ident[:])
            last.then_inc(kT_banked, 1)
            for n in range(NT):
                b = (7, 4, 5, 6)[n]
                if n >= 1:
                    pe.wait_ge(wspT_ready, 2)
                    pe.wait_ge(kT_ready, 1)
                for i in range(HG):
                    pair = uq[:, n, CB + i * P:CB + (i + 1) * P]
                    last = nc.tensor.transpose(bank[:, b, i * P:(i + 1) * P], pair, ident[:])
                last.then_inc(qT_banked, 1)
            pe.wait_ge(wspT_ready, 2)
            for g in range(G):
                last = nc.tensor.matmul(bank[:, g // 2, (g % 2) * 256:(g % 2) * 256 + 256], wspT[:, g, :],
                                        va[:, 0:NT, g * HD:(g + 1) * HD], start=True, stop=True)
                last.then_inc(gate_done, 1)
            pe.wait_ge(qT_ready, NT)
            pe.wait_ge(kT_ready, 1)
            pe.wait_ge(gate_read, G)

            def scores(u):
                n, g = UNITS[u]
                lo = P if n == 0 else 0
                if u >= 2:
                    pe.wait_ge(score_read, u - 1)
                for i in range(HG):
                    last = nc.tensor.matmul(s_bank(u)[:, i, lo:2 * P], qT[g * HD:(g + 1) * HD, n, i, :],
                                            kT[g * HD:(g + 1) * HD, (n - 1) * P + lo:(n + 1) * P],
                                            start=True, stop=True)
                last.then_inc(score_done, 1)

            def turn(u):
                n, g = UNITS[u]
                pe.wait_ge(exp_ready, u + 1)
                if u >= 1:
                    pe.wait_ge(pT_ready, u)
                js = (1,) if n == 0 else (0, 1)
                for i in range(HG):
                    for jj, j in enumerate(js):
                        x = i * len(js) + jj
                        last = nc.tensor.transpose(bank[:, 4 + x // 4, (x % 4) * P:(x % 4 + 1) * P],
                                                   probs[u % 2][:, i, j * P:(j + 1) * P], ident[:])
                last.then_inc(pT_banked, 1)

            def values(u):
                n, g = UNITS[u]
                pe.wait_ge(pT_ready, u + 1)
                if u >= 2:
                    pe.wait_ge(pv_read, u - 1)
                js = (1,) if n == 0 else (0, 1)
                for i in range(HG):
                    for jj, j in enumerate(js):
                        last = nc.tensor.matmul(o_bank(u)[:, i, :], pT[:, i * len(js) + jj, :],
                                                v_nat[:, n - 1 + j, g * HD:(g + 1) * HD],
                                                start=jj == 0, stop=j == 1)
                last.then_inc(pv_done, 1)

            scores(0)
            for u in range(len(UNITS)):
                if u + 1 < len(UNITS):
                    scores(u + 1)
                turn(u)
                values(u)
            pe.wait_ge(win_landed, 32)
            pe.wait_ge(win_new_landed, 32)
            pe.wait_ge(score_read, len(UNITS))
            for b in range(NS):
                last = nc.tensor.transpose(bank[:, b // 4, (b % 4) * P:(b % 4 + 1) * P], k_win[:, b, :], ident[:])
                if b % 4 == 3:
                    last.then_inc(ksT_banked, 1)
            for i in range(HG):
                pair = uq[0:NS, NT, CB + i * P:CB + (i + 1) * P]
                last = nc.tensor.transpose(bank[:, 2, i * NS:(i + 1) * NS], pair, ident[0:NS, 0:NS])
            last.then_inc(ksT_banked, 1)
            pe.wait_ge(ksT_ready, 3)
            for b in range(NS):
                for g in range(KV):
                    last = nc.tensor.matmul(bank[:, 2 + g, b * HG:(b + 1) * HG],
                                            ksT[g * HD:(g + 1) * HD, b, :], qsT[g * HD:(g + 1) * HD, :, b],
                                            start=True, stop=True)
            last.then_inc(ss_done, 1)
            pe.wait_ge(ss_cut, 1)
            nc.tensor.transpose(bank[0:NS * H, 4, 0:P], s_pre[:], ident[:]).then_inc(ssT_done, 1)
            pe.wait_ge(ss_prob, 1)
            nc.tensor.transpose(bank[:, 5, 0:NS * H], s_exp[:], ident[0:NS * H, 0:NS * H]).then_inc(spT_done, 1)
            pe.wait_ge(spT_ready, 1)
            pe.wait_ge(pv_read, len(UNITS))
            for b in range(NS):
                last = nc.tensor.matmul(bank[:, 6, b * H:(b + 1) * H], v_win[:, b, :], s_pT[:, b * H:(b + 1) * H],
                                        start=True, stop=True)
            last.then_inc(sy_done, 1)
            pe.wait_ge(sy_cut, 1)
            for i in range(HG):
                last = nc.tensor.transpose(bank[0:NS, 7, i * P:(i + 1) * P], ysT[:, i, :], ident[:])
            last.then_inc(syT_done, 1)

    x_res = [va, at("x_res_1", [P, TILES, CB], F32, SIDE)]
    junk = at("junk", [P, CB], F32, SIDE + 10240)
    assert TILES * CB * 4 <= 10240
    o = SIDE + 12288
    w_r = scratch("w_r", [P, KC, E])
    b_r = scratch("b_r", [P, E])
    iota_e = scratch("iota_e", [P, E])
    iota_128e = scratch("iota_128e", [P, E])
    before = scratch("before", [P, P])
    ones = scratch("ones", [P, P])
    iota_i = scratch("iota_i", [P, E], I32)
    assert o <= SIDE + 16384
    gain_o = gain
    hnT = at("hnT", [P, KC, P], F32, SIDE + 16384)
    gain_m = at("gain_m", [P, D], F32, SIDE + 20480)
    o = SIDE + 24576
    onehot = scratch("onehot", [P, TILES * TOPK, E])
    chosen = scratch("chosen", [P, TILES, E])
    slot_e = scratch("slot_e", [P, TILES, E])
    logits = scratch("logits", [P, TILES, E])
    assert o <= SIDE + 24576 + 2 * TILES * KVW * 4
    o = small + 832 + 2 * TABLE // P * 4
    o += -o % 32
    top = scratch("top", [P, TILES, 8])
    top_i = scratch("top_i", [P, TILES, 8], U32)
    top_f = scratch("top_f", [P, TILES * TOPK])
    gsum = scratch("gsum", [P, 2 * TILES])
    total = scratch("total", [P, E])
    extra = [scratch(f"extra_{i}", [P, E]) for i in range(3)]
    token_place = scratch("token_place", [P, TILES, TOPK, 2], I32)
    slot_i = scratch("slot_i", [P, TILES * TOPK], I32)
    slot_f = scratch("slot_f", [P, TILES * TOPK])
    assert o <= SIDE + 2 * TILE_B, o - SIDE - 2 * TILE_B
    hn = [at(f"hn_{i}", [P, D], F32, MAIN + 2 * XT_B + TILES * 2 * CB * 4 + i * D * 4) for i in range(2)]
    NB2 = OVER + 2
    iota_b = at("iota_b", [1, NB2], F32, MAIN)
    owner = at("owner", [1, NB2, E], F32, MAIN + 128)
    owner_f = at("owner_f", [1, NB2], F32, MAIN + 128 + NB2 * E * 4)
    blocks_f = at("blocks_f", [1, 1], F32, MAIN + 128 + NB2 * E * 4 + 128)
    product_prod = at("product_prod", [P, TILES * TOPK, E], F32, MAIN + 4096)
    LATE = MAIN + 2 * XT_B + TILES * 2 * CB * 4 + 2 * D * 4 + 512
    block_expert = at("block_expert", [1, NBMAX + 2], I32, LATE)
    n_extra = at("n_extra", [1, 1], I32, LATE + 256)

    r_dve, r_act = sem("r_dve"), sem("r_act")
    gain_o_landed, gain_m_landed, x_res_landed, router_landed = (sem("gain_o_landed"), sem("gain_m_landed"),
        [sem("x_res0_landed"), sem("x_res1_landed")], sem("router_landed"))
    y_ss, y_normed, yT_banked, yT_hi, yT_lo = sem("y_ss"), sem("y_normed"), sem("yT_banked"), sem("yT_hi"), sem("yT_lo")
    o_hi, o_lo, o_first, mix_done, h_ready = sem("o_hi"), sem("o_lo"), sem("o_first"), sem("mix_done"), sem("h_ready")
    h_ss, hn_ready, hnT_banked, hnT_ready, logit_done, logit_read = (sem("h_ss"), sem("hn_ready"), sem("hnT_banked"),
        sem("hnT_ready"), sem("logit_done"), sem("logit_read"))
    hn_stored, h_stored = [sem(f"hn_stored_{i}") for i in range(2)], sem("h_stored")
    route_consts, gate_in, gate_exp, chosen_ready, count_done, slots_ready, slots_stored = (sem(n) for n in (
        "route_consts", "gate_in", "gate_exp", "chosen_ready", "count_done", "slots_ready", "slots_stored"))
    o_used = used_after(o_first, mix_done)

    def rows_of(dram_rows, t):
        return dram_rows[t * P:t * P + ROWS[t]]

    def turned_h(act, t):
        R = ROWS[t]
        act.wait_ge(hnT_banked, t + 1)
        if t >= 1:
            act.wait_ge(logit_done, t)
        for j in range(2):
            last = nc.scalar.activation(hnT[:, 4 * j:4 * j + 4, 0:R],
                                        bank[:, 2 + j, 0:4 * R].rearrange("p (c r) -> p c r", c=4), ACT.Copy)
        last.then_inc(hnT_ready, 1)

    def choose(dve, mine, t):
        R = ROWS[t]
        dve.wait_ge(logit_done, t + 1)
        mine(nc.vector.tensor_tensor(logits[0:R, t, :], bank[0:R, 4 + 3 * (t % 2), 0:E], b_r[0:R, :], ALU.add), logit_read)
        mine.settle()
        mine(nc.vector.max(top[0:R, t, :], logits[0:R, t, :]))
        mine.settle()
        mine(nc.vector.max_index(top_i[0:R, t, :], top[0:R, t, :], logits[0:R, t, :]))

    with nc.Block() as block:
        @block.sync
        def _(sp):
            sp.dma_start(gain_m[:], g_moe[0:1, :].to_broadcast([P, D])).then_inc(gain_m_landed, 16)
            for w in range(2):
                cols = slice(w * CB, (w + 1) * CB)
                sp.dma_start(x_res[w][:, 0:NT, :], x_p[:, cols].rearrange("(n p) d -> p n d", p=P)).then_inc(x_res_landed[w], 16)
                sp.dma_start(x_res[w][0:NS, NT, :], x_s[:, cols]).then_inc(x_res_landed[w], 16)
            sp.dma_start(w_r[:], w_router[0].rearrange("(c p) e -> p c e", p=P)).then_inc(router_landed, 16)
            sp.dma_start(b_r[:], b_router[0:1, :].to_broadcast([P, E])).then_inc(router_landed, 16)
            for w in range(2):
                sp.wait_ge(o_hi, 2 * w + 2)
                sp.wait_ge(o_lo, 2 * w + 2)
                sp.dma_start(raw[w][:], w_gu_v[0, :, :, w * D:w * D + CB]).then_inc(raw_landed[w], 16)
            for t in range(TILES):
                sp.wait_ge(h_ready, TILES + t + 1)
                sp.dma_start(rows_of(h_rows, t), uq[0:ROWS[t], t, :]).then_inc(h_stored, 16)
                sp.wait_ge(hn_ready, t + 1)
                sp.dma_start(rows_of(hn_rows, t), hn[t % 2][0:ROWS[t], :]).then_inc(hn_stored[t % 2], 16)
            sp.wait_ge(h_stored, 16 * TILES)
            for i in range(2):
                sp.wait_ge(hn_stored[i], 16 * len(range(i, TILES, 2)))

        @block.gpsimd
        def _(pool):
            mine = pool_steps.on(pool)
            nc.gpsimd.iota(iota_i[:], pattern=[[1, E]], base=0, channel_multiplier=0)
            nc.gpsimd.iota(token_place[:, :, :, 0], pattern=[[P, TILES], [0, TOPK]], base=0, channel_multiplier=1)
            nc.gpsimd.iota(token_place[:, :, :, 1], pattern=[[P, TILES], [TOK, TOPK]], base=0, channel_multiplier=1)
            mine(nc.gpsimd.memset(before[:], 1.0))
            mine.settle()
            nc.gpsimd.memset(ones[:], 1.0)
            nc.gpsimd.affine_select(out=before[:], in_=before[:], compare_op=ALU.is_ge, fill=0.0, base=-1,
                                    pattern=[[1, P]], channel_multiplier=-1).then_inc(route_consts, 1)
            for t in range(TILES):
                for k in range(TOPK):
                    if t == 0 and k == 0:
                        pool.wait_ge(slots_ready, 1)
                    R, n = ROWS[t], t * TOPK + k
                    pool.indirect_dma_start(slot_table, bass.IndirectOffsetOnAxis(slot_i[0:R, n:n + 1], 0),
                                            token_place[0:R, t, k, :], None, bounds_check=TABLE - 1,
                                            oob_is_err=False).then_inc(slots_stored, 16)
            pool.wait_ge(slots_stored, 16 * TILES * TOPK)

        @block.scalar
        def _(act):
            mine = Signals(act, r_act)
            act.dma_start(gain_o[:, 0:CB], g_out_a[0:1, :].to_broadcast([P, CB])).then_inc(gain_o_landed, 16)
            act.dma_start(gain_o[:, CB:2 * CB], g_out_b[0:1, :].to_broadcast([P, CB])).then_inc(gain_o_landed, 16)
            for t in range(TILES):
                R, st = ROWS[t], stat[0:ROWS[t], 8 * t:8 * t + 8]
                for j in range(2):
                    if t + j > 0:
                        mine.settle()
                    mine(nc.scalar.activation(junk[0:R, :], uq[0:R, t, j * CB:(j + 1) * CB], ACT.Square,
                                              accum_out=st[:, j:j + 1]))
                mine.settle()
                nc.scalar.activation(st[:, 0:2], st[:, 0:2], ACT.Sqrt, scale=1.0 / CB, bias=EPS).then_inc(y_ss, 1)
            def hi(n):
                write_hi(act, n, n // 2, n % 2, CB, o_hi, o_used, 32)
            for n in range(LEAD):
                hi(n)
            for t in range(TILES):
                R, c0 = ROWS[t], column(t)
                act.wait_ge(yT_banked, t + 1)
                b = 2 * (t % 4)
                for j in range(2):
                    last = nc.scalar.activation(xT_hi[:, 4 * j:4 * j + 4, c0:c0 + R],
                                                bank[:, b + j, 0:4 * R].rearrange("p (c r) -> p c r", c=4), ACT.Copy)
                last.then_inc(yT_hi, 1)
            hi(3)
            for t in range(TILES):
                R = ROWS[t]
                act.wait_ge(h_ready, TILES + t + 1)
                if t >= 2:
                    act.wait_ge(hn_stored[t % 2], 16 * (t // 2))
                    act.wait_ge(hnT_banked, t - 1)
                elif t == 0:
                    act.wait_ge(h_ready, TILES)
                mine(nc.scalar.activation(hn[t % 2][0:R, :], uq[0:R, t, :], ACT.Square, accum_out=ss(t)))
                mine.settle()
                mine(nc.scalar.activation(ss(t), ss(t), ACT.Sqrt, scale=1.0 / D, bias=EPS), h_ss)
                if t >= 1:
                    turned_h(act, t - 1)
            turned_h(act, TILES - 1)
            act.wait_ge(gate_in, 1)
            nc.scalar.activation(gates[:], gates[:], ACT.Exp).then_inc(gate_exp, 1)

        @block.vector
        def _(dve):
            mine = Signals(dve, r_dve)

            def lo(n):
                write_lo(dve, n, n // 2, n % 2, CB, o_hi, o_lo, o_used, 32)
            dve.wait_ge(gain_o_landed, 32)
            mine(nc.vector.memset(top[:], 0.0))
            mine(nc.vector.memset(top_i[:], 0))
            for t in range(TILES):
                R, st = ROWS[t], stat[0:ROWS[t], 8 * t:8 * t + 8]
                dve.wait_ge(y_ss, t + 1)
                mine(nc.vector.reciprocal(st[:, 2:4], st[:, 0:2]))
                mine.settle()
                for j in range(2):
                    part = uq[0:R, t, j * CB:(j + 1) * CB]
                    ins = nc.vector.scalar_tensor_tensor(part, part, st[:, 2 + j:3 + j], gain_o[0:R, j * CB:(j + 1) * CB],
                                                         ALU.mult, ALU.mult)
                    mine(ins, y_normed if j == 1 else None)
            for n in range(LEAD):
                lo(n)
            for t in range(TILES):
                R, c0 = ROWS[t], column(t)
                dve.wait_ge(yT_banked, t + 1)
                dve.wait_ge(yT_hi, t + 1)
                b = 2 * (t % 4)
                for j in range(2):
                    last = nc.vector.tensor_tensor(xT_lo[:, 4 * j:4 * j + 4, c0:c0 + R],
                                                   bank[:, b + j, 0:4 * R].rearrange("p (c r) -> p c r", c=4),
                                                   xT_hi[:, 4 * j:4 * j + 4, c0:c0 + R].bitcast(F32), ALU.subtract)
                last.then_inc(yT_lo, 1)
            lo(3)
            for w in range(2):
                dve.wait_ge(x_res_landed[w], 32)
                for t in range(TILES):
                    R = ROWS[t]
                    dve.wait_ge(mix_done, TILES * w + t + 1)
                    mine(nc.vector.tensor_tensor(uq[0:R, t, w * CB:(w + 1) * CB], bank[0:R, zbank(w, t), :],
                                                 x_res[w][0:R, t, :], ALU.add), h_ready)
            dve.wait_ge(gain_m_landed, 16)
            dve.wait_ge(router_landed, 32)
            dve.wait_ge(route_consts, 1)
            mine(nc.vector.tensor_copy(iota_e[:], iota_i[:]))
            mine.settle()
            mine(nc.vector.tensor_scalar(iota_128e[:], iota_e[:], float(P), None, ALU.mult))
            for t in range(TILES):
                R = ROWS[t]
                dve.wait_ge(h_ss, t + 1)
                mine(nc.vector.reciprocal(rstd(t), ss(t)))
                mine.settle()
                mine(nc.vector.scalar_tensor_tensor(hn[t % 2][0:R, :], uq[0:R, t, :], rstd(t), gain_m[0:R, :],
                                                    ALU.mult, ALU.mult), hn_ready)
                if t >= 1:
                    choose(dve, mine, t - 1)
            choose(dve, mine, TILES - 1)
            mine.settle()
            mine(nc.vector.tensor_tensor(gates[:], top[:, :, 0:TOPK], top[:, :, 0:1].to_broadcast([P, TILES, TOPK]),
                                         ALU.subtract), gate_in)
            mine(nc.vector.tensor_copy(top_f[:].rearrange("p (t k) -> p t k", k=TOPK), top_i[:, :, 0:TOPK]))
            mine.settle()
            mine(nc.vector.tensor_tensor(onehot[:], iota_e[:].unsqueeze(1).to_broadcast([P, TILES * TOPK, E]),
                                         top_f[:].unsqueeze(2).to_broadcast([P, TILES * TOPK, E]), ALU.is_equal))
            mine.settle()
            by_choice = onehot[:].rearrange("p (t k) e -> p t e k", k=TOPK)
            mine(nc.vector.tensor_reduce(chosen[:], by_choice, AX, ALU.add), chosen_ready)
            dve.wait_ge(count_done, 1)
            mine(nc.vector.tensor_copy(total[:], bank[:, 6, 0:E]))
            mine.settle()
            mine(nc.vector.tensor_scalar(extra[0][:], total[:], float(P), None, ALU.is_gt))
            for j in range(2, -(-TOK // P)):
                mine.settle()
                mine(nc.vector.scalar_tensor_tensor(extra[0][:], total[:], float(j * P), extra[0][:], ALU.is_gt, ALU.add))
            mine.settle()
            mine(nc.vector.tensor_tensor_scan(extra[1][:], ones[:, 0:E], extra[0][:], 0.0, ALU.mult, ALU.add))
            mine.settle()
            mine(nc.vector.tensor_tensor(extra[2][:], extra[1][:], extra[0][:], ALU.subtract))
            mine.settle()
            mine(nc.vector.tensor_tensor(extra[2][:], extra[2][:], iota_e[:], ALU.subtract))
            mine.settle()
            mine(nc.vector.tensor_scalar(extra[2][:], extra[2][:], float(P), float((E - 1) * P), ALU.mult, ALU.add))
            mine.settle()
            position = bank[:, 5, 0:TILES * E].rearrange("p (t e) -> p t e", e=E)
            mine(nc.vector.tensor_scalar(slot_e[:], position, float(P), None, ALU.is_ge))
            mine.settle()
            mine(nc.vector.tensor_tensor(slot_e[:], slot_e[:], extra[2][:].unsqueeze(1).to_broadcast([P, TILES, E]), ALU.mult))
            mine.settle()
            mine(nc.vector.tensor_tensor(slot_e[:], slot_e[:], iota_128e[:].unsqueeze(1).to_broadcast([P, TILES, E]), ALU.add))
            mine.settle()
            mine(nc.vector.tensor_tensor(slot_e[:], slot_e[:], position, ALU.add))
            mine.settle()
            mine(nc.vector.tensor_tensor(product_prod[:].rearrange("p (t k) e -> p t k e", k=TOPK),
                                         onehot[:].rearrange("p (t k) e -> p t k e", k=TOPK),
                                         slot_e[:].unsqueeze(2).to_broadcast([P, TILES, TOPK, E]), ALU.mult))
            mine.settle()
            mine(nc.vector.tensor_reduce(slot_f[:], product_prod[:], AX, ALU.add))
            mine.settle()
            mine(nc.vector.tensor_copy(slot_i[:], slot_f[:]), slots_ready)
            mine(nc.vector.tensor_scalar(iota_b[:], iota_e[0:1, 0:NB2], 1.0, None, ALU.mult))
            mine.settle()
            mine(nc.vector.tensor_tensor(owner[:], iota_b[:].unsqueeze(2).to_broadcast([1, NB2, E]),
                                         extra[1][0:1, :].unsqueeze(1).to_broadcast([1, NB2, E]), ALU.is_ge))
            mine.settle()
            mine(nc.vector.tensor_reduce(owner_f[:], owner[:], AX, ALU.add))
            mine.settle()
            mine(nc.vector.tensor_copy(block_expert[0:1, 0:E], iota_i[0:1, :]))
            mine(nc.vector.tensor_scalar(block_expert[0:1, E:], owner_f[:], float(E - 1), None, ALU.min))
            mine(nc.vector.tensor_copy(n_extra[:], extra[1][0:1, E - 1:E]))
            dve.wait_ge(gate_exp, 1)
            mine(nc.vector.tensor_reduce(gsum[:, 0:TILES], gates[:], AX, ALU.add))
            mine.settle()
            mine(nc.vector.reciprocal(gsum[:, TILES:2 * TILES], gsum[:, 0:TILES]))
            mine.settle()
            mine(nc.vector.tensor_tensor(gates[:], gates[:], gsum[:, TILES:2 * TILES].unsqueeze(2).to_broadcast([P, TILES, TOPK]),
                                         ALU.mult))
            mine.settle()
            mine(nc.vector.tensor_tensor(product_prod[:], onehot[:],
                                         gates[:].rearrange("p t k -> p (t k)").unsqueeze(2).to_broadcast([P, TILES * TOPK, E]),
                                         ALU.mult))
            mine.settle()
            mine(nc.vector.tensor_reduce(gate_table[:], product_prod[:].rearrange("p (t k) e -> p t e k", k=TOPK), AX, ALU.add))

        @block.tensor
        def _(pe):
            for t in range(TILES):
                R = ROWS[t]
                pe.wait_ge(y_normed, t + 1)
                if t == 4:
                    pe.wait_ge(yT_lo, 1)
                for c in range(KC):
                    last = nc.tensor.transpose(bank[:, 2 * (t % 4) + c // 4, (c % 4) * R:(c % 4 + 1) * R],
                                               uq[0:R, t, c * P:(c + 1) * P], ident[0:R, 0:R])
                last.then_inc(yT_banked, 1)
            pe.wait_ge(yT_hi, TILES)
            pe.wait_ge(yT_lo, TILES)
            for n in range(4):
                w, h = n // 2, n % 2
                pe.wait_ge(o_hi, n + 1)
                pe.wait_ge(o_lo, n + 1)
                for t in range(TILES):
                    if h == 0 and TILES * w + t >= 8:
                        pe.wait_ge(h_ready, TILES * w + t - 7)
                    last = product(nc, bank[:, zbank(w, t), :], stationary(xT_hi, t), stationary(xT_lo, t),
                                   half_hi[n % LEAD], half_lo[n % LEAD],
                                   [(h * HALFK + k, k) for k in range(HALFK)], CB, h == 0, h == 1)
                    if h == 1:
                        last.then_inc(mix_done, 1)
                if h == 0:
                    last.then_inc(o_first, 1)
            pe.wait_ge(router_landed, 32)
            pe.wait_ge(h_ready, TILES + 3)
            for t in range(TILES):
                R = ROWS[t]
                pe.wait_ge(hn_ready, t + 1)
                if t >= 1:
                    pe.wait_ge(hnT_ready, t)
                for c in range(KC):
                    last = nc.tensor.transpose(bank[:, 2 + c // 4, (c % 4) * R:(c % 4 + 1) * R],
                                               hn[t % 2][0:R, c * P:(c + 1) * P], ident[0:R, 0:R])
                last.then_inc(hnT_banked, 1)
                pe.wait_ge(hnT_ready, t + 1)
                if t >= 2:
                    pe.wait_ge(logit_read, t - 1)
                for c in range(KC):
                    last = nc.tensor.matmul(bank[0:R, 4 + 3 * (t % 2), 0:E], hnT[:, c, 0:R], w_r[:, c, :],
                                            start=c == 0, stop=c == KC - 1)
                last.then_inc(logit_done, 1)
            pe.wait_ge(chosen_ready, 1)
            pe.wait_ge(route_consts, 1)
            for t in range(TILES):
                R = ROWS[t]
                for s in range(t):
                    nc.tensor.matmul(bank[0:R, 5, t * E:(t + 1) * E], ones[:, 0:R], chosen[:, s, :], start=s == 0, stop=False)
                nc.tensor.matmul(bank[0:R, 5, t * E:(t + 1) * E], before[0:R, 0:R], chosen[0:R, t, :], start=t == 0, stop=True)
            for t in range(TILES):
                last = nc.tensor.matmul(bank[:, 6, 0:E], ones[0:ROWS[t], :], chosen[0:ROWS[t], t, :],
                                        start=t == 0, stop=t == TILES - 1)
            last.then_inc(count_done, 1)

    o = MAIN
    xg = scratch("xg", [P, D])
    xg_hi = scratch("xg_hi", [P, KC, P], F32R)
    xg_lo = scratch("xg_lo", [P, KC, P], F32R)
    gate_sb = scratch("gate_sb", [P, CB])
    up_sb = scratch("up_sb", [P, CB])
    sig_sb = scratch("sig_sb", [P, CB])
    acts = scratch("acts", [P, D])
    aT_hi = scratch("aT_hi", [P, KC, P], F32R)
    aT_lo = scratch("aT_lo", [P, KC, P], F32R)
    y_sb = scratch("y_sb", [P, D])
    bias_sb = scratch("bias_sb", [34, D], F32R)
    ones_r = scratch("ones_r", [34, P], F32R)
    idx_in = scratch("idx_in", [P, 2], I32)
    idx_out = scratch("idx_out", [P, 2], I32)
    assert o <= LATE

    e_dve, indices_seen = sem("e_dve"), sem("indices_seen")
    hi_ready, lo_ready, half_used = sem("hi_ready"), sem("lo_ready"), sem("half_used")
    xg_clear, ones_ready, xg_landed, bias_landed, idx_in_landed, idx_out_landed, y_stored = (sem(n) for n in (
        "xg_clear", "ones_ready", "xg_landed", "bias_landed", "idx_in_landed", "idx_out_landed", "y_stored"))
    xg_turned, xg_hi_ready, xg_lo_ready = sem("xg_turned"), sem("xg_hi_ready"), sem("xg_lo_ready")
    acts_turned, aT_hi_ready, aT_lo_ready = sem("acts_turned"), sem("aT_hi_ready"), sem("aT_lo_ready")
    gate_ready, up_read, sig_ready, acts_ready, y_ready = (sem("gate_ready"), sem("up_read"), sem("sig_ready"),
                                                           sem("acts_ready"), sem("y_ready"))

    def half(b, h):
        return h if isinstance(b, int) and b == 0 else 12 * b - 4 + h

    def slot(b, h):
        return h % LEAD if isinstance(b, int) and b == 0 else (h - 4) % LEAD

    def landed(b, h):
        s = h // 2
        return s, 16 * (b + 3) if s < 2 else 16 * (b + 2) if s < 4 else 16 * b

    def down_half(last):
        return 0 if last else 8

    def blocks(engine):
        return engine.value_load(n_extra[0:1, 0:1], min_val=0, max_val=OVER) + E

    def expert_of(engine, b):
        return b if isinstance(b, int) else engine.value_load(block_expert[0:1, bass.ds(b, 1)], min_val=0, max_val=E - 1)

    with nc.Block() as block:
        @block.sync
        def _(sp):
            def free(b, h):
                sp.wait_ge(hi_ready, half(b, h) + 1)
                sp.wait_ge(lo_ready, half(b, h) + 1)

            def gate_up(b):
                e = expert_of(sp, b)
                for s in range(4):
                    free(b - 1, 2 * s + 1)
                    c0 = (s % 2) * D + (s // 2) * CB
                    sp.dma_start(raw[s][:], w_gu_v[e, :, :, c0:c0 + CB]).then_inc(raw_landed[s], 16)

            def down(b, first=False):
                e = expert_of(sp, b - 1)
                for s in range(2):
                    if not first:
                        free(b - 1, 9 + 2 * s)
                    sp.dma_start(raw[4 + s][:], w_dn_v[e, :, :, s * CB:(s + 1) * CB]).then_inc(raw_landed[4 + s], 16)

            nb = blocks(sp)
            down(1, first=True)
            gate_up(1)
            with sp.Fori(2, nb) as b:
                gate_up(b)
                down(b)
            down(nb)
            for s in range(2):
                free(nb - 1, 2 * s + 1)
                sp.dma_start(raw[s][:], w_pg_v[:, :, s * CB:(s + 1) * CB]).then_inc(raw_landed[s], 16)
            free(nb - 1, 5)
            sp.dma_start(raw[2][:].rearrange("p c n -> p (c n)")[:, 0:PC * D].rearrange("p (c n) -> p c n", c=PC),
                         w_pp_v).then_inc(raw_landed[2], 16)

        @block.gpsimd
        def _(pool):
            nb = blocks(pool)
            last_token, last_row = pool.to_reg(TOK - 1), pool.to_reg(TOPK * TOK - 1)

            def fetch(b):
                pool.dma_start(idx_in[:], slot_table[b * P:(b + 1) * P, :] if isinstance(b, int)
                               else slot_table[bass.ds(b * P, P), :]).then_inc(idx_in_landed, 16)
                pool.wait_ge(idx_in_landed, 16 * (b + 1))
                if not isinstance(b, int) or b >= 1:
                    pool.wait_ge(xg_turned, b)
                pool.sem_inc(indices_seen, 1)
                pool.indirect_dma_start(xg[:], None, hn_rows, bass.IndirectOffsetOnAxis(idx_in[:, 0:1], 0),
                                        bounds_check=last_token, oob_is_err=False).then_inc(xg_landed, 16)
                pool.wait_ge(xg_landed, 16 * (b + 1))

            def bias(b):
                e = expert_of(pool, b)
                if not isinstance(b, int) or b >= 1:
                    pool.wait_ge(half_used, half(b - 1, 7) + 1)
                for s in range(2):
                    pool.dma_start(bias_sb[32 * s:32 * s + 2, :].bitcast(F32), bias_rows[e, s]).then_inc(bias_landed, 16)

            def store(b):
                pool.dma_start(idx_out[:], slot_table[bass.ds(b * P, P), :] if not isinstance(b, int)
                               else slot_table[b * P:(b + 1) * P, :]).then_inc(idx_out_landed, 16)
                pool.wait_ge(idx_out_landed, 16 * (b + 1))
                pool.wait_ge(y_ready, 2 * (b + 1))
                pool.sem_inc(indices_seen, 1)
                pool.indirect_dma_start(expert_rows, bass.IndirectOffsetOnAxis(idx_out[:, 1:2], 0), y_sb[:], None,
                                        bounds_check=last_row, oob_is_err=False).then_inc(y_stored, 16)
                pool.wait_ge(y_stored, 16 * (b + 1))

            pool.wait_ge(xg_clear, 1)
            fetch(0)
            bias(0)
            fetch(1)
            bias(1)
            fetch(2)
            bias(2)
            fetch(3)
            store(0)
            with pool.Fori(2, nb) as b:
                bias(b + 1)
                fetch(b + 2)
                store(b - 1)
            store(nb - 1)

        @block.scalar
        def _(act):
            nb = blocks(act)

            def hi(b, h, down=0):
                s, value = landed(b, h + down)
                act.wait_ge(raw_landed[s], value)
                if not isinstance(b, int) or half(b, h) >= LEAD:
                    act.wait_ge(half_used, half(b, h) - LEAD + 1)
                nc.scalar.activation(half_hi[slot(b, h)][:], raw_half(s, h % 2), ACT.Copy).then_inc(hi_ready, 1)

            def x_hi(b):
                act.wait_ge(xg_turned, b + 1)
                for j in range(2):
                    last = nc.scalar.activation(xg_hi[:, 4 * j:4 * j + 4, :], bank[:, 6 + j, :], ACT.Copy)
                last.then_inc(xg_hi_ready, 1)

            def a_hi(b, p):
                act.wait_ge(acts_turned, 2 * b + p + 1)
                nc.scalar.activation(aT_hi[:, 4 * p:4 * p + 4, :], bank[:, 6 + p, :], ACT.Copy).then_inc(aT_hi_ready, 1)

            def sigmoid(b, p):
                act.wait_ge(gate_ready, 2 * b + p + 1)
                if not isinstance(b, int) or b + p > 0:
                    act.wait_ge(acts_ready, 2 * b + p)
                nc.scalar.activation(sig_sb[:], gate_sb[:], ACT.Sigmoid, scale=ALPHA).then_inc(sig_ready, 1)

            def y_out(b, s, last=False):
                act.wait_ge(half_used, half(b + 1, down_half(last) + 2 * s + 1) + 1)
                if s == 0 and (not isinstance(b, int) or b >= 1):
                    act.wait_ge(y_stored, 16 * b)
                nc.scalar.activation(y_sb[:, s * CB:(s + 1) * CB], bank[:, 4 + s, :], ACT.Copy).then_inc(y_ready, 1)

            def turn(b, down, carried):
                hi(b, 0)
                hi(b, 1)
                if carried:
                    y_out(b - 2, 1)
                if down:
                    a_hi(b - 1, 0)
                for h in (2, 3, 4, 5):
                    hi(b, h)
                if down:
                    a_hi(b - 1, 1)
                hi(b, 6)
                sigmoid(b, 0)
                hi(b, 7)
                if down:
                    hi(b, 8)
                    hi(b, 9)
                    hi(b, 10)
                x_hi(b + 1)
                sigmoid(b, 1)
                if down:
                    hi(b, 11)
                    y_out(b - 1, 0)

            x_hi(0)
            turn(0, False, False)
            turn(1, True, False)
            with act.Fori(2, nb) as b:
                turn(b, True, True)
            y_out(nb - 2, 1)
            a_hi(nb - 1, 0)
            hi(nb, 0, 8)
            hi(nb, 1, 8)
            hi(nb, 2, 8)
            a_hi(nb - 1, 1)
            hi(nb, 3, 8)
            y_out(nb - 1, 0, True)
            y_out(nb - 1, 1, True)

        @block.vector
        def _(dve):
            mine = Signals(dve, e_dve)
            nb = blocks(dve)

            def lo(b, h, down=0):
                s, value = landed(b, h + down)
                dve.wait_ge(raw_landed[s], value)
                dve.wait_ge(hi_ready, half(b, h) + 1)
                if not isinstance(b, int) or half(b, h) >= LEAD:
                    dve.wait_ge(half_used, half(b, h) - LEAD + 1)
                mine(nc.vector.tensor_tensor(half_lo[slot(b, h)][:], raw_half(s, h % 2),
                                             half_hi[slot(b, h)][:].bitcast(F32), ALU.subtract), lo_ready)

            def x_lo(b):
                dve.wait_ge(xg_turned, b + 1)
                dve.wait_ge(xg_hi_ready, b + 1)
                for j in range(2):
                    last = nc.vector.tensor_tensor(xg_lo[:, 4 * j:4 * j + 4, :], bank[:, 6 + j, :],
                                                   xg_hi[:, 4 * j:4 * j + 4, :].bitcast(F32), ALU.subtract)
                mine(last, xg_lo_ready)

            def a_lo(b, p):
                dve.wait_ge(acts_turned, 2 * b + p + 1)
                dve.wait_ge(aT_hi_ready, 2 * b + p + 1)
                mine(nc.vector.tensor_tensor(aT_lo[:, 4 * p:4 * p + 4, :], bank[:, 6 + p, :],
                                             aT_hi[:, 4 * p:4 * p + 4, :].bitcast(F32), ALU.subtract), aT_lo_ready)

            def clamp(b, p):
                dve.wait_ge(half_used, half(b, 4 * p + 3) + 1)
                mine.settle()
                mine(nc.vector.tensor_scalar(gate_sb[:], bank[:, 2 * p, :], LIMIT, None, ALU.min), gate_ready)
                mine(nc.vector.tensor_scalar(up_sb[:], bank[:, 2 * p + 1, :], -LIMIT, LIMIT, ALU.max, ALU.min), up_read)
                mine.settle()
                mine(nc.vector.scalar_tensor_tensor(up_sb[:], up_sb[:], 1.0, gate_sb[:], ALU.add, ALU.mult))

            def activate(b, p):
                dve.wait_ge(sig_ready, 2 * b + p + 1)
                mine.settle()
                if not isinstance(b, int) or b >= 1:
                    dve.wait_ge(acts_turned, 2 * (b - 1) + p + 1)
                mine(nc.vector.tensor_tensor(acts[:, p * CB:(p + 1) * CB], up_sb[:], sig_sb[:], ALU.mult), acts_ready)

            def turn(b, down):
                lo(b, 0)
                lo(b, 1)
                if down:
                    a_lo(b - 1, 0)
                for h in (2, 3, 4, 5):
                    lo(b, h)
                if down:
                    a_lo(b - 1, 1)
                clamp(b, 0)
                lo(b, 6)
                activate(b, 0)
                lo(b, 7)
                if down:
                    lo(b, 8)
                    lo(b, 9)
                    lo(b, 10)
                x_lo(b + 1)
                clamp(b, 1)
                if down:
                    lo(b, 11)
                activate(b, 1)

            mine(nc.vector.memset(xg[:], 0.0), xg_clear)
            mine(nc.vector.memset(ones_r[:].bitcast(F32), 1.0), ones_ready)
            x_lo(0)
            turn(0, False)
            turn(1, True)
            grows = {lo_ready: 12, xg_lo_ready: 1, aT_lo_ready: 2, gate_ready: 2, up_read: 2, e_dve: 2, acts_ready: 2}
            with dve.Fori(2, nb) as b:
                mine.enter_loop(b - 2, grows)
                turn(b, True)
            mine.leave_loop(nb - 2)
            a_lo(nb - 1, 0)
            lo(nb, 0, 8)
            lo(nb, 1, 8)
            lo(nb, 2, 8)
            a_lo(nb - 1, 1)
            lo(nb, 3, 8)

        @block.tensor
        def _(pe):
            nb = blocks(pe)

            def taken(b, h):
                pe.wait_ge(hi_ready, half(b, h) + 1)
                pe.wait_ge(lo_ready, half(b, h) + 1)

            def turn_x(b):
                pe.wait_ge(xg_landed, 16 * (b + 1))
                if not isinstance(b, int) or b >= 2:
                    pe.wait_ge(aT_hi_ready, 2 * (b - 1))
                    pe.wait_ge(aT_lo_ready, 2 * (b - 1))
                for c in range(KC):
                    last = nc.tensor.transpose(bank[:, 6 + c // 4, (c % 4) * P:(c % 4 + 1) * P],
                                               xg[:, c * P:(c + 1) * P], ident[:])
                last.then_inc(xg_turned, 1)

            def turn_acts(b, p):
                pe.wait_ge(acts_ready, 2 * b + p + 1)
                pe.wait_ge(xg_hi_ready, b + 2)
                pe.wait_ge(xg_lo_ready, b + 2)
                for c in range(4):
                    last = nc.tensor.transpose(bank[:, 6 + p, c * P:(c + 1) * P],
                                               acts[:, p * CB + c * P:p * CB + (c + 1) * P], ident[:])
                last.then_inc(acts_turned, 1)

            def gate_up(b, p):
                if not isinstance(b, int) or b >= 1:
                    pe.wait_ge(up_read, 2 * (b - 1) + p + 1)
                if p == 0:
                    pe.wait_ge(bias_landed, 32 * (b + 1))
                    pe.wait_ge(xg_hi_ready, b + 1)
                    pe.wait_ge(xg_lo_ready, b + 1)
                for s in range(2):
                    out = bank[:, 2 * p + s, :]
                    nc.tensor.matmul(out, ones_r[32 * s:32 * s + 2, :], bias_sb[32 * s:32 * s + 2, p * CB:(p + 1) * CB],
                                     start=True, stop=False)
                    for i in range(2):
                        h = 4 * p + 2 * s + i
                        taken(b, h)
                        product(nc, out, lambda c: xg_hi[:, c, :], lambda c: xg_lo[:, c, :], half_hi[slot(b, h)],
                                half_lo[slot(b, h)], [(i * HALFK + k, k) for k in range(HALFK)], CB, False, i == 1
                                ).then_inc(half_used, 1)

            def down(b, last=False):
                pe.wait_ge(aT_hi_ready, 2 * b)
                pe.wait_ge(aT_lo_ready, 2 * b)
                for s in range(2):
                    if not isinstance(b, int) or b >= 2:
                        pe.wait_ge(y_ready, 2 * (b - 2) + s + 1)
                    for i in range(2):
                        h = down_half(last) + 2 * s + i
                        taken(b, h)
                        product(nc, bank[:, 4 + s, :], lambda c: aT_hi[:, c, :], lambda c: aT_lo[:, c, :],
                                half_hi[slot(b, h)], half_lo[slot(b, h)], [(i * HALFK + k, k) for k in range(HALFK)],
                                CB, i == 0, i == 1).then_inc(half_used, 1)

            def turn(b, has_down):
                gate_up(b, 0)
                if has_down:
                    turn_acts(b - 1, 1)
                gate_up(b, 1)
                turn_x(b + 1)
                if has_down:
                    down(b)
                turn_acts(b, 0)

            pe.wait_ge(ones_ready, 1)
            turn_x(0)
            turn(0, False)
            turn(1, True)
            with pe.Fori(2, nb) as b:
                turn(b, True)
            turn_acts(nb - 1, 1)
            down(nb, True)

    o = RAW + 3 * TILE_B
    wg_hi = scratch("wg_hi", [P, KC, D], F32R)
    wg_lo = scratch("wg_lo", [P, KC, D], F32R)
    wp_hi = scratch("wp_hi", [P, PC, D], F32R)
    wp_lo = scratch("wp_lo", [P, PC, D], F32R)
    gain_p = scratch("gain_p", [P, D])
    gain_f = scratch("gain_f", [P, D])
    b_down = scratch("b_down", [E, D])
    ple_in = [scratch(f"ple_in_{i}", [P, PLE]) for i in range(2)]
    gT = scratch("gT", [E, P])
    f_stat = scratch("f_stat", [P, 8 * TILES])
    assert o <= MAIN
    o = MAIN
    y_in = [scratch(f"y_in_{i}", [P, TOPK, D]) for i in range(2)]
    h_in = [scratch(f"h_in_{i}", [P, D]) for i in range(2)]
    f_norm = scratch("f_norm", [P, D])
    sg = scratch("sg", [P, D])
    fT_hi = scratch("fT_hi", [P, KC, P], F32R)
    fT_lo = scratch("fT_lo", [P, KC, P], F32R)
    pT_hi = scratch("pT_hi", [P, PC, P], F32R)
    pT_lo = scratch("pT_lo", [P, PC, P], F32R)
    assert o <= keep, o - keep

    f_act, f_dve = sem("f_act"), sem("f_dve")
    f_consts, h_in_landed, y_in_landed, ple_landed = (sem("f_consts"), [sem(f"h_in_landed_{i}") for i in range(2)],
        [sem(f"y_in_landed_{i}") for i in range(2)], [sem(f"ple_landed_{i}") for i in range(2)])
    wg_hi_ready, wg_lo_ready = sem("wg_hi_ready"), sem("wg_lo_ready")
    gT_banked, gT_ready, bdn_done, pT_in_banked, pT_hi_ready, pT_lo_ready = (sem(n) for n in (
        "gT_banked", "gT_ready", "bdn_done", "ple_banked", "ple_hi_ready", "ple_lo_ready"))
    moe_ready, f_ss, f_normed, fT_banked, fT_hi_ready, fT_lo_ready = (sem(n) for n in (
        "moe_ready", "f_ss", "f_normed", "fT_banked", "fT_hi_ready", "fT_lo_ready"))
    ple_done, sg_ready, out_ready, out_ss, y_final, out_stored = (sem(n) for n in (
        "ple_done", "sg_ready", "out_ready", "out_ss", "y_final", "out_stored"))
    y_by_token = expert_rows.rearrange("(k t) n -> t k n", k=TOPK)
    y_p, y_s = y_prompt[0], y_sample[:, 0, :]
    raw_pp = raw[2][:].rearrange("p c n -> p (c n)")[:, 0:PC * D].rearrange("p (c n) -> p c n", c=PC)

    with nc.Block() as block:
        @block.sync
        def _(sp):
            sp.dma_start(gain_p[:], g_ple[0:1, :].to_broadcast([P, D])).then_inc(f_consts, 16)
            sp.dma_start(b_down[:], b_dn[0]).then_inc(f_consts, 16)
            sp.dma_start(gain_f[:], g_final.rearrange("(o d) -> o d", o=1).to_broadcast([P, D])).then_inc(f_consts, 16)
            for t in range(TILES):
                R, i = ROWS[t], t % 2
                if t >= 2:
                    sp.wait_ge(out_stored, 16 * (t - 1))
                sp.dma_start(h_in[i][0:R, :], rows_of(h_rows, t)).then_inc(h_in_landed[i], 16)
                sp.dma_start(y_in[i][0:R], rows_of(y_by_token, t)).then_inc(y_in_landed[i], 16)
                if t >= 2:
                    sp.wait_ge(pT_in_banked, t - 1)
                sp.dma_start(ple_in[i][0:R, :], tokens(p_prompt[0, 0], p_sample[0, :, 0, :], t)).then_inc(ple_landed[i], 16)
                if t >= 1:
                    sp.wait_ge(y_final, t)
                    sp.dma_start(tokens(y_p, y_s, t - 1), h_in[1 - i][0:ROWS[t - 1], :]).then_inc(out_stored, 16)
            sp.wait_ge(y_final, TILES)
            sp.dma_start(tokens(y_p, y_s, NT), h_in[NT % 2][0:ROWS[NT], :]).then_inc(out_stored, 16)
            sp.wait_ge(out_stored, 16 * TILES)

        @block.scalar
        def _(act):
            mine = Signals(act, f_act)
            nb = blocks(act)

            def early(t):
                R, i = ROWS[t], t % 2
                act.wait_ge(gT_banked, t + 1)
                nc.scalar.activation(gT[:, 0:R], bank[0:E, 3, 0:R], ACT.Copy).then_inc(gT_ready, 1)
                act.wait_ge(pT_in_banked, t + 1)
                nc.scalar.activation(pT_hi[:, :, 0:R], bank[:, 2, 0:PC * R].rearrange("p (c r) -> p c r", c=PC),
                                     ACT.Copy).then_inc(pT_hi_ready, 1)
                act.wait_ge(moe_ready, t + 1)
                st = f_stat[0:R, 8 * t:8 * t + 8]
                if t >= 1:
                    act.wait_ge(fT_banked, t)
                mine(nc.scalar.activation(f_norm[0:R, :], h_in[i][0:R, :], ACT.Square, accum_out=st[:, 0:1]))
                mine.settle()
                mine(nc.scalar.activation(st[:, 0:1], st[:, 0:1], ACT.Sqrt, scale=1.0 / D, bias=EPS), f_ss)

            early(0)
            for w in range(2):
                act.wait_ge(raw_landed[w], 16 * (nb + 3))
                nc.scalar.activation(wg_hi[:, :, w * CB:(w + 1) * CB], raw[w][:], ACT.Copy).then_inc(wg_hi_ready, 1)
            act.wait_ge(raw_landed[2], 16 * (nb + 2))
            nc.scalar.activation(wp_hi[:], raw_pp, ACT.Copy).then_inc(wg_hi_ready, 1)
            for t in range(TILES):
                R, i = ROWS[t], t % 2
                act.wait_ge(fT_banked, t + 1)
                for j in range(2):
                    last = nc.scalar.activation(fT_hi[:, 4 * j:4 * j + 4, 0:R],
                                                bank[:, 2 + j, 0:4 * R].rearrange("p (c r) -> p c r", c=4), ACT.Copy)
                last.then_inc(fT_hi_ready, 1)
                act.wait_ge(ple_done, t + 1)
                if t >= 1:
                    act.wait_ge(out_ready, t)
                mine(nc.scalar.activation(sg[0:R, :], bank[0:R, 4:6, :].rearrange("p b n -> p (b n)"), ACT.Sigmoid), sg_ready)
                act.wait_ge(out_ready, t + 1)
                st = f_stat[0:R, 8 * t:8 * t + 8]
                mine(nc.scalar.activation(sg[0:R, :], h_in[i][0:R, :], ACT.Square, accum_out=st[:, 2:3]))
                mine.settle()
                mine(nc.scalar.activation(st[:, 2:3], st[:, 2:3], ACT.Sqrt, scale=1.0 / D, bias=EPS), out_ss)
                if t + 1 < TILES:
                    early(t + 1)

        @block.vector
        def _(dve):
            mine = Signals(dve, f_dve)
            nb = blocks(dve)

            def early(t):
                R, i = ROWS[t], t % 2
                h, st = h_in[i][0:R, :], f_stat[0:R, 8 * t:8 * t + 8]
                dve.wait_ge(pT_hi_ready, t + 1)
                mine(nc.vector.tensor_tensor(pT_lo[:, :, 0:R], bank[:, 2, 0:PC * R].rearrange("p (c r) -> p c r", c=PC),
                                             pT_hi[:, :, 0:R].bitcast(F32), ALU.subtract), pT_lo_ready)
                dve.wait_ge(h_in_landed[i], 16 * (t // 2 + 1))
                dve.wait_ge(bdn_done, t + 1)
                mine(nc.vector.tensor_tensor(h, h, bank[0:R, 0:2, :].rearrange("p b n -> p (b n)"), ALU.add))
                dve.wait_ge(y_in_landed[i], 16 * (t // 2 + 1))
                for k in range(TOPK):
                    mine.settle()
                    mine(nc.vector.scalar_tensor_tensor(h, y_in[i][0:R, k, :], gates[0:R, t, k:k + 1], h, ALU.mult, ALU.add),
                         moe_ready if k == TOPK - 1 else None)
                dve.wait_ge(f_ss, t + 1)
                mine(nc.vector.reciprocal(st[:, 1:2], st[:, 0:1]))
                mine.settle()
                mine(nc.vector.scalar_tensor_tensor(f_norm[0:R, :], h, st[:, 1:2], gain_p[0:R, :], ALU.mult, ALU.mult), f_normed)

            dve.wait_ge(f_consts, 48)
            early(0)
            for w in range(2):
                dve.wait_ge(wg_hi_ready, w + 1)
                mine(nc.vector.tensor_tensor(wg_lo[:, :, w * CB:(w + 1) * CB], raw[w][:],
                                             wg_hi[:, :, w * CB:(w + 1) * CB].bitcast(F32), ALU.subtract), wg_lo_ready)
            dve.wait_ge(wg_hi_ready, 3)
            mine(nc.vector.tensor_tensor(wp_lo[:], raw_pp, wp_hi[:].bitcast(F32), ALU.subtract), wg_lo_ready)
            for t in range(TILES):
                R, i = ROWS[t], t % 2
                h, st = h_in[i][0:R, :], f_stat[0:R, 8 * t:8 * t + 8]
                dve.wait_ge(fT_hi_ready, t + 1)
                for j in range(2):
                    last = nc.vector.tensor_tensor(fT_lo[:, 4 * j:4 * j + 4, 0:R],
                                                   bank[:, 2 + j, 0:4 * R].rearrange("p (c r) -> p c r", c=4),
                                                   fT_hi[:, 4 * j:4 * j + 4, 0:R].bitcast(F32), ALU.subtract)
                mine(last, fT_lo_ready)
                dve.wait_ge(sg_ready, t + 1)
                mine(nc.vector.tensor_tensor(sg[0:R, :], sg[0:R, :], bank[0:R, 6:8, :].rearrange("p b n -> p (b n)"), ALU.mult))
                mine.settle()
                mine(nc.vector.tensor_tensor(h, h, sg[0:R, :], ALU.add), out_ready)
                dve.wait_ge(out_ss, t + 1)
                mine(nc.vector.reciprocal(st[:, 3:4], st[:, 2:3]))
                mine.settle()
                mine(nc.vector.scalar_tensor_tensor(h, h, st[:, 3:4], gain_f[0:R, :], ALU.mult, ALU.mult), y_final)
                if t + 1 < TILES:
                    early(t + 1)

        @block.tensor
        def _(pe):
            def early(t):
                R, i = ROWS[t], t % 2
                if t >= 1:
                    pe.wait_ge(fT_lo_ready, t)
                nc.tensor.transpose(bank[0:E, 3, 0:R], gate_table[0:R, t, :], ident[0:R, 0:R]).then_inc(gT_banked, 1)
                pe.wait_ge(ple_landed[i], 16 * (t // 2 + 1))
                for c in range(PC):
                    last = nc.tensor.transpose(bank[:, 2, c * R:(c + 1) * R], ple_in[i][0:R, c * P:(c + 1) * P],
                                               ident[0:R, 0:R])
                last.then_inc(pT_in_banked, 1)
                pe.wait_ge(gT_ready, t + 1)
                pe.wait_ge(f_consts, 48)
                if t >= 1:
                    pe.wait_ge(moe_ready, t)
                for j in range(2):
                    last = nc.tensor.matmul(bank[0:R, j, :], gT[:, 0:R], b_down[:, j * CB:(j + 1) * CB], start=True, stop=True)
                last.then_inc(bdn_done, 1)

            early(0)
            for t in range(TILES):
                R, i = ROWS[t], t % 2
                pe.wait_ge(f_normed, t + 1)
                pe.wait_ge(pT_lo_ready, t + 1)
                for c in range(KC):
                    last = nc.tensor.transpose(bank[:, 2 + c // 4, (c % 4) * R:(c % 4 + 1) * R],
                                               f_norm[0:R, c * P:(c + 1) * P], ident[0:R, 0:R])
                last.then_inc(fT_banked, 1)
                pe.wait_ge(wg_lo_ready, 3)
                if t >= 1:
                    pe.wait_ge(out_ready, t)
                for w in range(2):
                    product(nc, bank[:, 6 + w, :], lambda c: pT_hi[:, c, :], lambda c: pT_lo[:, c, :],
                            wp_hi[:, :, w * CB:(w + 1) * CB], wp_lo[:, :, w * CB:(w + 1) * CB],
                            [(k, k) for k in range(PC)], CB, True, True)
                pe.wait_ge(fT_lo_ready, t + 1)
                for w in range(2):
                    last = product(nc, bank[:, 4 + w, :], lambda c: fT_hi[:, c, :], lambda c: fT_lo[:, c, :],
                                   wg_hi[:, :, w * CB:(w + 1) * CB], wg_lo[:, :, w * CB:(w + 1) * CB],
                                   [(k, k) for k in range(KC)], CB, True, True)
                last.then_inc(ple_done, 1)
                if t + 1 < TILES:
                    early(t + 1)
    ctx.close()




_INS = ['x_prompt', 'x_sample', 'cache_swa_k', 'cache_swa_v', 'p_prompt', 'p_sample', 'g_mix', 'w_in', 'ln_v_g',
        'ln_v_b', 'w_sp', 'b_sp', 'sinks', 'g_out_a', 'g_out_b', 'w_o', 'g_moe', 'w_router', 'b_router', 'w_gu',
        'b_gu', 'w_dn', 'b_dn', 'g_ple', 'w_ple_gate', 'w_ple_proj', 'g_final']


def kernel(**inputs):
    import numpy as _np
    import concourse.bacc as _bacc
    from concourse import mybir as _mybir
    from concourse.bass_utils import run_bass_kernel_spmd as _run

    nc = _bacc.Bacc("TRN2", target_bir_lowering=False, num_devices=1)
    arrays, args = {}, []
    for name in _INS:
        a = _np.ascontiguousarray(inputs[name])
        arrays[f"in_{name}"] = a
        args.append(nc.dram_tensor(f"in_{name}", a.shape, _mybir.dt.from_np(a.dtype), kind="ExternalInput").ap())
    L, B, S, D = inputs['p_prompt'].shape[0], *inputs['x_prompt'].shape
    _, DB, W, KV, HD = inputs['cache_swa_k'].shape
    DS = inputs['x_sample'].shape[1]
    A = inputs['ln_v_g'].shape[1]
    shapes = [(B, S, D), (DB, DS, D), (L, B, W, KV, HD), (L, B, W, KV, HD), (L, DB, W, KV, HD), (L, DB, W, KV, HD),
              (L, DB, DS, A)]
    for i, shape in enumerate(shapes):
        args.append(nc.dram_tensor(f"out_{i}", shape, _mybir.dt.float32, kind="ExternalOutput").ap())
    hybrid_layer(nc, *args)
    r = _run(nc, [arrays], core_ids=[0])
    return tuple(r.results[0][f"out_{i}"] for i in range(len(shapes)))
```

```python
from contextlib import ExitStack

import concourse.bass as bass
from concourse import mybir

F32 = mybir.dt.float32
F32R = mybir.dt.float32r
I32 = mybir.dt.int32
U32 = mybir.dt.uint32
ALU = mybir.AluOpType
ACT = mybir.ActivationFunctionType
AX = mybir.AxisListType.X

P = 128
EPS = 1e-5
NEG = -3.4028235e38
ALPHA = 1.702
LIMIT = 7.0


class Signals:

    def __init__(self, engine, step):
        self.engine, self.step = engine, step
        self.count, self.grows, self.turn, self.last = {}, {}, 0, None

    def __call__(self, instruction, sem=None):
        sem = self.step if sem is None else sem
        instruction.then_inc(sem, 1)
        self.count[sem] = self.count.get(sem, 0) + 1
        self.last = sem
        return instruction

    def on(self, engine):
        self.engine = engine
        return self

    def settle(self):
        sem = self.last
        self.engine.wait_ge(sem, self.turn * self.grows.get(sem, 0) + self.count[sem])

    def enter_loop(self, turn, grows):
        self.turn, self.grows, self.entry = turn, grows, dict(self.count)

    def leave_loop(self, turns):
        for sem, n in self.count.items():
            assert n - self.entry.get(sem, 0) == self.grows.get(sem, 0), (sem, n - self.entry.get(sem, 0))
        self.count = dict(self.entry)
        self.turn = turns


def product(nc, out, x_hi, x_lo, w_hi, w_lo, chunks, cols, start, stop):
    for i, (cx, cw) in enumerate(chunks):
        for j, (a, b) in enumerate(((x_hi, w_hi), (x_hi, w_lo), (x_lo, w_hi))):
            last = nc.tensor.matmul(out, a(cx), b[:, cw, 0:cols], start=start and i == 0 and j == 0,
                                    stop=stop and i == len(chunks) - 1 and j == 2)
    return last


def hybrid_layer(nc, x_prompt, x_sample, cache_k, cache_v, p_prompt, p_sample, g_mix, w_in, ln_v_g,
                 ln_v_b, w_sp, b_sp, sinks, g_out_a, g_out_b, w_o, g_moe, w_router, b_router, w_gu,
                 b_gu, w_dn, b_dn, g_ple, w_ple_gate, w_ple_proj, g_final,
                 y_prompt, y_sample, prompt_k, prompt_v, sample_k, sample_v, sample_chunk_v):
    SEQ, D = x_prompt.shape[1:]
    NS = x_sample.shape[0]
    NT = SEQ // P
    TILES = NT + 1
    ROWS = [P] * NT + [NS]
    TOK = SEQ + NS
    KC = D // P
    HALFK = KC // 2
    G, CH = w_sp.shape[1:3]
    HD = cache_k.shape[-1]
    KV = cache_k.shape[3]
    AW = G * HD
    H = sinks.shape[1]
    HG = H // KV
    BW = H * HD
    KVW = KV * HD
    E = w_router.shape[2]
    TOPK = 4
    PLE = w_ple_proj.shape[1]
    PC = PLE // P
    CB = 512
    OVER = TOPK * TOK // (P + 1)
    NBMAX = E + OVER
    TABLE = (NBMAX + 2) * P
    NOWHERE = 1 << 20
    assert CH == P and AW == CB and BW == CB and D == 2 * CB and KC == 8 and TOK * TOPK < NOWHERE
    SLOPES = [2.0 ** (-8.0 * (h + 1) / H) for h in range(H)]
    LEAD = 3

    TILE_B = KC * CB * 4
    HALF_B = TILE_B // 2
    RAW = -(-nc.sbuf_base // 64) * 64
    SPLIT = RAW + 6 * TILE_B
    MAIN = SPLIT + 2 * LEAD * HALF_B
    SIDE = RAW + 4 * TILE_B
    XT_B = KC * TOK * 4

    def at(name, shape, dt, offset):
        return nc.alloc_sbuf_tensor_at(name, shape, dt, offset=offset)

    raw = [at(f"raw_{s}", [P, KC, CB], F32, RAW + s * TILE_B) for s in range(6)]
    half_hi = [at(f"half_hi_{s}", [P, HALFK, CB], F32R, SPLIT + 2 * s * HALF_B) for s in range(LEAD)]
    half_lo = [at(f"half_lo_{s}", [P, HALFK, CB], F32R, SPLIT + (2 * s + 1) * HALF_B) for s in range(LEAD)]

    uq = at("uq", [P, TILES, 2 * CB], F32, MAIN + 2 * XT_B)
    va = at("va", [P, TILES, CB], F32, MAIN + 2 * XT_B + TILES * 2 * CB * 4)
    keep = MAIN + 2 * XT_B + TILES * 3 * CB * 4
    ident = at("ident", [P, P], F32, keep)
    gates = at("gates", [P, TILES, TOPK], F32, keep + 512)
    gate_table = at("gate_table", [P, TILES, E], F32, keep + 640)
    END = keep + 640 + TILES * E * 4
    assert END <= nc.sbuf_usable_end, (END, nc.sbuf_usable_end)

    ctx = ExitStack()

    def sem(name):
        return ctx.enter_context(nc.semaphore(name))

    def dram(name, shape, dt):
        return nc.dram_tensor(name, shape, dt, kind="Internal").ap()

    hn_rows = dram("hn_rows", [TOK, D], F32)
    h_rows = dram("h_rows", [TOK, D], F32)
    expert_rows = dram("expert_rows", [TOPK * TOK, D], F32)
    slot_table = dram("slot_table", [TABLE, 2], I32)
    bias_rows = dram("bias_rows", [E, 2, 2, D], F32)
    bank = ctx.enter_context(nc.psum_tensor("bank", [P, 8, 512], F32))

    def tokens(ap_prompt, ap_sample, t):
        return ap_prompt[t * P:(t + 1) * P] if t < NT else ap_sample

    def column(t):
        return NS + t * P if t < NT else 0

    def stationary(xT, t):
        return lambda c: xT[:, c, column(t):column(t) + P]

    x_p, x_s = x_prompt[0], x_sample[:, 0, :]
    w_in_v = w_in[0].rearrange("(c p) n -> p c n", p=P)
    w_o_v = w_o[0].rearrange("(c p) n -> p c n", p=P)
    w_gu_v = w_gu[0].rearrange("e (c p) n -> e p c n", p=P)
    w_dn_v = w_dn[0].rearrange("e (c p) n -> e p c n", p=P)
    w_pg_v = w_ple_gate[0].rearrange("(c p) n -> p c n", p=P)
    w_pp_v = w_ple_proj[0].rearrange("(c p) n -> p c n", p=P)
    IN_COLS = [CB, CB, CB, 2 * KVW]

    raw_landed = [sem(f"raw_landed_{s}") for s in range(6)]

    x_squares = at("x_squares", [P, D], F32, SIDE)
    wsp = at("wsp", [P, G, P], F32, SIDE + 8192)
    wspT = at("wspT", [P, G, P], F32, SIDE + 12288)
    gain = at("gain", [P, D], F32, SIDE + 16384)
    lng = at("lng", [P, CB], F32, SIDE + 20480)
    lnb = at("lnb", [P, CB], F32, SIDE + 22528)
    k_nat = at("k_nat", [P, TILES, KVW], F32, SIDE + 24576)
    v_nat = at("v_nat", [P, TILES, KVW], F32, SIDE + 24576 + TILES * KVW * 4)
    small = SIDE + 24576 + 2 * TILES * KVW * 4
    stat = at("stat", [P, 8 * TILES], F32, small)
    bnst = at("bnst", [P, TILES, 6], F32, small + 256)
    bspT = at("bspT", [P, G], F32, small + 512)
    w00 = at("w00", [NS, G], F32, small + 576)
    b00 = at("b00", [NS, G], F32, small + 640)
    sink_b = at("sink_b", [P, H], F32, small + 704)
    sink64 = at("sink64", [NS * H, 1], F32, small + 768)
    nowhere = at("nowhere", [P, 2 * TABLE // P], I32, small + 832)
    behind = small + 832 + 2 * TABLE // P * 4
    behind += -behind % 32
    dist_i = at("dist_i", [P, 2 * P], I32, SIDE + 12288)
    dist_f = at("dist_f", [P, 2 * P], F32, SIDE + 13312)
    alibi = at("alibi", [P, H, 2 * P], F32, SIDE)
    xT_hi = at("xT_hi", [P, KC, TOK], F32R, MAIN)
    xT_lo = at("xT_lo", [P, KC, TOK], F32R, MAIN + XT_B)
    NQ = 4
    bias_f = at("bias_f", [E * NQ, 2 * D // NQ], F32, MAIN + 2 * XT_B + TILES * 2 * CB * 4)
    bias_h = at("bias_h", [E * NQ, 2 * D // NQ], F32R, MAIN + 2 * XT_B + TILES * 2 * CB * 4 + 2048)
    bias_l = at("bias_l", [E * NQ, 2 * D // NQ], F32R, MAIN + 2 * XT_B + TILES * 2 * CB * 4 + 4096)

    def ss(t):
        return stat[0:ROWS[t], 8 * t:8 * t + 1]

    def rstd(t):
        return stat[0:ROWS[t], 8 * t + 1:8 * t + 2]

    x_landed = [sem(f"x_landed_{t}") for t in range(TILES)]
    gain_landed, consts_landed, bias_landed0, bias_stored = sem("gain_landed"), sem("consts_landed"), sem("bias_landed0"), sem("bias_stored")
    bias_low = sem("bias_low")
    p_out, ident_ready = sem("p_out"), sem("ident_ready")
    x_ss, x_normed, xT_banked = sem("x_ss"), sem("x_normed"), sem("xT_banked")
    xT_hi_ready, xT_lo_ready = sem("xT_hi_ready"), sem("xT_lo_ready")
    p_hi, p_lo, z_first = sem("p_hi"), sem("p_lo"), sem("z_first")
    z_done, z_read, v_var, v_std, va_ready, bias_cut = sem("z_done"), sem("z_read"), sem("v_var"), sem("v_std"), sem("va_ready"), sem("bias_cut")
    wsp_cut, table_ready = sem("wsp_cut"), sem("table_ready")
    pool_steps, act_steps, dve_steps = (Signals(None, sem(n)) for n in ("pool_step", "act_step", "dve_step"))

    def raw_half(s, h, cols=CB):
        return raw[s][:, h * HALFK:(h + 1) * HALFK, 0:cols]

    def split_columns(w):
        return IN_COLS[w] if w < len(IN_COLS) else CB

    def write_hi(act, n, s, h, cols, hi_sem, wait_used, landed_value):
        act.wait_ge(raw_landed[s], landed_value)
        if n >= LEAD:
            wait_used(act, n - LEAD)
        nc.scalar.activation(half_hi[n % LEAD][:, :, 0:cols], raw_half(s, h, cols), ACT.Copy).then_inc(hi_sem, 1)

    def write_lo(dve, n, s, h, cols, hi_sem, lo_sem, wait_used, landed_value):
        dve.wait_ge(raw_landed[s], landed_value)
        dve.wait_ge(hi_sem, n + 1)
        if n >= LEAD:
            wait_used(dve, n - LEAD)
        nc.vector.tensor_tensor(half_lo[n % LEAD][:, :, 0:cols], raw_half(s, h, cols),
                                half_hi[n % LEAD][:, :, 0:cols].bitcast(F32), ALU.subtract).then_inc(lo_sem, 1)

    def used_after(first, done):
        def wait_used(engine, n):
            if n % 2 == 0:
                engine.wait_ge(first, n // 2 + 1)
            else:
                engine.wait_ge(done, TILES * (n // 2 + 1))
        return wait_used

    NZ = 2 * len(IN_COLS)

    z_used = used_after(z_first, z_done)

    def zbank(w, t):
        return (TILES * w + t + 2) % 8

    def turned_before(t):
        return max(t, 1)

    with nc.Block() as block:
        @block.sync
        def _(sp):
            for t in range(TILES):
                sp.dma_start(uq[0:ROWS[t], t, :], tokens(x_p, x_s, t)).then_inc(x_landed[t], 16)
            col = 0
            for w, cols in enumerate(IN_COLS):
                sp.dma_start(raw[w][:, :, 0:cols], w_in_v[:, :, col:col + cols]).then_inc(raw_landed[w], 16)
                col += cols
            sp.wait_ge(bias_cut, 1)
            sp.wait_ge(bias_low, 1)
            for part, rows in enumerate((bias_h, bias_l)):
                sp.dma_start(bias_rows[:, :, part, :].rearrange("e s (f n) -> (e s) f n", n=CB), rows[:].bitcast(F32)).then_inc(bias_stored, 16)
            for w in range(2):
                sp.wait_ge(p_hi, 2 * w + 2)
                sp.wait_ge(p_lo, 2 * w + 2)
                sp.dma_start(raw[w][:], w_o_v[:, :, w * CB:(w + 1) * CB]).then_inc(raw_landed[w], 16)
            for w in range(2, 4):
                sp.wait_ge(p_hi, 2 * w + 2)
                sp.wait_ge(p_lo, 2 * w + 2)
                c0 = (w - 2) * D + CB
                sp.dma_start(raw[w][:], w_gu_v[0, :, :, c0:c0 + CB]).then_inc(raw_landed[w], 16)

        @block.gpsimd
        def _(pool):
            mine = pool_steps.on(pool)
            pool.dma_start(gain[:], g_mix[0:1, :].to_broadcast([P, D])).then_inc(gain_landed, 16)
            mine(nc.gpsimd.memset(ident[:], 0.0))
            mine.settle()
            nc.gpsimd.affine_select(out=ident[:], in_=ident[:], compare_op=ALU.not_equal, fill=1.0, base=0,
                                    pattern=[[-1, P]], channel_multiplier=1).then_inc(ident_ready, 1)
            mine(nc.gpsimd.memset(nowhere[:], NOWHERE))
            mine.settle()
            pool.dma_start(slot_table.rearrange("(p n) o -> p (n o)", p=P), nowhere[:]).then_inc(table_ready, 16)
            pool.dma_start(wsp[:], w_sp[0].rearrange("g t s -> t g s")).then_inc(consts_landed, 16)
            with nc.allow_non_contiguous_dma(reason="a few hundred single elements"):
                pool.dma_start(bspT[:], b_sp[0].rearrange("g t -> t g")).then_inc(consts_landed, 16)
                pool.dma_start(w00[:], w_sp[0, :, 0, 0:1].rearrange("g o -> o g").to_broadcast([NS, G])).then_inc(consts_landed, 16)
                pool.dma_start(b00[:], b_sp[0, :, 0:1].rearrange("g o -> o g").to_broadcast([NS, G])).then_inc(consts_landed, 16)
                for b in range(NS):
                    pool.dma_start(sink64[b * H:(b + 1) * H, :], sinks.rearrange("o h -> h o")).then_inc(consts_landed, 16)
            pool.dma_start(lng[:], ln_v_g[0:1, :].to_broadcast([P, CB])).then_inc(consts_landed, 16)
            pool.dma_start(lnb[:], ln_v_b[0:1, :].to_broadcast([P, CB])).then_inc(consts_landed, 16)
            pool.dma_start(sink_b[:], sinks[0:1, :].to_broadcast([P, H])).then_inc(consts_landed, 16)
            pool.wait_ge(consts_landed, 16 * (7 + NS))
            nc.gpsimd.affine_select(out=wsp[:], in_=wsp[:], compare_op=ALU.is_ge, fill=0.0, base=0,
                                    pattern=[[0, G], [-1, P]], channel_multiplier=1).then_inc(wsp_cut, 1)
            pool.wait_ge(table_ready, 16)
            mine(nc.gpsimd.iota(dist_i[:], pattern=[[-1, 2 * P]], base=P, channel_multiplier=1))
            mine.settle()
            mine(nc.gpsimd.tensor_copy(dist_f[:], dist_i[:]))
            mine.settle()
            pool.wait_ge(x_ss, TILES)
            for h in range(H):
                mine(nc.gpsimd.tensor_scalar(alibi[:, h, :], dist_f[:], -SLOPES[h], None, ALU.mult))
            mine.settle()
            mine(nc.gpsimd.affine_select(out=alibi[:], in_=alibi[:], compare_op=ALU.is_ge, fill=NEG, base=P,
                                         pattern=[[0, H], [-1, 2 * P]], channel_multiplier=1))
            mine.settle()
            mine(nc.gpsimd.affine_select(out=alibi[:], in_=alibi[:], compare_op=ALU.is_ge, fill=NEG, base=-1,
                                         pattern=[[0, H], [1, 2 * P]], channel_multiplier=-1))
            pool.wait_ge(va_ready, 1)
            pool.dma_start(sample_chunk_v[0, :, 0, :], va[0:NS, NT, :]).then_inc(p_out, 16)
            pool.wait_ge(z_read, 4 * TILES)
            pool.dma_start(prompt_k[0, 0].rearrange("s k d -> s (k d)"), k_nat[:, NT - 1, :]).then_inc(p_out, 16)
            pool.dma_start(prompt_v[0, 0].rearrange("s k d -> s (k d)"), v_nat[:, NT - 1, :]).then_inc(p_out, 16)
            pool.wait_ge(p_out, 48)

        @block.scalar
        def _(act):
            mine = act_steps.on(act)
            for t in range(TILES):
                R = ROWS[t]
                act.wait_ge(x_landed[t], 16)
                if t == 1:
                    act.dma_start(bias_f[:], b_gu[0].rearrange("e (q n) -> (e q) n", q=NQ)).then_inc(bias_landed0, 16)
                mine(nc.scalar.activation(x_squares[0:R, :], uq[0:R, t, :], ACT.Square, accum_out=ss(t)))
                mine.settle()
                nc.scalar.activation(ss(t), ss(t), ACT.Sqrt, scale=1.0 / D, bias=EPS).then_inc(x_ss, 1)
            def hi(n):
                w = n // 2
                write_hi(act, n, w, n % 2, split_columns(w), p_hi, z_used, 16)

            for t in range(TILES):
                R, c0 = ROWS[t], column(t)
                act.wait_ge(xT_banked, t + 1)
                b = 2 * (t % 4)
                for j in range(2):
                    last = nc.scalar.activation(xT_hi[:, 4 * j:4 * j + 4, c0:c0 + R],
                                                bank[:, b + j, 0:4 * R].rearrange("p (c r) -> p c r", c=4), ACT.Copy)
                last.then_inc(xT_hi_ready, 1)
                if t == 2:
                    hi(0)
            for n in range(1, LEAD):
                hi(n)
            act.wait_ge(bias_landed0, 16)
            nc.scalar.activation(bias_h[:], bias_f[:], ACT.Copy).then_inc(bias_cut, 1)
            for w in range(len(IN_COLS)):
                if 2 * w + LEAD < NZ:
                    hi(2 * w + LEAD)
                for t in range(TILES):
                    R, src = ROWS[t], bank[0:ROWS[t], zbank(w, t), :]
                    act.wait_ge(z_done, TILES * w + t + 1)
                    if w == 1 and t == 0:
                        act.wait_ge(bias_stored, 32)
                    if w == 0:
                        ins = nc.scalar.activation(uq[0:R, t, 0:CB], src, ACT.Gelu_apprx_tanh)
                    elif w == 1:
                        ins = nc.scalar.activation(va[0:R, t, :], src, ACT.Gelu_apprx_tanh)
                    elif w == 2:
                        ins = nc.scalar.activation(uq[0:R, t, CB:2 * CB].rearrange("p (i g d) -> p g i d", g=KV, i=HG),
                                                   src.rearrange("p (g i d) -> p g i d", g=KV, i=HG), ACT.Copy)
                    else:
                        nc.scalar.activation(k_nat[0:R, t, :], src[:, 0:KVW], ACT.Copy)
                        ins = nc.scalar.activation(v_nat[0:R, t, :], src[:, KVW:2 * KVW], ACT.Copy)
                    ins.then_inc(z_read, 1)
                if 2 * w + LEAD + 1 < NZ:
                    hi(2 * w + LEAD + 1)
                if w == 2:
                    for t in range(TILES):
                        act.wait_ge(v_var, t + 1)
                        nc.scalar.activation(stat[0:ROWS[t], 8 * t + 4:8 * t + 5], stat[0:ROWS[t], 8 * t + 3:8 * t + 4],
                                             ACT.Sqrt, bias=EPS).then_inc(v_std, 1)

        @block.vector
        def _(dve):
            mine = dve_steps.on(dve)
            dve.wait_ge(gain_landed, 16)
            for t in range(TILES):
                R = ROWS[t]
                dve.wait_ge(x_ss, t + 1)
                mine(nc.vector.reciprocal(rstd(t), ss(t)))
                mine.settle()
                mine(nc.vector.scalar_tensor_tensor(uq[0:R, t, :], uq[0:R, t, :], rstd(t), gain[0:R, :],
                                               ALU.mult, ALU.mult), x_normed)
            def lo(n):
                w = n // 2
                write_lo(dve, n, w, n % 2, split_columns(w), p_hi, p_lo, z_used, 16)

            for t in range(TILES):
                R, c0 = ROWS[t], column(t)
                dve.wait_ge(xT_banked, t + 1)
                dve.wait_ge(xT_hi_ready, t + 1)
                b = 2 * (t % 4)
                for j in range(2):
                    last = nc.vector.tensor_tensor(xT_lo[:, 4 * j:4 * j + 4, c0:c0 + R],
                                                   bank[:, b + j, 0:4 * R].rearrange("p (c r) -> p c r", c=4),
                                                   xT_hi[:, 4 * j:4 * j + 4, c0:c0 + R].bitcast(F32), ALU.subtract)
                last.then_inc(xT_lo_ready, 1)
                if t == 2:
                    lo(0)
            for n in range(1, NZ):
                lo(n)
                if n == LEAD - 1:
                    dve.wait_ge(bias_cut, 1)
                    mine(nc.vector.tensor_tensor(bias_l[:], bias_f[:], bias_h[:].bitcast(F32), ALU.subtract), bias_low)
            for t in range(TILES):
                R = ROWS[t]
                dve.wait_ge(z_read, TILES + t + 1)
                mine(nc.vector.bn_stats(bnst[0:R, t, :], va[0:R, t, :]))
                mine.settle()
                nc.vector.bn_aggr(stat[0:R, 8 * t + 2:8 * t + 4], bnst[0:R, t, :]).then_inc(v_var, 1)
            dve.wait_ge(consts_landed, 16 * (7 + NS))
            for t in reversed(range(TILES)):
                R, v = ROWS[t], va[0:ROWS[t], t, :]
                dve.wait_ge(v_std, TILES)
                mine(nc.vector.reciprocal(stat[0:R, 8 * t + 5:8 * t + 6], stat[0:R, 8 * t + 4:8 * t + 5]))
                mine.settle()
                mine(nc.vector.tensor_scalar(v, v, stat[0:R, 8 * t + 2:8 * t + 3], stat[0:R, 8 * t + 5:8 * t + 6],
                                             ALU.subtract, ALU.mult))
                mine.settle()
                mine(nc.vector.tensor_tensor(v, v, lng[0:R, :], ALU.mult))
                mine.settle()
                mine(nc.vector.tensor_tensor(v, v, lnb[0:R, :], ALU.add), va_ready)

        @block.tensor
        def _(pe):
            pe.wait_ge(ident_ready, 1)
            for t in range(TILES):
                R = ROWS[t]
                pe.wait_ge(x_normed, t + 1)
                if t == 4:
                    pe.wait_ge(xT_hi_ready, 1)
                    pe.wait_ge(xT_lo_ready, 1)
                for c in range(KC):
                    last = nc.tensor.transpose(bank[:, 2 * (t % 4) + c // 4, (c % 4) * R:(c % 4 + 1) * R],
                                               uq[0:R, t, c * P:(c + 1) * P], ident[0:R, 0:R])
                last.then_inc(xT_banked, 1)
            for n in range(NZ):
                w, h = n // 2, n % 2
                pe.wait_ge(p_hi, n + 1)
                pe.wait_ge(p_lo, n + 1)
                for t in range(TILES):
                    if n == 0:
                        pe.wait_ge(xT_hi_ready, turned_before(t) + 1)
                        pe.wait_ge(xT_lo_ready, turned_before(t) + 1)
                    if h == 0 and TILES * w + t >= 8:
                        pe.wait_ge(z_read, TILES * w + t - 7)
                    last = product(nc, bank[:, zbank(w, t), 0:IN_COLS[w]], stationary(xT_hi, t), stationary(xT_lo, t),
                                   half_hi[n % LEAD], half_lo[n % LEAD],
                                   [(h * HALFK + k, k) for k in range(HALFK)], IN_COLS[w], h == 0, h == 1)
                    if h == 1:
                        last.then_inc(z_done, 1)
                if h == 0:
                    last.then_inc(z_first, 1)

    o = MAIN
    def scratch(name, shape, dt=F32):
        nonlocal o
        size = 4
        for n in shape[1:]:
            size *= n
        t = at(name, shape, dt, o)
        o += -(-size // 32) * 32
        return t

    kT = scratch("kT", [P, SEQ])
    qT = scratch("qT", [P, NT, HG, P])
    probs = [scratch(f"probs_{i}", [P, HG, 2 * P]) for i in range(2)]
    pT = scratch("pT", [P, HG * 2, P])
    m_ = [scratch(f"stats_{i}", [P, 8, HG]) for i in range(3)]
    bias_s = scratch("bias_s", [P, H])
    dist_s = scratch("dist_s", [P, 2])
    slope_s = scratch("slope_s", [P, H])
    ksT = scratch("ksT", [P, NS, P])
    qsT = scratch("qsT", [P, HG, NS])
    s_pre = scratch("s_pre", [P, NS * H])
    s_exp = scratch("s_exp", [NS * H, P])
    s_st = scratch("s_st", [NS * H, 8])
    s_pT = scratch("s_pT", [P, NS * H])
    ysT = scratch("ysT", [P, HG, NS])
    k_win = scratch("k_win", [P, NS, KVW])
    assert o <= MAIN + 2 * XT_B, o - MAIN - 2 * XT_B
    v_win = at("v_win", [P, NS, KVW], F32, SIDE + 8192)
    UNITS = [(n, g) for n in range(NT) for g in range(KV)]

    iota_ready = sem("iota_ready")
    win_landed, a_out = sem("win_landed"), sem("a_out")
    wspT_banked, wspT_ready, gate_done, gate_read = sem("wspT_banked"), sem("wspT_ready"), sem("gate_done"), sem("gate_read")
    kT_banked, kT_ready, qT_banked, qT_ready, ksT_banked, ksT_ready = (sem("kT_banked"), sem("kT_ready"),
        sem("qT_banked"), sem("qT_ready"), sem("ksT_banked"), sem("ksT_ready"))
    score_done, score_read, max_ready, exp_ready = sem("score_done"), sem("score_read"), sem("max_ready"), sem("exp_ready")
    pT_banked, pT_ready, pv_done, pv_read = sem("pT_banked"), sem("pT_ready"), sem("pv_done"), sem("pv_read")
    ss_done, ss_cut, ssT_done, ss_exp, ss_prob, spT_done, spT_ready, sy_done, sy_cut, syT_done, sy_ready = (
        sem(n) for n in ("s_score_done", "s_score_cut", "s_score_turned", "s_exp_ready", "s_prob_ready", "s_probT_done",
                         "s_probT_ready", "s_pv_done", "s_pv_cut", "s_pv_turned", "s_y_ready"))

    o_hi, o_lo, o_first, mix_done, y_ss, y_normed, gain_o_landed = (sem(n) for n in (
        "o_hi", "o_lo", "o_first", "mix_done", "y_ss", "y_normed", "gain_o_landed"))
    o_used = used_after(o_first, mix_done)
    gain_o = gain

    def y_squares(mine, t, squares):
        R, st = ROWS[t], stat[0:ROWS[t], 8 * t:8 * t + 8]
        for j in range(2):
            if t + j > 0:
                mine.settle()
            mine(nc.scalar.activation(squares[0:R, :], uq[0:R, t, j * CB:(j + 1) * CB], ACT.Square,
                                      accum_out=st[:, j:j + 1]))

    def y_root(t):
        st = stat[0:ROWS[t], 8 * t:8 * t + 8]
        nc.scalar.activation(st[:, 0:2], st[:, 0:2], ACT.Sqrt, scale=1.0 / CB, bias=EPS).then_inc(y_ss, 1)

    def y_norm(dve, mine, t):
        R, st = ROWS[t], stat[0:ROWS[t], 8 * t:8 * t + 8]
        dve.wait_ge(y_ss, t + 1)
        mine(nc.vector.reciprocal(st[:, 2:4], st[:, 0:2]))
        mine.settle()
        for j in range(2):
            part = uq[0:R, t, j * CB:(j + 1) * CB]
            ins = nc.vector.scalar_tensor_tensor(part, part, st[:, 2 + j:3 + j], gain_o[0:R, j * CB:(j + 1) * CB],
                                                 ALU.mult, ALU.mult)
            mine(ins, y_normed if j == 1 else None)

    def turned(act, u):
        n, g = UNITS[u]
        act.wait_ge(pT_banked, u + 1)
        if n == 0:
            nc.scalar.activation(pT[:, 0:HG, :], bank[:, 4, :], ACT.Copy).then_inc(pT_ready, 1)
        else:
            nc.scalar.activation(pT[:], bank[:, 4:6, :], ACT.Copy).then_inc(pT_ready, 1)

    def s_bank(u):
        b = 2 * (u % 2)
        return bank[:, b:b + 2, :].rearrange("p b (i s) -> p (b i) s", s=2 * P)

    def o_bank(u):
        return bank[:, 6 + u % 2, 0:HG * HD].rearrange("p (i d) -> p i d", i=HG)

    with nc.Block() as block:
        @block.sync
        def _(sp):
            for win, cache, new in ((k_win, cache_k, k_nat), (v_win, cache_v, v_nat)):
                if win is v_win:
                    sp.wait_ge(wspT_banked, 2)
                sp.dma_start(win[0:P - 1], cache[0, :, 1:P].rearrange("b s k d -> s b (k d)")).then_inc(win_landed, 16)
                sp.dma_start(win[P - 1:P], new[0:NS, NT, :]).then_inc(win_landed, 16)
            sp.wait_ge(win_landed, 64)
            for win, out in ((k_win, sample_k), (v_win, sample_v)):
                sp.dma_start(out[0].rearrange("b s k d -> s b (k d)"), win[:]).then_inc(a_out, 16)
            sp.wait_ge(a_out, 32)

        @block.gpsimd
        def _(pool):
            mine = pool_steps.on(pool)
            for h in range(H):
                mine(nc.gpsimd.memset(slope_s[:, h:h + 1], -SLOPES[h]))
            nc.gpsimd.iota(dist_s[:, 0:1].bitcast(I32), pattern=[[0, 1]], base=P - 1, channel_multiplier=-1).then_inc(iota_ready, 1)

        @block.scalar
        def _(act):
            mine = act_steps.on(act)
            act.dma_start(gain_o[:, 0:CB], g_out_a[0:1, :].to_broadcast([P, CB])).then_inc(gain_o_landed, 16)
            act.dma_start(gain_o[:, CB:2 * CB], g_out_b[0:1, :].to_broadcast([P, CB])).then_inc(gain_o_landed, 16)
            for j in range(2):
                act.wait_ge(wspT_banked, j + 1)
                nc.scalar.activation(wspT[:, 4 * j:4 * j + 4, :], bank[:, 4 + j, :], ACT.Copy).then_inc(wspT_ready, 1)
            act.wait_ge(kT_banked, 1)
            nc.scalar.activation(kT[:], bank[:, 6, :], ACT.Copy).then_inc(kT_ready, 1)
            for n in range(NT):
                act.wait_ge(qT_banked, n + 1)
                nc.scalar.activation(qT[:, n, :, :], bank[:, (7, 4, 5, 6)[n], :], ACT.Copy).then_inc(qT_ready, 1)
            for n in range(LEAD):
                write_hi(act, n, n // 2, n % 2, CB, o_hi, o_used, 32)

            def exps(u):
                n, g = UNITS[u]
                lo = P if n == 0 else 0
                st, pr = m_[u % 3], probs[u % 2]
                act.wait_ge(max_ready, u + 1)
                for i in range(HG):
                    nc.scalar.activation(pr[:, i, lo:2 * P], pr[:, i, lo:2 * P], ACT.Exp, bias=st[:, 1, i:i + 1],
                                         accum_out=st[:, 3, i:i + 1])
                nc.scalar.activation(st[:, 2, :], st[:, 2, :], ACT.Exp).then_inc(exp_ready, 1)

            exps(0)
            for u in range(len(UNITS)):
                turned(act, u)
                if u + 1 < len(UNITS):
                    exps(u + 1)
            for j in range(2):
                act.wait_ge(ksT_banked, j + 1)
                nc.scalar.activation(ksT[:, 4 * j:4 * j + 4, :], bank[:, j, :], ACT.Copy).then_inc(ksT_ready, 1)
            act.wait_ge(ksT_banked, 3)
            nc.scalar.activation(qsT[:], bank[:, 2, 0:HG * NS], ACT.Copy).then_inc(ksT_ready, 1)
            act.wait_ge(pv_read, len(UNITS))
            act.wait_ge(gate_read, G)
            for t in range(NT):
                y_squares(mine, t, probs[0][:].rearrange("p i s -> p (i s)")[:, 0:CB])
            act.wait_ge(ss_cut, 2)
            nc.scalar.activation(s_exp[:], bank[0:NS * H, 4, 0:P], ACT.Exp, bias=s_st[:, 1:2], accum_out=s_st[:, 3:4])
            nc.scalar.activation(s_st[:, 2:3], s_st[:, 2:3], ACT.Exp).then_inc(ss_exp, 1)
            mine.settle()
            for t in range(NT):
                y_root(t)
            act.wait_ge(spT_done, 1)
            nc.scalar.activation(s_pT[:], bank[:, 5, 0:NS * H], ACT.Copy).then_inc(spT_ready, 1)
            act.wait_ge(sy_done, 1)
            pv = bank[:, 6, 0:NS * H].rearrange("p (b h) -> p h b", h=H)
            nc.scalar.activation(ysT[0:HD], pv[0:HD, 0:HG], ACT.Copy)
            nc.scalar.activation(ysT[HD:2 * HD], pv[HD:2 * HD, HG:H], ACT.Copy).then_inc(sy_cut, 1)
            act.wait_ge(syT_done, 1)
            nc.scalar.activation(uq[0:NS, NT, CB:2 * CB].rearrange("p (g i d) -> p i g d", g=KV, i=HG),
                                 bank[0:NS, 7, :].rearrange("p (i g d) -> p i g d", g=KV, i=HG), ACT.Copy).then_inc(sy_ready, 1)

        @block.vector
        def _(dve):
            mine = dve_steps.on(dve)
            dve.wait_ge(iota_ready, 1)
            mine(nc.vector.tensor_copy(dist_s[:, 1:2], dist_s[:, 0:1].bitcast(I32)))
            mine.settle()
            mine(nc.vector.tensor_scalar(bias_s[:], slope_s[:], dist_s[:, 1:2], None, ALU.mult))
            for g in range(G):
                dve.wait_ge(gate_done, 2 * (g // 2) + 2)
                y = uq[:, 0:NT, g * HD:(g + 1) * HD]
                mine(nc.vector.scalar_tensor_tensor(y, bank[:, g // 2, (g % 2) * 256:(g % 2) * 256 + 256]
                     .rearrange("p (n d) -> p n d", n=NT), bspT[:, g:g + 1], y, ALU.add, ALU.mult), gate_read)
            vs = va[0:NS, NT, :].rearrange("p (g d) -> p g d", g=G)
            ys = uq[0:NS, NT, 0:CB].rearrange("p (g d) -> p g d", g=G)
            mine(nc.vector.tensor_tensor(vs, vs, w00[:].unsqueeze(2).to_broadcast([NS, G, HD]), ALU.mult))
            mine.settle()
            mine(nc.vector.tensor_tensor(vs, vs, b00[:].unsqueeze(2).to_broadcast([NS, G, HD]), ALU.add))
            mine.settle()
            mine(nc.vector.tensor_tensor(ys, ys, vs, ALU.mult))

            def scores(u):
                n, g = UNITS[u]
                lo = P if n == 0 else 0
                st, pr = m_[u % 3], probs[u % 2]
                dve.wait_ge(score_done, u + 1)
                if u >= 2:
                    dve.wait_ge(pT_banked, u - 1)
                mine(nc.vector.scalar_tensor_tensor(pr[:, :, lo:2 * P], s_bank(u)[:, :, lo:2 * P], HD ** -0.5,
                     alibi[:, g * HG:(g + 1) * HG, lo:2 * P], ALU.mult, ALU.add), score_read)
                mine.settle()
                mine(nc.vector.tensor_reduce(st[:, 0, :], pr[:, :, lo:2 * P], AX, ALU.max))
                mine.settle()
                sk = sink_b[:, g * HG:(g + 1) * HG]
                mine(nc.vector.tensor_tensor(st[:, 0, :], st[:, 0, :], sk, ALU.max))
                mine.settle()
                mine(nc.vector.tensor_scalar(st[:, 1, :], st[:, 0, :], -1.0, None, ALU.mult))
                mine.settle()
                mine(nc.vector.tensor_tensor(st[:, 2, :], sk, st[:, 1, :], ALU.add), max_ready)

            def values(u):
                n, g = UNITS[u]
                st = m_[u % 3]
                dve.wait_ge(exp_ready, u + 1)
                mine(nc.vector.tensor_tensor(st[:, 4, :], st[:, 3, :], st[:, 2, :], ALU.add))
                mine.settle()
                mine(nc.vector.reciprocal(st[:, 5, :], st[:, 4, :]))
                mine.settle()
                dve.wait_ge(pv_done, u + 1)
                mine(nc.vector.tensor_tensor(
                    uq[:, n, CB + g * HG * HD:CB + (g + 1) * HG * HD].rearrange("p (i d) -> p i d", i=HG),
                    o_bank(u), st[:, 5, :].unsqueeze(2).to_broadcast([P, HG, HD]), ALU.mult), pv_read)

            for u in range(len(UNITS)):
                scores(u)
                if u >= 2:
                    values(u - 2)
            values(len(UNITS) - 2)
            values(len(UNITS) - 1)
            for n in range(LEAD):
                write_lo(dve, n, n // 2, n % 2, CB, o_hi, o_lo, o_used, 32)
            dve.wait_ge(ss_done, 1)
            for g in range(KV):
                h0 = g * HG
                ins = nc.vector.scalar_tensor_tensor(s_pre[:].rearrange("p (b h) -> p b h", h=H)[:, :, h0:h0 + HG],
                     bank[:, 2 + g, 0:NS * HG].rearrange("p (b h) -> p b h", h=HG), HD ** -0.5,
                     bias_s[:, h0:h0 + HG].unsqueeze(1).to_broadcast([P, NS, HG]), ALU.mult, ALU.add)
                mine(ins, ss_cut if g == KV - 1 else None)
            dve.wait_ge(ssT_done, 1)
            mine(nc.vector.tensor_reduce(s_st[:, 0:1], bank[0:NS * H, 4, 0:P], AX, ALU.max))
            mine.settle()
            mine(nc.vector.tensor_tensor(s_st[:, 0:1], s_st[:, 0:1], sink64[:], ALU.max))
            mine.settle()
            mine(nc.vector.tensor_scalar(s_st[:, 1:2], s_st[:, 0:1], -1.0, None, ALU.mult))
            mine.settle()
            mine(nc.vector.tensor_tensor(s_st[:, 2:3], sink64[:], s_st[:, 1:2], ALU.add), ss_cut)
            dve.wait_ge(ss_exp, 1)
            mine(nc.vector.tensor_tensor(s_st[:, 4:5], s_st[:, 3:4], s_st[:, 2:3], ALU.add))
            mine.settle()
            mine(nc.vector.reciprocal(s_st[:, 5:6], s_st[:, 4:5]))
            mine.settle()
            mine(nc.vector.tensor_scalar(s_exp[:], s_exp[:], s_st[:, 5:6], None, ALU.mult), ss_prob)
            dve.wait_ge(gain_o_landed, 32)
            for t in range(NT):
                y_norm(dve, mine, t)

        @block.tensor
        def _(pe):
            for g in range(G):
                last = nc.tensor.transpose(bank[:, 4 + g // 4, (g % 4) * P:(g % 4 + 1) * P], wsp[:, g, :], ident[:])
                if g % 4 == 3:
                    last.then_inc(wspT_banked, 1)
            for n in range(NT):
                last = nc.tensor.transpose(bank[:, 6, n * P:(n + 1) * P], k_nat[:, n, :], ident[:])
            last.then_inc(kT_banked, 1)
            for n in range(NT):
                b = (7, 4, 5, 6)[n]
                if n >= 1:
                    pe.wait_ge(wspT_ready, 2)
                    pe.wait_ge(kT_ready, 1)
                for i in range(HG):
                    pair = uq[:, n, CB + i * P:CB + (i + 1) * P]
                    last = nc.tensor.transpose(bank[:, b, i * P:(i + 1) * P], pair, ident[:])
                last.then_inc(qT_banked, 1)
            pe.wait_ge(wspT_ready, 2)
            for g in range(G):
                last = nc.tensor.matmul(bank[:, g // 2, (g % 2) * 256:(g % 2) * 256 + 256], wspT[:, g, :],
                                        va[:, 0:NT, g * HD:(g + 1) * HD], start=True, stop=True)
                last.then_inc(gate_done, 1)
            pe.wait_ge(qT_ready, NT)
            pe.wait_ge(kT_ready, 1)
            pe.wait_ge(gate_read, G)

            def scores(u):
                n, g = UNITS[u]
                lo = P if n == 0 else 0
                if u >= 2:
                    pe.wait_ge(score_read, u - 1)
                for i in range(HG):
                    last = nc.tensor.matmul(s_bank(u)[:, i, lo:2 * P], qT[g * HD:(g + 1) * HD, n, i, :],
                                            kT[g * HD:(g + 1) * HD, (n - 1) * P + lo:(n + 1) * P],
                                            start=True, stop=True)
                last.then_inc(score_done, 1)

            def turn(u):
                n, g = UNITS[u]
                pe.wait_ge(exp_ready, u + 1)
                if u >= 1:
                    pe.wait_ge(pT_ready, u)
                js = (1,) if n == 0 else (0, 1)
                for i in range(HG):
                    for jj, j in enumerate(js):
                        x = i * len(js) + jj
                        last = nc.tensor.transpose(bank[:, 4 + x // 4, (x % 4) * P:(x % 4 + 1) * P],
                                                   probs[u % 2][:, i, j * P:(j + 1) * P], ident[:])
                last.then_inc(pT_banked, 1)

            def values(u):
                n, g = UNITS[u]
                pe.wait_ge(pT_ready, u + 1)
                if u >= 2:
                    pe.wait_ge(pv_read, u - 1)
                js = (1,) if n == 0 else (0, 1)
                for i in range(HG):
                    for jj, j in enumerate(js):
                        last = nc.tensor.matmul(o_bank(u)[:, i, :], pT[:, i * len(js) + jj, :],
                                                v_nat[:, n - 1 + j, g * HD:(g + 1) * HD],
                                                start=jj == 0, stop=j == 1)
                last.then_inc(pv_done, 1)

            scores(0)
            scores(1)
            for u in range(len(UNITS)):
                turn(u)
                if u + 2 < len(UNITS):
                    scores(u + 2)
                values(u)
            pe.wait_ge(win_landed, 64)
            pe.wait_ge(score_read, len(UNITS))
            for b in range(NS):
                last = nc.tensor.transpose(bank[:, b // 4, (b % 4) * P:(b % 4 + 1) * P], k_win[:, b, :], ident[:])
                if b % 4 == 3:
                    last.then_inc(ksT_banked, 1)
            for i in range(HG):
                pair = uq[0:NS, NT, CB + i * P:CB + (i + 1) * P]
                last = nc.tensor.transpose(bank[:, 2, i * NS:(i + 1) * NS], pair, ident[0:NS, 0:NS])
            last.then_inc(ksT_banked, 1)
            pe.wait_ge(ksT_ready, 3)
            for b in range(NS):
                for g in range(KV):
                    last = nc.tensor.matmul(bank[:, 2 + g, b * HG:(b + 1) * HG],
                                            ksT[g * HD:(g + 1) * HD, b, :], qsT[g * HD:(g + 1) * HD, :, b],
                                            start=True, stop=True)
            last.then_inc(ss_done, 1)
            pe.wait_ge(ss_cut, 1)
            nc.tensor.transpose(bank[0:NS * H, 4, 0:P], s_pre[:], ident[:]).then_inc(ssT_done, 1)
            pe.wait_ge(ss_prob, 1)
            nc.tensor.transpose(bank[:, 5, 0:NS * H], s_exp[:], ident[0:NS * H, 0:NS * H]).then_inc(spT_done, 1)
            pe.wait_ge(spT_ready, 1)
            pe.wait_ge(pv_read, len(UNITS))
            for b in range(NS):
                last = nc.tensor.matmul(bank[:, 6, b * H:(b + 1) * H], v_win[:, b, :], s_pT[:, b * H:(b + 1) * H],
                                        start=True, stop=True)
            last.then_inc(sy_done, 1)
            pe.wait_ge(sy_cut, 1)
            for i in range(HG):
                last = nc.tensor.transpose(bank[0:NS, 7, i * P:(i + 1) * P], ysT[:, i, :], ident[:])
            last.then_inc(syT_done, 1)

    x_res = [va, at("x_res_1", [P, TILES, CB], F32, SIDE)]
    junk = at("junk", [P, CB], F32, SIDE + 10240)
    assert TILES * CB * 4 <= 10240
    o = SPLIT + 2 * HALF_B
    w_r = scratch("w_r", [P, KC, E])
    b_r = scratch("b_r", [P, E])
    gain_m = scratch("gain_m", [P, D])
    iota_e = scratch("iota_e", [P, E])
    iota_128e = scratch("iota_128e", [P, E])
    before = scratch("before", [P, P])
    ones = scratch("ones", [P, P])
    iota_i = scratch("iota_i", [P, E], I32)
    hnT = [scratch(f"hnT_{i}", [P, KC, P]) for i in range(2)]
    h_stat = scratch("h_stat", [P, 8 * TILES])
    onehot = scratch("onehot", [P, TILES, TOPK, E])
    chosen = scratch("chosen", [P, TILES, E])
    chosen_sum = scratch("chosen_sum", [P, NT, E])
    slot_e = scratch("slot_e", [P, TILES, E])
    logits = scratch("logits", [P, TILES, E])
    to_place = scratch("to_place", [P, TOPK, E])
    top = scratch("top", [P, TILES, 8])
    top_i = scratch("top_i", [P, TILES, 8], U32)
    top_f = scratch("top_f", [P, TILES, TOPK])
    gsum = scratch("gsum", [P, 2 * TILES])
    total = scratch("total", [P, E])
    extra = [scratch(f"extra_{i}", [P, E]) for i in range(3)]
    token_place = scratch("token_place", [P, TILES, TOPK, 2], I32)
    slot_i = scratch("slot_i", [P, TILES, TOPK], I32)
    slot_f = scratch("slot_f", [P, TILES, TOPK])
    beyond = scratch("beyond", [P, TILES, E])
    beyond_i = scratch("beyond_i", [P, TILES, TOPK], I32)
    assert LEAD == 3 and o <= SPLIT + 2 * LEAD * HALF_B
    hn = [at(f"hn_{i}", [P, D], F32, MAIN + 2 * XT_B + TILES * 2 * CB * 4 + i * D * 4) for i in range(2)]
    NB2 = OVER + 2
    iota_b = at("iota_b", [1, NB2], F32, MAIN)
    owner = at("owner", [1, NB2, E], F32, MAIN + 128)
    owner_f = at("owner_f", [1, NB2], F32, MAIN + 128 + NB2 * E * 4)
    blocks_f = at("blocks_f", [1, 1], F32, MAIN + 128 + NB2 * E * 4 + 128)
    product_prod = at("product_prod", [P, TILES * TOPK, E], F32, MAIN + 4096)
    LATE = MAIN + 2 * XT_B + TILES * 2 * CB * 4 + 2 * D * 4 + 512
    block_expert = at("block_expert", [1, NBMAX + 2], I32, LATE)
    n_extra = at("n_extra", [1, 1], I32, LATE + 256)
    any_extra = at("any_extra", [1, 1], I32, LATE + 288)

    gain_m_landed, x_res_landed, router_landed = (sem("gain_m_landed"),
        [sem("x_res0_landed"), sem("x_res1_landed")], sem("router_landed"))
    yT_banked, yT_hi, yT_lo, h_ready = sem("yT_banked"), sem("yT_hi"), sem("yT_lo"), sem("h_ready")
    h_ss, hn_ready, hnT_banked, hnT_ready, logit_done, logit_read = (sem("h_ss"), sem("hn_ready"), sem("hnT_banked"),
        sem("hnT_ready"), sem("logit_done"), sem("logit_read"))
    hn_stored, h_stored = [sem(f"hn_stored_{i}") for i in range(2)], sem("h_stored")
    route_consts, gate_in, gate_exp, chosen_ready, count_done, slots_ready, slots_stored = (sem(n) for n in (
        "route_consts", "gate_in", "gate_exp", "chosen_ready", "count_done", "slots_ready", "slots_stored"))
    placed, place_read, extra_known, beyond_ready = sem("placed"), sem("place_read"), sem("extra_known"), sem("beyond_ready")

    def h_ss_at(t):
        return h_stat[0:ROWS[t], 8 * t:8 * t + 1]

    def h_rstd_at(t):
        return h_stat[0:ROWS[t], 8 * t + 1:8 * t + 2]

    def rows_of(dram_rows, t):
        return dram_rows[t * P:t * P + ROWS[t]]

    def turned_h(act, t):
        R = ROWS[t]
        act.wait_ge(hnT_banked, t + 1)
        if t >= 2:
            act.wait_ge(logit_done, t - 1)
        for j in range(2):
            last = nc.scalar.activation(hnT[t % 2][:, 4 * j:4 * j + 4, 0:R],
                                        bank[:, 2 - 2 * (t % 2) + j, 0:4 * R].rearrange("p (c r) -> p c r", c=4), ACT.Copy)
        last.then_inc(hnT_ready, 1)

    def choose(dve, mine, t):
        R = ROWS[t]
        dve.wait_ge(logit_done, t + 1)
        mine(nc.vector.tensor_tensor(logits[0:R, t, :], bank[0:R, 4 + 3 * (t % 2), 0:E], b_r[0:R, :], ALU.add), logit_read)
        mine.settle()
        mine(nc.vector.max(top[0:R, t, :], logits[0:R, t, :]))
        mine.settle()
        mine(nc.vector.max_index(top_i[0:R, t, :], top[0:R, t, :], logits[0:R, t, :]))
        mine.settle()
        mine(nc.vector.tensor_copy(top_f[0:R, t, :], top_i[0:R, t, 0:TOPK]))
        mine.settle()
        mine(nc.vector.tensor_tensor(onehot[0:R, t], iota_e[0:R].unsqueeze(1).to_broadcast([R, TOPK, E]),
                                     top_f[0:R, t].unsqueeze(2).to_broadcast([R, TOPK, E]), ALU.is_equal))
        mine.settle()
        mine(nc.vector.tensor_reduce(chosen[0:R, t, :], onehot[0:R, t].rearrange("p k e -> p e k"), AX, ALU.add),
             chosen_ready if t in (0, NT) else None)
        if 0 < t < NT:
            mine.settle()
            mine(nc.vector.tensor_tensor(chosen_sum[:, t, :], chosen_sum[:, t - 1, :] if t > 1 else chosen[:, 0, :],
                                         chosen[:, t, :], ALU.add), chosen_ready)

    def place(dve, mine, t):
        R = ROWS[t]
        dve.wait_ge(placed, t + 1)
        mine(nc.vector.tensor_scalar(beyond[0:R, t, :], bank[0:R, 5 + t % 2, 0:E], float(P), float(NOWHERE), ALU.is_ge, ALU.mult))
        mine(nc.vector.tensor_tensor(slot_e[0:R, t, :], bank[0:R, 5 + t % 2, 0:E], iota_128e[0:R, :], ALU.add), place_read)
        mine.settle()
        mine(nc.vector.tensor_tensor(logits[0:R, t, :], slot_e[0:R, t, :], beyond[0:R, t, :], ALU.add))
        mine.settle()
        mine(nc.vector.tensor_tensor(to_place[0:R], onehot[0:R, t], logits[0:R, t, :].unsqueeze(1).to_broadcast([R, TOPK, E]),
                                     ALU.mult))
        mine.settle()
        mine(nc.vector.tensor_reduce(slot_f[0:R, t, :], to_place[0:R], AX, ALU.add))
        mine.settle()
        mine(nc.vector.tensor_copy(slot_i[0:R, t, :], slot_f[0:R, t, :]), slots_ready)

    with nc.Block() as block:
        @block.sync
        def _(sp):
            def expert0(w):
                sp.wait_ge(o_hi, 2 * w + 2)
                sp.wait_ge(o_lo, 2 * w + 2)
                sp.dma_start(raw[w][:], w_gu_v[0, :, :, w * D:w * D + CB]).then_inc(raw_landed[w], 16)

            for w in range(2):
                cols = slice(w * CB, (w + 1) * CB)
                sp.dma_start(x_res[w][:, 0:NT, :], x_p[:, cols].rearrange("(n p) d -> p n d", p=P)).then_inc(x_res_landed[w], 16)
                sp.dma_start(x_res[w][0:NS, NT, :], x_s[:, cols]).then_inc(x_res_landed[w], 16)
            expert0(0)
            sp.wait_ge(o_first, 2)
            sp.dma_start(gain_m[:], g_moe[0:1, :].to_broadcast([P, D])).then_inc(gain_m_landed, 16)
            sp.dma_start(w_r[:], w_router[0].rearrange("(c p) e -> p c e", p=P)).then_inc(router_landed, 16)
            sp.dma_start(b_r[:], b_router[0:1, :].to_broadcast([P, E])).then_inc(router_landed, 16)
            expert0(1)
            for t in range(TILES):
                sp.wait_ge(h_ready, TILES + t + 1)
                sp.dma_start(rows_of(h_rows, t), uq[0:ROWS[t], t, :]).then_inc(h_stored, 16)
                sp.wait_ge(hn_ready, t + 1)
                sp.dma_start(rows_of(hn_rows, t), hn[t % 2][0:ROWS[t], :]).then_inc(hn_stored[t % 2], 16)
                if t in (2, 4):
                    w = t // 2 - 1
                    sp.dma_start(raw[4 + w][:], w_dn_v[0, :, :, w * CB:(w + 1) * CB]).then_inc(raw_landed[4 + w], 16)
            sp.wait_ge(h_stored, 16 * TILES)
            for i in range(2):
                sp.wait_ge(hn_stored[i], 16 * len(range(i, TILES, 2)))

        @block.gpsimd
        def _(pool):
            mine = pool_steps.on(pool)
            pool.wait_ge(o_first, 2)
            nc.gpsimd.iota(iota_i[:], pattern=[[1, E]], base=0, channel_multiplier=0)
            nc.gpsimd.iota(token_place[:, :, :, 0], pattern=[[P, TILES], [0, TOPK]], base=0, channel_multiplier=1)
            nc.gpsimd.iota(token_place[:, :, :, 1], pattern=[[P, TILES], [TOK, TOPK]], base=0, channel_multiplier=1)
            mine(nc.gpsimd.memset(before[:], 1.0))
            mine.settle()
            nc.gpsimd.memset(ones[:], 1.0)
            nc.gpsimd.affine_select(out=before[:], in_=before[:], compare_op=ALU.is_ge, fill=0.0, base=-1,
                                    pattern=[[1, P]], channel_multiplier=-1).then_inc(route_consts, 1)
            def scatter(t, slots):
                for k in range(TOPK):
                    pool.indirect_dma_start(slot_table, bass.IndirectOffsetOnAxis(slots[0:ROWS[t], t, k:k + 1], 0),
                                            token_place[0:ROWS[t], t, k, :], None, bounds_check=TABLE - 1,
                                            oob_is_err=False).then_inc(slots_stored, 16)

            for t in range(TILES):
                pool.wait_ge(slots_ready, t + 1)
                scatter(t, slot_i)
            pool.wait_ge(extra_known, 1)
            some = pool.value_load(any_extra[0:1, 0:1], min_val=0, max_val=1)
            with pool.If(some > 0):
                pool.wait_ge(beyond_ready, 1)
                for t in range(TILES):
                    scatter(t, beyond_i)
                pool.wait_ge(slots_stored, 2 * 16 * TILES * TOPK)
            pool.wait_ge(slots_stored, 16 * TILES * TOPK)

        @block.scalar
        def _(act):
            mine = act_steps.on(act)
            y_squares(mine, NT, junk)
            mine.settle()
            y_root(NT)
            for t in range(TILES):
                R, c0 = ROWS[t], column(t)
                act.wait_ge(yT_banked, t + 1)
                b = 2 * (t % 4)
                for j in range(2):
                    last = nc.scalar.activation(xT_hi[:, 4 * j:4 * j + 4, c0:c0 + R],
                                                bank[:, b + j, 0:4 * R].rearrange("p (c r) -> p c r", c=4), ACT.Copy)
                last.then_inc(yT_hi, 1)
            write_hi(act, LEAD, LEAD // 2, LEAD % 2, CB, o_hi, o_used, 32)
            for t in range(TILES):
                R = ROWS[t]
                act.wait_ge(h_ready, TILES + t + 1)
                if t >= 2:
                    act.wait_ge(hn_stored[t % 2], 16 * (t // 2))
                    act.wait_ge(hnT_banked, t - 1)
                elif t == 0:
                    act.wait_ge(h_ready, TILES)
                mine(nc.scalar.activation(hn[t % 2][0:R, :], uq[0:R, t, :], ACT.Square, accum_out=h_ss_at(t)))
                mine.settle()
                mine(nc.scalar.activation(h_ss_at(t), h_ss_at(t), ACT.Sqrt, scale=1.0 / D, bias=EPS), h_ss)
                if t >= 1:
                    turned_h(act, t - 1)
            turned_h(act, TILES - 1)
            act.wait_ge(gate_in, 1)
            nc.scalar.activation(gates[:], gates[:], ACT.Exp).then_inc(gate_exp, 1)

        @block.vector
        def _(dve):
            mine = dve_steps.on(dve)

            y_norm(dve, mine, NT)
            for t in range(TILES):
                R, c0 = ROWS[t], column(t)
                dve.wait_ge(yT_banked, t + 1)
                dve.wait_ge(yT_hi, t + 1)
                b = 2 * (t % 4)
                for j in range(2):
                    last = nc.vector.tensor_tensor(xT_lo[:, 4 * j:4 * j + 4, c0:c0 + R],
                                                   bank[:, b + j, 0:4 * R].rearrange("p (c r) -> p c r", c=4),
                                                   xT_hi[:, 4 * j:4 * j + 4, c0:c0 + R].bitcast(F32), ALU.subtract)
                last.then_inc(yT_lo, 1)
            write_lo(dve, LEAD, LEAD // 2, LEAD % 2, CB, o_hi, o_lo, o_used, 32)
            for w in range(2):
                if w == 1:
                    dve.wait_ge(o_first, 2)
                    mine(nc.vector.memset(top[:], 0.0))
                    for table in (onehot, slot_e, beyond):
                        mine(nc.vector.memset(table[:], 0.0))
                dve.wait_ge(x_res_landed[w], 32)
                for t in range(TILES):
                    R = ROWS[t]
                    dve.wait_ge(mix_done, TILES * w + t + 1)
                    mine(nc.vector.tensor_tensor(uq[0:R, t, w * CB:(w + 1) * CB], bank[0:R, zbank(w, t), :],
                                                 x_res[w][0:R, t, :], ALU.add), h_ready)
            dve.wait_ge(gain_m_landed, 16)
            dve.wait_ge(router_landed, 32)
            dve.wait_ge(route_consts, 1)
            mine(nc.vector.tensor_copy(iota_e[:], iota_i[:]))
            mine.settle()
            mine(nc.vector.tensor_scalar(iota_128e[:], iota_e[:], float(P), None, ALU.mult))
            for t in range(TILES):
                R = ROWS[t]
                dve.wait_ge(h_ss, t + 1)
                mine(nc.vector.reciprocal(h_rstd_at(t), h_ss_at(t)))
                mine.settle()
                mine(nc.vector.scalar_tensor_tensor(hn[t % 2][0:R, :], uq[0:R, t, :], h_rstd_at(t), gain_m[0:R, :],
                                                    ALU.mult, ALU.mult), hn_ready)
                if t >= 2:
                    choose(dve, mine, t - 2)
                if t >= 3:
                    place(dve, mine, t - 3)
            for t in range(NT - 1, TILES):
                choose(dve, mine, t)
                place(dve, mine, t - 1)
            place(dve, mine, NT)
            mine.settle()
            mine(nc.vector.tensor_tensor(gates[:], top[:, :, 0:TOPK], top[:, :, 0:1].to_broadcast([P, TILES, TOPK]),
                                         ALU.subtract), gate_in)
            dve.wait_ge(count_done, 1)
            mine(nc.vector.tensor_copy(total[:], bank[:, 6, 0:E]))
            mine.settle()
            mine(nc.vector.tensor_scalar(extra[0][:], total[:], float(P), None, ALU.is_gt))
            for j in range(2, -(-TOK // P)):
                mine.settle()
                mine(nc.vector.scalar_tensor_tensor(extra[0][:], total[:], float(j * P), extra[0][:], ALU.is_gt, ALU.add))
            mine.settle()
            mine(nc.vector.tensor_tensor_scan(extra[1][:], ones[:, 0:E], extra[0][:], 0.0, ALU.mult, ALU.add))
            mine.settle()
            mine(nc.vector.tensor_copy(n_extra[:], extra[1][0:1, E - 1:E]))
            mine(nc.vector.tensor_scalar(any_extra[:], extra[1][0:1, E - 1:E], 1.0, None, ALU.min), extra_known)
            mine(nc.vector.tensor_tensor(extra[2][:], extra[1][:], extra[0][:], ALU.subtract))
            mine.settle()
            mine(nc.vector.tensor_tensor(extra[2][:], extra[2][:], iota_e[:], ALU.subtract))
            mine.settle()
            mine(nc.vector.tensor_scalar(extra[2][:], extra[2][:], float(P), float((E - 1) * P), ALU.mult, ALU.add))
            mine.settle()
            mine(nc.vector.tensor_tensor(slot_e[:], slot_e[:], extra[2][:].unsqueeze(1).to_broadcast([P, TILES, E]), ALU.add))
            mine.settle()
            mine(nc.vector.tensor_tensor(slot_e[:], slot_e[:], beyond[:], ALU.subtract))
            mine.settle()
            mine(nc.vector.tensor_scalar(slot_e[:], slot_e[:], float(NOWHERE), None, ALU.add))
            mine.settle()
            mine(nc.vector.tensor_tensor(product_prod[:].rearrange("p (t k) e -> p t k e", k=TOPK), onehot[:],
                                         slot_e[:].unsqueeze(2).to_broadcast([P, TILES, TOPK, E]), ALU.mult))
            mine.settle()
            mine(nc.vector.tensor_reduce(slot_f[:], product_prod[:].rearrange("p (t k) e -> p t k e", k=TOPK), AX, ALU.add))
            mine.settle()
            mine(nc.vector.tensor_copy(beyond_i[:], slot_f[:]), beyond_ready)
            mine(nc.vector.tensor_scalar(iota_b[:], iota_e[0:1, 0:NB2], 1.0, None, ALU.mult))
            mine.settle()
            mine(nc.vector.tensor_tensor(owner[:], iota_b[:].unsqueeze(2).to_broadcast([1, NB2, E]),
                                         extra[1][0:1, :].unsqueeze(1).to_broadcast([1, NB2, E]), ALU.is_ge))
            mine.settle()
            mine(nc.vector.tensor_reduce(owner_f[:], owner[:], AX, ALU.add))
            mine.settle()
            mine(nc.vector.tensor_copy(block_expert[0:1, 0:E], iota_i[0:1, :]))
            mine(nc.vector.tensor_scalar(block_expert[0:1, E:], owner_f[:], float(E - 1), None, ALU.min))
            dve.wait_ge(gate_exp, 1)
            mine(nc.vector.tensor_reduce(gsum[:, 0:TILES], gates[:], AX, ALU.add))
            mine.settle()
            mine(nc.vector.reciprocal(gsum[:, TILES:2 * TILES], gsum[:, 0:TILES]))
            mine.settle()
            mine(nc.vector.tensor_tensor(gates[:], gates[:], gsum[:, TILES:2 * TILES].unsqueeze(2).to_broadcast([P, TILES, TOPK]),
                                         ALU.mult))
            mine.settle()
            mine(nc.vector.tensor_tensor(product_prod[:], onehot[:].rearrange("p t k e -> p (t k) e"),
                                         gates[:].rearrange("p t k -> p (t k)").unsqueeze(2).to_broadcast([P, TILES * TOPK, E]),
                                         ALU.mult))
            mine.settle()
            mine(nc.vector.tensor_reduce(gate_table[:], product_prod[:].rearrange("p (t k) e -> p t e k", k=TOPK), AX, ALU.add))

        @block.tensor
        def _(pe):
            def positions(t):
                R, here = ROWS[t], chosen[0:ROWS[t], t, :]
                earlier = chosen[:, 0, :] if t <= 1 else chosen_sum[:, t - 1, :]
                if t == 0:
                    pe.wait_ge(route_consts, 1)
                pe.wait_ge(chosen_ready, t + 1)
                if t >= 2:
                    pe.wait_ge(place_read, t - 1)
                if t > 0:
                    nc.tensor.matmul(bank[0:R, 5 + t % 2, 0:E], ones[:, 0:R], earlier, start=True, stop=False)
                nc.tensor.matmul(bank[0:R, 5 + t % 2, 0:E], before[0:R, 0:R], here, start=t == 0, stop=True).then_inc(placed, 1)
                if t == NT:
                    pe.wait_ge(place_read, NT)
                    nc.tensor.matmul(bank[:, 6, 0:E], ones[:], earlier, start=True, stop=False)
                    nc.tensor.matmul(bank[:, 6, 0:E], ones[0:R, :], here, start=False, stop=True).then_inc(count_done, 1)

            for t in range(TILES):
                R = ROWS[t]
                pe.wait_ge(y_normed, t + 1)
                if t == 4:
                    pe.wait_ge(yT_lo, 1)
                for c in range(KC):
                    last = nc.tensor.transpose(bank[:, 2 * (t % 4) + c // 4, (c % 4) * R:(c % 4 + 1) * R],
                                               uq[0:R, t, c * P:(c + 1) * P], ident[0:R, 0:R])
                last.then_inc(yT_banked, 1)
            for n in range(4):
                w, h = n // 2, n % 2
                pe.wait_ge(o_hi, n + 1)
                pe.wait_ge(o_lo, n + 1)
                for t in range(TILES):
                    if n == 0:
                        pe.wait_ge(yT_hi, turned_before(t) + 1)
                        pe.wait_ge(yT_lo, turned_before(t) + 1)
                    if h == 0 and TILES * w + t >= 8:
                        pe.wait_ge(h_ready, TILES * w + t - 7)
                    last = product(nc, bank[:, zbank(w, t), :], stationary(xT_hi, t), stationary(xT_lo, t),
                                   half_hi[n % LEAD], half_lo[n % LEAD],
                                   [(h * HALFK + k, k) for k in range(HALFK)], CB, h == 0, h == 1)
                    if h == 1:
                        last.then_inc(mix_done, 1)
                if h == 0:
                    last.then_inc(o_first, 1)
            def turn_h(t):
                R = ROWS[t]
                pe.wait_ge(hn_ready, t + 1)
                if t >= 2:
                    pe.wait_ge(hnT_ready, t - 1)
                for c in range(KC):
                    last = nc.tensor.transpose(bank[:, 2 - 2 * (t % 2) + c // 4, (c % 4) * R:(c % 4 + 1) * R],
                                               hn[t % 2][0:R, c * P:(c + 1) * P], ident[0:R, 0:R])
                last.then_inc(hnT_banked, 1)

            pe.wait_ge(router_landed, 32)
            pe.wait_ge(h_ready, 2 * TILES)
            turn_h(0)
            for t in range(TILES):
                R = ROWS[t]
                if t + 1 < TILES:
                    turn_h(t + 1)
                pe.wait_ge(hnT_ready, t + 1)
                if t >= 2:
                    pe.wait_ge(logit_read, t - 1)
                for c in range(KC):
                    last = nc.tensor.matmul(bank[0:R, 4 + 3 * (t % 2), 0:E], hnT[t % 2][:, c, 0:R], w_r[:, c, :],
                                            start=c == 0, stop=c == KC - 1)
                last.then_inc(logit_done, 1)
                if t >= 1:
                    positions(t - 1)
            positions(NT)

    o = MAIN
    xg = scratch("xg", [P, D])
    xg_hi = scratch("xg_hi", [P, KC, P], F32R)
    xg_lo = scratch("xg_lo", [P, KC, P], F32R)
    gate_sb = scratch("gate_sb", [P, CB])
    up_sb = scratch("up_sb", [P, CB])
    sig_sb = scratch("sig_sb", [P, CB])
    acts = scratch("acts", [P, D])
    aT_hi = scratch("aT_hi", [P, KC, P], F32R)
    aT_lo = scratch("aT_lo", [P, KC, P], F32R)
    y_sb = scratch("y_sb", [P, D])
    bias_sb = scratch("bias_sb", [34, D], F32R)
    ones_r = scratch("ones_r", [34, P], F32R)
    idx_in = scratch("idx_in", [P, 2], I32)
    idx_out = scratch("idx_out", [P, 2], I32)
    assert o <= LATE

    e_dve, indices_seen = sem("e_dve"), sem("indices_seen")
    hi_ready, lo_ready, half_used = sem("hi_ready"), sem("lo_ready"), sem("half_used")
    xg_clear, ones_ready, xg_landed, bias_landed, idx_in_landed, idx_out_landed, y_stored = (sem(n) for n in (
        "xg_clear", "ones_ready", "xg_landed", "bias_landed", "idx_in_landed", "idx_out_landed", "y_stored"))
    xg_turned, xg_hi_ready, xg_lo_ready = sem("xg_turned"), sem("xg_hi_ready"), sem("xg_lo_ready")
    acts_turned, aT_hi_ready, aT_lo_ready = sem("acts_turned"), sem("aT_hi_ready"), sem("aT_lo_ready")
    gate_ready, up_read, sig_ready, acts_ready, y_ready = (sem("gate_ready"), sem("up_read"), sem("sig_ready"),
                                                           sem("acts_ready"), sem("y_ready"))

    def half(b, h):
        return h if isinstance(b, int) and b == 0 else 12 * b - 4 + h

    def slot(b, h):
        return h % LEAD if isinstance(b, int) and b == 0 else (h - 4) % LEAD

    def landed(b, h):
        s = h // 2
        return s, 16 * (b + 3) if s < 2 else 16 * (b + 2) if s < 4 else 16 * b

    def down_half(last):
        return 0 if last else 8

    def blocks(engine):
        return engine.value_load(n_extra[0:1, 0:1], min_val=0, max_val=OVER) + E

    def expert_of(engine, b):
        return b if isinstance(b, int) else engine.value_load(block_expert[0:1, bass.ds(b, 1)], min_val=0, max_val=E - 1)

    with nc.Block() as block:
        @block.sync
        def _(sp):
            def free(b, h):
                sp.wait_ge(hi_ready, half(b, h) + 1)
                sp.wait_ge(lo_ready, half(b, h) + 1)

            def gate_up(b):
                e = expert_of(sp, b)
                for s in range(4):
                    free(b - 1, 2 * s + 1)
                    c0 = (s % 2) * D + (s // 2) * CB
                    sp.dma_start(raw[s][:], w_gu_v[e, :, :, c0:c0 + CB]).then_inc(raw_landed[s], 16)

            def down(b):
                e = expert_of(sp, b - 1)
                for s in range(2):
                    free(b - 1, 9 + 2 * s)
                    sp.dma_start(raw[4 + s][:], w_dn_v[e, :, :, s * CB:(s + 1) * CB]).then_inc(raw_landed[4 + s], 16)

            nb = blocks(sp)
            sp.wait_ge(xg_landed, 16)
            gate_up(1)
            with sp.Fori(2, nb) as b:
                gate_up(b)
                down(b)
            for s in range(2):
                free(nb - 1, 2 * s + 1)
                sp.dma_start(raw[s][:], w_pg_v[:, :, s * CB:(s + 1) * CB]).then_inc(raw_landed[s], 16)
            free(nb - 1, 5)
            sp.dma_start(raw[2][:].rearrange("p c n -> p (c n)")[:, 0:PC * D].rearrange("p (c n) -> p c n", c=PC),
                         w_pp_v).then_inc(raw_landed[2], 16)
            down(nb)

        @block.gpsimd
        def _(pool):
            nb = blocks(pool)
            last_token, last_row = pool.to_reg(TOK - 1), pool.to_reg(TOPK * TOK - 1)

            def fetch(b):
                pool.dma_start(idx_in[:], slot_table[b * P:(b + 1) * P, :] if isinstance(b, int)
                               else slot_table[bass.ds(b * P, P), :]).then_inc(idx_in_landed, 16)
                pool.wait_ge(idx_in_landed, 16 * (b + 1))
                if not isinstance(b, int) or b >= 1:
                    pool.wait_ge(xg_turned, b)
                pool.sem_inc(indices_seen, 1)
                pool.indirect_dma_start(xg[:], None, hn_rows, bass.IndirectOffsetOnAxis(idx_in[:, 0:1], 0),
                                        bounds_check=last_token, oob_is_err=False).then_inc(xg_landed, 16)
                pool.wait_ge(xg_landed, 16 * (b + 1))

            def bias(b):
                e = expert_of(pool, b)
                if not isinstance(b, int) or b >= 1:
                    pool.wait_ge(half_used, half(b - 1, 7) + 1)
                for s in range(2):
                    pool.dma_start(bias_sb[32 * s:32 * s + 2, :].bitcast(F32), bias_rows[e, s]).then_inc(bias_landed, 16)

            def store(b):
                pool.dma_start(idx_out[:], slot_table[bass.ds(b * P, P), :] if not isinstance(b, int)
                               else slot_table[b * P:(b + 1) * P, :]).then_inc(idx_out_landed, 16)
                pool.wait_ge(idx_out_landed, 16 * (b + 1))
                pool.wait_ge(y_ready, 2 * (b + 1))
                pool.sem_inc(indices_seen, 1)
                pool.indirect_dma_start(expert_rows, bass.IndirectOffsetOnAxis(idx_out[:, 1:2], 0), y_sb[:], None,
                                        bounds_check=last_row, oob_is_err=False).then_inc(y_stored, 16)
                pool.wait_ge(y_stored, 16 * (b + 1))

            bias(0)
            pool.wait_ge(xg_clear, 1)
            fetch(0)
            fetch(1)
            bias(1)
            fetch(2)
            bias(2)
            fetch(3)
            store(0)
            with pool.Fori(2, nb) as b:
                bias(b + 1)
                fetch(b + 2)
                store(b - 1)
            store(nb - 1)

        @block.scalar
        def _(act):
            nb = blocks(act)

            def hi(b, h, down=0):
                s, value = landed(b, h + down)
                act.wait_ge(raw_landed[s], value)
                if not isinstance(b, int) or half(b, h) >= LEAD:
                    act.wait_ge(half_used, half(b, h) - LEAD + 1)
                nc.scalar.activation(half_hi[slot(b, h)][:], raw_half(s, h % 2), ACT.Copy).then_inc(hi_ready, 1)

            def x_hi(b):
                act.wait_ge(xg_turned, b + 1)
                for j in range(2):
                    last = nc.scalar.activation(xg_hi[:, 4 * j:4 * j + 4, :], bank[:, 6 + j, :], ACT.Copy)
                last.then_inc(xg_hi_ready, 1)

            def a_hi(b, p):
                act.wait_ge(acts_turned, 2 * b + p + 1)
                nc.scalar.activation(aT_hi[:, 4 * p:4 * p + 4, :], bank[:, 6 + p, :], ACT.Copy).then_inc(aT_hi_ready, 1)

            def sigmoid(b, p):
                act.wait_ge(gate_ready, 2 * b + p + 1)
                if not isinstance(b, int) or b + p > 0:
                    act.wait_ge(acts_ready, 2 * b + p)
                nc.scalar.activation(sig_sb[:], gate_sb[:], ACT.Sigmoid, scale=ALPHA).then_inc(sig_ready, 1)

            def y_out(b, s, last=False):
                act.wait_ge(half_used, half(b + 1, down_half(last) + 2 * s + 1) + 1)
                if s == 0 and (not isinstance(b, int) or b >= 1):
                    act.wait_ge(y_stored, 16 * b)
                nc.scalar.activation(y_sb[:, s * CB:(s + 1) * CB], bank[:, 4 + s, :], ACT.Copy).then_inc(y_ready, 1)

            def turn(b, down, carried):
                if carried:
                    hi(b, 0)
                    hi(b, 1)
                if carried:
                    y_out(b - 2, 1)
                if down:
                    a_hi(b - 1, 0)
                for h in (2, 3, 4, 5) if down else (3, 4, 5):
                    hi(b, h)
                if down:
                    a_hi(b - 1, 1)
                hi(b, 6)
                sigmoid(b, 0)
                hi(b, 7)
                if down:
                    hi(b, 8)
                    hi(b, 9)
                    hi(b, 10)
                else:
                    hi(b + 1, 0)
                    hi(b + 1, 1)
                x_hi(b + 1)
                sigmoid(b, 1)
                if down:
                    hi(b, 11)
                    y_out(b - 1, 0)

            for h in range(LEAD):
                hi(0, h)
            x_hi(0)
            turn(0, False, False)
            turn(1, True, False)
            with act.Fori(2, nb) as b:
                turn(b, True, True)
            y_out(nb - 2, 1)
            a_hi(nb - 1, 0)
            hi(nb, 0, 8)
            a_hi(nb - 1, 1)
            hi(nb, 1, 8)
            hi(nb, 2, 8)
            hi(nb, 3, 8)
            y_out(nb - 1, 0, True)
            y_out(nb - 1, 1, True)

        @block.vector
        def _(dve):
            mine = Signals(dve, e_dve)
            nb = blocks(dve)

            def lo(b, h, down=0):
                s, value = landed(b, h + down)
                dve.wait_ge(raw_landed[s], value)
                dve.wait_ge(hi_ready, half(b, h) + 1)
                if not isinstance(b, int) or half(b, h) >= LEAD:
                    dve.wait_ge(half_used, half(b, h) - LEAD + 1)
                mine(nc.vector.tensor_tensor(half_lo[slot(b, h)][:], raw_half(s, h % 2),
                                             half_hi[slot(b, h)][:].bitcast(F32), ALU.subtract), lo_ready)

            def x_lo(b):
                dve.wait_ge(xg_turned, b + 1)
                dve.wait_ge(xg_hi_ready, b + 1)
                for j in range(2):
                    last = nc.vector.tensor_tensor(xg_lo[:, 4 * j:4 * j + 4, :], bank[:, 6 + j, :],
                                                   xg_hi[:, 4 * j:4 * j + 4, :].bitcast(F32), ALU.subtract)
                mine(last, xg_lo_ready)

            def a_lo(b, p):
                dve.wait_ge(acts_turned, 2 * b + p + 1)
                dve.wait_ge(aT_hi_ready, 2 * b + p + 1)
                mine(nc.vector.tensor_tensor(aT_lo[:, 4 * p:4 * p + 4, :], bank[:, 6 + p, :],
                                             aT_hi[:, 4 * p:4 * p + 4, :].bitcast(F32), ALU.subtract), aT_lo_ready)

            def clamp(b, p):
                dve.wait_ge(half_used, half(b, 4 * p + 3) + 1)
                mine.settle()
                mine(nc.vector.tensor_scalar(gate_sb[:], bank[:, 2 * p, :], LIMIT, None, ALU.min), gate_ready)
                mine(nc.vector.tensor_scalar(up_sb[:], bank[:, 2 * p + 1, :], -LIMIT, LIMIT, ALU.max, ALU.min), up_read)
                mine.settle()
                mine(nc.vector.scalar_tensor_tensor(up_sb[:], up_sb[:], 1.0, gate_sb[:], ALU.add, ALU.mult))

            def activate(b, p):
                dve.wait_ge(sig_ready, 2 * b + p + 1)
                mine.settle()
                if not isinstance(b, int) or b >= 1:
                    dve.wait_ge(acts_turned, 2 * (b - 1) + p + 1)
                mine(nc.vector.tensor_tensor(acts[:, p * CB:(p + 1) * CB], up_sb[:], sig_sb[:], ALU.mult), acts_ready)

            def turn(b, down):
                if down:
                    if not isinstance(b, int):
                        lo(b, 0)
                        lo(b, 1)
                    a_lo(b - 1, 0)
                for h in (2, 3, 4, 5) if down else (3, 4, 5):
                    lo(b, h)
                if down:
                    a_lo(b - 1, 1)
                clamp(b, 0)
                lo(b, 6)
                activate(b, 0)
                lo(b, 7)
                if down:
                    lo(b, 8)
                    lo(b, 9)
                    lo(b, 10)
                else:
                    lo(b + 1, 0)
                    lo(b + 1, 1)
                x_lo(b + 1)
                clamp(b, 1)
                if down:
                    lo(b, 11)
                activate(b, 1)

            mine(nc.vector.memset(xg[:], 0.0), xg_clear)
            mine(nc.vector.memset(ones_r[:].bitcast(F32), 1.0), ones_ready)
            for h in range(LEAD):
                lo(0, h)
            x_lo(0)
            turn(0, False)
            turn(1, True)
            grows = {lo_ready: 12, xg_lo_ready: 1, aT_lo_ready: 2, gate_ready: 2, up_read: 2, e_dve: 2, acts_ready: 2}
            with dve.Fori(2, nb) as b:
                mine.enter_loop(b - 2, grows)
                turn(b, True)
            mine.leave_loop(nb - 2)
            a_lo(nb - 1, 0)
            lo(nb, 0, 8)
            a_lo(nb - 1, 1)
            lo(nb, 1, 8)
            lo(nb, 2, 8)
            lo(nb, 3, 8)

        @block.tensor
        def _(pe):
            nb = blocks(pe)

            def taken(b, h):
                pe.wait_ge(hi_ready, half(b, h) + 1)
                pe.wait_ge(lo_ready, half(b, h) + 1)

            def turn_x(b):
                pe.wait_ge(xg_landed, 16 * (b + 1))
                if not isinstance(b, int) or b >= 2:
                    pe.wait_ge(aT_hi_ready, 2 * (b - 1))
                    pe.wait_ge(aT_lo_ready, 2 * (b - 1))
                for c in range(KC):
                    last = nc.tensor.transpose(bank[:, 6 + c // 4, (c % 4) * P:(c % 4 + 1) * P],
                                               xg[:, c * P:(c + 1) * P], ident[:])
                last.then_inc(xg_turned, 1)

            def turn_acts(b, p):
                pe.wait_ge(acts_ready, 2 * b + p + 1)
                pe.wait_ge(xg_hi_ready, b + 2)
                pe.wait_ge(xg_lo_ready, b + 2)
                for c in range(4):
                    last = nc.tensor.transpose(bank[:, 6 + p, c * P:(c + 1) * P],
                                               acts[:, p * CB + c * P:p * CB + (c + 1) * P], ident[:])
                last.then_inc(acts_turned, 1)

            def gate_up(b, p):
                if not isinstance(b, int) or b >= 1:
                    pe.wait_ge(up_read, 2 * (b - 1) + p + 1)
                if p == 0:
                    pe.wait_ge(bias_landed, 32 * (b + 1))
                    pe.wait_ge(xg_hi_ready, b + 1)
                    pe.wait_ge(xg_lo_ready, b + 1)
                for s in range(2):
                    out = bank[:, 2 * p + s, :]
                    nc.tensor.matmul(out, ones_r[32 * s:32 * s + 2, :], bias_sb[32 * s:32 * s + 2, p * CB:(p + 1) * CB],
                                     start=True, stop=False)
                    for i in range(2):
                        h = 4 * p + 2 * s + i
                        taken(b, h)
                        product(nc, out, lambda c: xg_hi[:, c, :], lambda c: xg_lo[:, c, :], half_hi[slot(b, h)],
                                half_lo[slot(b, h)], [(i * HALFK + k, k) for k in range(HALFK)], CB, False, i == 1
                                ).then_inc(half_used, 1)

            def down(b, last=False):
                pe.wait_ge(aT_hi_ready, 2 * b)
                pe.wait_ge(aT_lo_ready, 2 * b)
                for s in range(2):
                    if not isinstance(b, int) or b >= 2:
                        pe.wait_ge(y_ready, 2 * (b - 2) + s + 1)
                    for i in range(2):
                        h = down_half(last) + 2 * s + i
                        taken(b, h)
                        product(nc, bank[:, 4 + s, :], lambda c: aT_hi[:, c, :], lambda c: aT_lo[:, c, :],
                                half_hi[slot(b, h)], half_lo[slot(b, h)], [(i * HALFK + k, k) for k in range(HALFK)],
                                CB, i == 0, i == 1).then_inc(half_used, 1)

            def turn(b, has_down):
                gate_up(b, 0)
                if has_down:
                    turn_acts(b - 1, 1)
                gate_up(b, 1)
                turn_x(b + 1)
                if has_down:
                    down(b)
                turn_acts(b, 0)

            pe.wait_ge(ones_ready, 1)
            turn_x(0)
            turn(0, False)
            turn(1, True)
            with pe.Fori(2, nb) as b:
                turn(b, True)
            turn_acts(nb - 1, 1)
            down(nb, True)

    o = RAW + 2 * TILE_B + PC * D * 4
    pT_hi = [scratch(f"pT_hi_{i}", [P, PC, P], F32R) for i in range(2)]
    pT_lo = [scratch(f"pT_lo_{i}", [P, PC, P], F32R) for i in range(2)]
    assert o <= RAW + 3 * TILE_B
    o = RAW + 3 * TILE_B
    wg_hi = scratch("wg_hi", [P, KC, D], F32R)
    wg_lo = scratch("wg_lo", [P, KC, D], F32R)
    wp_hi = scratch("wp_hi", [P, PC, D], F32R)
    wp_lo = scratch("wp_lo", [P, PC, D], F32R)
    gain_p = scratch("gain_p", [P, D])
    gain_f = scratch("gain_f", [P, D])
    b_down = scratch("b_down", [E, D])
    ple_in = [scratch(f"ple_in_{i}", [P, PLE]) for i in range(2)]
    gT = scratch("gT", [E, P])
    f_stat = scratch("f_stat", [P, 8 * TILES])
    assert o <= MAIN
    o = MAIN
    HB = 3
    y_in = [scratch(f"y_in_{i}", [P, TOPK, D]) for i in range(2)]
    h_in = [scratch(f"h_in_{i}", [P, D]) for i in range(HB)]
    f_norm = scratch("f_norm", [P, D])
    sg = scratch("sg", [P, D])
    fT_hi = scratch("fT_hi", [P, KC, P], F32R)
    fT_lo = scratch("fT_lo", [P, KC, P], F32R)
    assert o <= keep, o - keep

    gains_landed, b_down_landed = sem("gains_landed"), sem("b_down_landed")
    h_in_landed, y_in_landed, ple_landed = ([sem(f"h_in_landed_{i}") for i in range(HB)],
        [sem(f"y_in_landed_{i}") for i in range(2)], [sem(f"ple_landed_{i}") for i in range(2)])
    y_first_landed = sem("y_first_landed")
    wg_hi_ready, wg_lo_ready = sem("wg_hi_ready"), sem("wg_lo_ready")
    turned_in, turned_read, pT_lo_ready, bdn_done = sem("turned_in"), sem("turned_read"), sem("pT_lo_ready"), sem("bdn_done")
    moe_ready, f_ss, f_normed, fT_banked, fT_hi_ready, fT_lo_ready = (sem(n) for n in (
        "moe_ready", "f_ss", "f_normed", "fT_banked", "fT_hi_ready", "fT_lo_ready"))
    ple_gate_done, ple_proj_done, sg_ready, out_ready, out_ss, y_final, out_stored, embedding_read = (sem(n) for n in (
        "ple_gate_done", "ple_proj_done", "sg_ready", "out_ready", "out_ss", "y_final", "out_stored", "embedding_read"))
    y_by_token = expert_rows.rearrange("(k t) n -> t k n", k=TOPK)
    y_p, y_s = y_prompt[0], y_sample[:, 0, :]
    raw_pp = raw[2][:].rearrange("p c n -> p (c n)")[:, 0:PC * D].rearrange("p (c n) -> p c n", c=PC)

    def two_banks(b, R):
        return bank[0:R, b:b + 2, :].rearrange("p b n -> p (b n)")

    with nc.Block() as block:
        @block.sync
        def _(sp):
            for t in range(TILES):
                R = ROWS[t]
                if t >= 2:
                    sp.wait_ge(turned_in, t - 1)
                sp.dma_start(ple_in[t % 2][0:R, :], tokens(p_prompt[0, 0], p_sample[0, :, 0, :], t)).then_inc(ple_landed[t % 2], 16)
                if t == 0:
                    sp.dma_start(b_down[:], b_dn[0]).then_inc(b_down_landed, 16)
                    sp.dma_start(h_in[0][:], rows_of(h_rows, 0)).then_inc(h_in_landed[0], 16)
                    sp.dma_start(y_in[0][:, 0:2, :], y_by_token[0:R, 0:2, :]).then_inc(y_first_landed, 16)
                    sp.dma_start(y_in[0][:, 2:TOPK, :], y_by_token[0:R, 2:TOPK, :]).then_inc(y_in_landed[0], 16)
                    sp.dma_start(gain_p[:], g_ple[0:1, :].to_broadcast([P, D])).then_inc(gains_landed, 16)
                    sp.dma_start(gain_f[:], g_final.rearrange("(o d) -> o d", o=1).to_broadcast([P, D])).then_inc(gains_landed, 16)
                    continue
                if t >= 2:
                    sp.wait_ge(moe_ready, t - 1)
                sp.dma_start(y_in[t % 2][0:R], rows_of(y_by_token, t)).then_inc(y_in_landed[t % 2], 16)
                if t >= HB:
                    sp.wait_ge(out_stored, 16 * (t - HB + 1))
                sp.dma_start(h_in[t % HB][0:R, :], rows_of(h_rows, t)).then_inc(h_in_landed[t % HB], 16)

        @block.gpsimd
        def _(pool):
            for t in range(TILES):
                pool.wait_ge(y_final, t + 1)
                pool.dma_start(tokens(y_p, y_s, t), h_in[t % HB][0:ROWS[t], :]).then_inc(out_stored, 16)
            pool.wait_ge(out_stored, 16 * TILES)

        @block.scalar
        def _(act):
            mine = act_steps.on(act)
            nb = blocks(act)

            def inputs(t):
                R = ROWS[t]
                act.wait_ge(turned_in, t + 1)
                if t >= 1:
                    act.wait_ge(bdn_done, t)
                if t >= 2:
                    act.wait_ge(ple_proj_done, t - 1)
                nc.scalar.activation(gT[:, 0:R], bank[0:E, 0, 0:R], ACT.Copy)
                nc.scalar.activation(pT_hi[t % 2][:, :, 0:R], bank[:, 1, 0:PC * R].rearrange("p (c r) -> p c r", c=PC),
                                     ACT.Copy).then_inc(turned_read, 1)

            def norm_in(t):
                R = ROWS[t]
                act.wait_ge(moe_ready, t + 1)
                st = f_stat[0:R, 8 * t:8 * t + 8]
                if t >= 1:
                    act.wait_ge(fT_banked, t)
                mine(nc.scalar.activation(f_norm[0:R, :], h_in[t % HB][0:R, :], ACT.Square, accum_out=st[:, 0:1]))
                mine.settle()
                mine(nc.scalar.activation(st[:, 0:1], st[:, 0:1], ACT.Sqrt, scale=1.0 / D, bias=EPS), f_ss)

            def norm_out(t):
                R = ROWS[t]
                st = f_stat[0:R, 8 * t:8 * t + 8]
                act.wait_ge(out_ready, t + 1)
                mine(nc.scalar.activation(sg[0:R, :], h_in[t % HB][0:R, :], ACT.Square, accum_out=st[:, 2:3]))
                mine.settle()
                mine(nc.scalar.activation(st[:, 2:3], st[:, 2:3], ACT.Sqrt, scale=1.0 / D, bias=EPS), out_ss)

            act.wait_ge(raw_landed[2], 16 * (nb + 2))
            nc.scalar.activation(wp_hi[:], raw_pp, ACT.Copy).then_inc(wg_hi_ready, 1)
            inputs(0)
            for w in range(2):
                act.wait_ge(raw_landed[w], 16 * (nb + 3))
                nc.scalar.activation(wg_hi[:, :, w * CB:(w + 1) * CB], raw[w][:], ACT.Copy).then_inc(wg_hi_ready, 1)
            norm_in(0)
            for t in range(TILES):
                R = ROWS[t]
                act.wait_ge(fT_banked, t + 1)
                for j in range(2):
                    last = nc.scalar.activation(fT_hi[:, 4 * j:4 * j + 4, 0:R],
                                                bank[:, 2 + j, 0:4 * R].rearrange("p (c r) -> p c r", c=4), ACT.Copy)
                last.then_inc(fT_hi_ready, 1)
                if t + 1 < TILES:
                    inputs(t + 1)
                if t >= 1:
                    norm_out(t - 1)
                if t + 1 < TILES:
                    norm_in(t + 1)
                act.wait_ge(ple_gate_done, t + 1)
                if t >= 1:
                    mine.settle()
                mine(nc.scalar.activation(sg[0:R, :], two_banks(4, R), ACT.Sigmoid), sg_ready)
            norm_out(TILES - 1)

        @block.vector
        def _(dve):
            mine = dve_steps.on(dve)

            def inputs(t):
                R = ROWS[t]
                dve.wait_ge(turned_read, t + 1)
                if t >= 2:
                    dve.wait_ge(ple_proj_done, t - 1)
                mine(nc.vector.tensor_tensor(pT_lo[t % 2][:, :, 0:R], bank[:, 1, 0:PC * R].rearrange("p (c r) -> p c r", c=PC),
                                             pT_hi[t % 2][:, :, 0:R].bitcast(F32), ALU.subtract), pT_lo_ready)

            def add_experts(t):
                R = ROWS[t]
                h = h_in[t % HB][0:R, :]
                dve.wait_ge(h_in_landed[t % HB], 16 * (t // HB + 1))
                dve.wait_ge(bdn_done, t + 1)
                mine(nc.vector.tensor_tensor(h, h, two_banks(0, R), ALU.add))
                for k in range(TOPK):
                    if k == 0 and t == 0:
                        dve.wait_ge(y_first_landed, 16)
                    elif k == 0 or (k == 2 and t == 0):
                        dve.wait_ge(y_in_landed[t % 2], 16 * (t // 2 + 1))
                    mine.settle()
                    mine(nc.vector.scalar_tensor_tensor(h, y_in[t % 2][0:R, k, :], gates[0:R, t, k:k + 1], h, ALU.mult, ALU.add),
                         moe_ready if k == TOPK - 1 else None)

            def norm_in(t):
                R = ROWS[t]
                h, st = h_in[t % HB][0:R, :], f_stat[0:R, 8 * t:8 * t + 8]
                dve.wait_ge(f_ss, t + 1)
                mine(nc.vector.reciprocal(st[:, 1:2], st[:, 0:1]))
                mine.settle()
                mine(nc.vector.scalar_tensor_tensor(f_norm[0:R, :], h, st[:, 1:2], gain_p[0:R, :], ALU.mult, ALU.mult), f_normed)

            def gate_embedding(t):
                R = ROWS[t]
                dve.wait_ge(sg_ready, t + 1)
                dve.wait_ge(ple_proj_done, t + 1)
                mine(nc.vector.tensor_tensor(sg[0:R, :], sg[0:R, :], two_banks(6, R), ALU.mult), embedding_read)

            def add_embedding(t):
                R = ROWS[t]
                h = h_in[t % HB][0:R, :]
                dve.wait_ge(embedding_read, t + 1)
                mine(nc.vector.tensor_tensor(h, h, sg[0:R, :], ALU.add), out_ready)

            def norm_out(t):
                R = ROWS[t]
                h, st = h_in[t % HB][0:R, :], f_stat[0:R, 8 * t:8 * t + 8]
                dve.wait_ge(out_ss, t + 1)
                mine(nc.vector.reciprocal(st[:, 3:4], st[:, 2:3]))
                mine.settle()
                mine(nc.vector.scalar_tensor_tensor(h, h, st[:, 3:4], gain_f[0:R, :], ALU.mult, ALU.mult), y_final)

            def split_gate(w):
                dve.wait_ge(wg_hi_ready, w + 2)
                mine(nc.vector.tensor_tensor(wg_lo[:, :, w * CB:(w + 1) * CB], raw[w][:],
                                             wg_hi[:, :, w * CB:(w + 1) * CB].bitcast(F32), ALU.subtract), wg_lo_ready)

            dve.wait_ge(wg_hi_ready, 1)
            mine(nc.vector.tensor_tensor(wp_lo[:], raw_pp, wp_hi[:].bitcast(F32), ALU.subtract), wg_lo_ready)
            inputs(0)
            add_experts(0)
            split_gate(0)
            dve.wait_ge(gains_landed, 32)
            norm_in(0)
            for t in range(TILES):
                R = ROWS[t]
                if t >= 1:
                    gate_embedding(t - 1)
                dve.wait_ge(fT_banked, t + 1)
                dve.wait_ge(fT_hi_ready, t + 1)
                for j in range(2):
                    last = nc.vector.tensor_tensor(fT_lo[:, 4 * j:4 * j + 4, 0:R],
                                                   bank[:, 2 + j, 0:4 * R].rearrange("p (c r) -> p c r", c=4),
                                                   fT_hi[:, 4 * j:4 * j + 4, 0:R].bitcast(F32), ALU.subtract)
                mine(last, fT_lo_ready)
                if t + 1 < TILES:
                    inputs(t + 1)
                if t == 0:
                    split_gate(1)
                else:
                    add_embedding(t - 1)
                if t + 1 < TILES:
                    add_experts(t + 1)
                if t >= 1:
                    norm_out(t - 1)
                if t + 1 < TILES:
                    norm_in(t + 1)
            gate_embedding(TILES - 1)
            add_embedding(TILES - 1)
            norm_out(TILES - 1)

        @block.tensor
        def _(pe):
            def turn_inputs(t):
                R = ROWS[t]
                pe.wait_ge(ple_landed[t % 2], 16 * (t // 2 + 1))
                if t >= 1:
                    pe.wait_ge(moe_ready, t)
                nc.tensor.transpose(bank[0:E, 0, 0:R], gate_table[0:R, t, :], ident[0:R, 0:R])
                for c in range(PC):
                    last = nc.tensor.transpose(bank[:, 1, c * R:(c + 1) * R], ple_in[t % 2][0:R, c * P:(c + 1) * P],
                                               ident[0:R, 0:R])
                last.then_inc(turned_in, 1)

            def down_bias(t):
                pe.wait_ge(turned_read, t + 1)
                pe.wait_ge(pT_lo_ready, t + 1)
                for j in range(2):
                    last = nc.tensor.matmul(bank[0:ROWS[t], j, :], gT[:, 0:ROWS[t]], b_down[:, j * CB:(j + 1) * CB],
                                            start=True, stop=True)
                last.then_inc(bdn_done, 1)

            def project(t):
                for w in range(2):
                    last = product(nc, bank[:, 6 + w, :], lambda c: pT_hi[t % 2][:, c, :], lambda c: pT_lo[t % 2][:, c, :],
                                   wp_hi[:, :, w * CB:(w + 1) * CB], wp_lo[:, :, w * CB:(w + 1) * CB],
                                   [(k, k) for k in range(PC)], CB, True, True)
                last.then_inc(ple_proj_done, 1)

            turn_inputs(0)
            pe.wait_ge(b_down_landed, 16)
            down_bias(0)
            pe.wait_ge(wg_lo_ready, 1)
            project(0)
            for t in range(TILES):
                R = ROWS[t]
                pe.wait_ge(f_normed, t + 1)
                for c in range(KC):
                    last = nc.tensor.transpose(bank[:, 2 + c // 4, (c % 4) * R:(c % 4 + 1) * R],
                                               f_norm[0:R, c * P:(c + 1) * P], ident[0:R, 0:R])
                last.then_inc(fT_banked, 1)
                if t + 1 < TILES:
                    turn_inputs(t + 1)
                if t >= 1:
                    pe.wait_ge(embedding_read, t)
                    project(t)
                if t + 1 < TILES:
                    down_bias(t + 1)
                pe.wait_ge(fT_hi_ready, t + 1)
                pe.wait_ge(fT_lo_ready, t + 1)
                if t >= 1:
                    pe.wait_ge(sg_ready, t)
                for w in range(2):
                    if t == 0:
                        pe.wait_ge(wg_lo_ready, w + 2)
                    last = product(nc, bank[:, 4 + w, :], lambda c: fT_hi[:, c, :], lambda c: fT_lo[:, c, :],
                                   wg_hi[:, :, w * CB:(w + 1) * CB], wg_lo[:, :, w * CB:(w + 1) * CB],
                                   [(k, k) for k in range(KC)], CB, True, True)
                last.then_inc(ple_gate_done, 1)
    ctx.close()






_INS = ['x_prompt', 'x_sample', 'cache_swa_k', 'cache_swa_v', 'p_prompt', 'p_sample', 'g_mix', 'w_in', 'ln_v_g',
        'ln_v_b', 'w_sp', 'b_sp', 'sinks', 'g_out_a', 'g_out_b', 'w_o', 'g_moe', 'w_router', 'b_router', 'w_gu',
        'b_gu', 'w_dn', 'b_dn', 'g_ple', 'w_ple_gate', 'w_ple_proj', 'g_final']


def kernel(**inputs):
    import numpy as _np
    import concourse.bacc as _bacc
    from concourse import mybir as _mybir
    from concourse.bass_utils import run_bass_kernel_spmd as _run

    nc = _bacc.Bacc("TRN2", target_bir_lowering=False, num_devices=1)
    arrays, args = {}, []
    for name in _INS:
        a = _np.ascontiguousarray(inputs[name])
        arrays[f"in_{name}"] = a
        args.append(nc.dram_tensor(f"in_{name}", a.shape, _mybir.dt.from_np(a.dtype), kind="ExternalInput").ap())
    L, B, S, D = inputs['p_prompt'].shape[0], *inputs['x_prompt'].shape
    _, DB, W, KV, HD = inputs['cache_swa_k'].shape
    DS = inputs['x_sample'].shape[1]
    A = inputs['ln_v_g'].shape[1]
    shapes = [(B, S, D), (DB, DS, D), (L, B, W, KV, HD), (L, B, W, KV, HD), (L, DB, W, KV, HD), (L, DB, W, KV, HD),
              (L, DB, DS, A)]
    for i, shape in enumerate(shapes):
        args.append(nc.dram_tensor(f"out_{i}", shape, _mybir.dt.float32, kind="ExternalOutput").ap())
    hybrid_layer(nc, *args)
    r = _run(nc, [arrays], core_ids=[0])
    return tuple(r.results[0][f"out_{i}"] for i in range(len(shapes)))
```
